# Optimizing a Trainium2 kernel written in Bass

```python
import jax, jax.numpy as jnp
from jax import lax
import numpy as np

D_MODEL = 1024
BATCH = 1
SEQ = 256
DEPTH = 2

N_A = DEPTH // 2
N_B = DEPTH - N_A

LRU_WIDTH = D_MODEL
LRU_HEADS = 8
LRU_BLOCK = LRU_WIDTH // LRU_HEADS
LRU_CONV = 4
LRU_C = 8.0

N_HEADS = 8
HEAD_DIM = D_MODEL // N_HEADS
Q_BLOCK = 128

D_FF = 3 * D_MODEL
FFN_CONV = 3

DN_ALPHA = (2 * DEPTH) ** 0.25
DN_BETA = (8 * DEPTH) ** -0.25
LN_EPS = 1e-5


def layer_norm(x, g, b):
    xf = x.astype(jnp.float32)
    mu = jnp.mean(xf, axis=-1, keepdims=True)
    xc = xf - mu
    var = jnp.mean(xc * xc, axis=-1, keepdims=True)
    y = xc * lax.rsqrt(var + LN_EPS) * g.astype(jnp.float32) + b.astype(jnp.float32)
    return y.astype(x.dtype)

def causal_depthwise_conv(x, w, b):
    K = w.shape[0]
    S = x.shape[1]
    xp = jnp.pad(x, ((0, 0), (K - 1, 0), (0, 0)))
    y = b + xp[:, 0:S] * w[0]
    for k in range(1, K):
        y = y + xp[:, k:k + S] * w[k]
    return y

def _lin_combine(left, right):
    a1, b1 = left
    a2, b2 = right
    return a1 * a2, a2 * b1 + b2

def rg_lru_block(x, w_in, b_in, conv_w, conv_b, w_gates, b_gates, a_param, w_out, b_out):
    B, S, _ = x.shape
    proj = x @ w_in + b_in
    y_br = jax.nn.gelu(proj[..., :LRU_WIDTH])
    x_br = causal_depthwise_conv(proj[..., LRU_WIDTH:], conv_w, conv_b)
    xb = x_br.reshape(B, S, LRU_HEADS, LRU_BLOCK)
    gates = jnp.einsum('bsnc,ncg->bsng', xb, w_gates) + b_gates
    gates = jax.nn.sigmoid(gates.astype(jnp.float32))
    gate_i = gates[..., :LRU_BLOCK].reshape(B, S, LRU_WIDTH)
    gate_r = gates[..., LRU_BLOCK:].reshape(B, S, LRU_WIDTH)
    log_a = -LRU_C * gate_r * jax.nn.softplus(-a_param.astype(jnp.float32))
    a = jnp.exp(log_a)
    mult = jnp.sqrt(jnp.maximum(1.0 - jnp.exp(2.0 * log_a), 0.0))
    is_start = (jnp.arange(S) == 0)[None, :, None]
    mult = jnp.where(is_start, 1.0, mult)
    u = mult * gate_i * x_br.astype(jnp.float32)
    _, h = lax.associative_scan(_lin_combine, (a, u), axis=1)
    return (h.astype(x.dtype) * y_br) @ w_out + b_out

def stick_breaking_attention(q, k, v):
    B, S, H, Dh = q.shape
    scale = Dh ** -0.5
    outs = []
    for i in range(S // Q_BLOCK):
        q0 = i * Q_BLOCK
        kv_len = q0 + Q_BLOCK
        q_blk = q[:, q0:kv_len]
        k_p = k[:, :kv_len]
        v_p = v[:, :kv_len]
        z = jnp.einsum('bqhd,bkhd->bhqk', q_blk, k_p).astype(jnp.float32) * scale
        q_pos = q0 + jnp.arange(Q_BLOCK)
        k_pos = jnp.arange(kv_len)
        mask = k_pos[None, :] < q_pos[:, None]
        log_beta = jax.nn.log_sigmoid(z)
        log_1m = jnp.where(mask, jax.nn.log_sigmoid(-z), 0.0)
        suffix = lax.cumsum(log_1m, axis=3, reverse=True) - log_1m
        w = jnp.where(mask, jnp.exp(log_beta + suffix), 0.0)
        o = jnp.einsum('bhqk,bkhd->bqhd', w, v_p.astype(jnp.float32))
        outs.append(o.astype(q.dtype))
    return jnp.concatenate(outs, axis=1)

def conv_ffn(x, w_up, conv_w, conv_b, w_down):
    h = causal_depthwise_conv(x @ w_up, conv_w, conv_b)
    return (jax.nn.gelu(h[..., :D_FF]) * h[..., D_FF:]) @ w_down

def first_inputs(seed: int = 0) -> dict:
    key = jax.random.key(seed)
    ks = jax.random.split(key, 24)
    f32 = jnp.float32

    def nrm(k, shape, fan_in, gain=1.0):
        return jax.random.normal(k, shape, f32) * (gain * fan_in ** -0.5)

    def small(k, shape):
        return 0.01 * jax.random.normal(k, shape, f32)

    W, HD = LRU_WIDTH, N_HEADS * HEAD_DIM
    u = jax.random.uniform(ks[8], (N_A, W), f32, minval=0.9, maxval=0.999)
    s = u ** (1.0 / LRU_C)
    lru_a_param = jnp.log(s) - jnp.log1p(-s)
    kv_w = jnp.concatenate([nrm(ks[11], (D_MODEL, HD), D_MODEL),
                            nrm(ks[12], (D_MODEL, HD), D_MODEL, DN_BETA)], axis=1)
    return {
        "x": jax.random.normal(ks[0], (BATCH, SEQ, D_MODEL), f32),
        "lru_w_in": nrm(ks[1], (N_A, D_MODEL, 2 * W), D_MODEL),
        "lru_b_in": small(ks[2], (N_A, 2 * W)),
        "lru_conv_w": nrm(ks[3], (N_A, LRU_CONV, W), LRU_CONV),
        "lru_conv_b": small(ks[4], (N_A, W)),
        "lru_w_gates": nrm(ks[5], (N_A, LRU_HEADS, LRU_BLOCK, 2 * LRU_BLOCK), LRU_BLOCK),
        "lru_b_gates": small(ks[6], (N_A, LRU_HEADS, 2 * LRU_BLOCK)),
        "lru_a_param": lru_a_param,
        "lru_w_out": nrm(ks[9], (N_A, W, D_MODEL), W, DN_BETA),
        "lru_b_out": small(ks[10], (N_A, D_MODEL)),
        "kv_w": kv_w,
        "attn_w_q": nrm(ks[13], (N_B, D_MODEL, HD), D_MODEL),
        "attn_w_out": nrm(ks[14], (N_B, HD, D_MODEL), HD, DN_BETA),
        "ffn_w_up": nrm(ks[15], (DEPTH, D_MODEL, 2 * D_FF), D_MODEL),
        "ffn_conv_w": nrm(ks[16], (DEPTH, FFN_CONV, 2 * D_FF), FFN_CONV),
        "ffn_conv_b": small(ks[17], (DEPTH, 2 * D_FF)),
        "ffn_w_down": nrm(ks[18], (DEPTH, D_FF, D_MODEL), D_FF, DN_BETA),
        "ln_g": 1.0 + small(ks[19], (DEPTH, 2, D_MODEL)),
        "ln_b": small(ks[20], (DEPTH, 2, D_MODEL)),
    }

def first_block(x, lru_w_in, lru_b_in, lru_conv_w, lru_conv_b, lru_w_gates, lru_b_gates,
              lru_a_param, lru_w_out, lru_b_out, kv_w, attn_w_q, attn_w_out,
              ffn_w_up, ffn_conv_w, ffn_conv_b, ffn_w_down, ln_g, ln_b):
    B, S, _ = x.shape
    HD = N_HEADS * HEAD_DIM
    k_sh = None
    v_sh = None
    for layer in range(DEPTH):
        if layer < N_A:
            mix = rg_lru_block(x, lru_w_in[layer], lru_b_in[layer], lru_conv_w[layer],
                               lru_conv_b[layer], lru_w_gates[layer], lru_b_gates[layer],
                               lru_a_param[layer], lru_w_out[layer], lru_b_out[layer])
        else:
            if layer == N_A:
                kv = x @ kv_w
                k_sh = kv[..., :HD].reshape(B, S, N_HEADS, HEAD_DIM)
                v_sh = kv[..., HD:].reshape(B, S, N_HEADS, HEAD_DIM)
            j = layer - N_A
            q = (x @ attn_w_q[j]).reshape(B, S, N_HEADS, HEAD_DIM)
            o = stick_breaking_attention(q, k_sh, v_sh).reshape(B, S, HD)
            mix = o @ attn_w_out[j]
        x = layer_norm(DN_ALPHA * x + mix, ln_g[layer, 0], ln_b[layer, 0])
        f = conv_ffn(x, ffn_w_up[layer], ffn_conv_w[layer], ffn_conv_b[layer], ffn_w_down[layer])
        x = layer_norm(DN_ALPHA * x + f, ln_g[layer, 1], ln_b[layer, 1])
    return x


GRID_W = 64
CTX_LEN = 256
A_GROUPS = 4
A_GROUP_DIM = 128
A_WIDTH = A_GROUPS * A_GROUP_DIM
B_WIDTH = 512
CONV_WIDTH = 31
CONV_PAD = (CONV_WIDTH - 1) // 2
AB_IN = A_WIDTH + 2 * B_WIDTH
AB_MIX = A_WIDTH + B_WIDTH
C_HEADS = 4
C_KV_HEADS = 2
C_GROUP = C_HEADS // C_KV_HEADS
C_HEAD_DIM = 128
C_WIDTH = C_HEADS * C_HEAD_DIM
C_KV_WIDTH = C_KV_HEADS * C_HEAD_DIM
D_HEADS = 4
D_NOPE = 128
D_ROPE = 64
D_V = 128
Q_LORA = 384
KV_LORA = 256
D_WIDTH = D_HEADS * D_V
CD_IN = C_WIDTH + 2 * C_KV_WIDTH + Q_LORA + KV_LORA + D_ROPE
CD_SPLITS = [C_WIDTH, C_WIDTH + C_KV_WIDTH, C_WIDTH + 2 * C_KV_WIDTH,
             C_WIDTH + 2 * C_KV_WIDTH + Q_LORA, C_WIDTH + 2 * C_KV_WIDTH + Q_LORA + KV_LORA]
CD_MIX = C_WIDTH + D_WIDTH
ROPE_THETA = 10000.0
N_GROUPS = 4
EXPERTS_PER_GROUP = 8
N_EXPERTS = N_GROUPS * EXPERTS_PER_GROUP
TOP_K = 2
EXPERT_FF = 512
EXPERT_BLOCK = 128
N_MOD = 6
RMS_EPS = 1e-6
MOD_INIT = 0.5
ROUTER_BIAS_INIT = 0.01
N_EVEN = (DEPTH + 1) // 2
N_ODD = DEPTH // 2


def rmsnorm(x, g):
    xf = x.astype(jnp.float32)
    y = xf * lax.rsqrt(jnp.mean(xf * xf, axis=-1, keepdims=True) + RMS_EPS)
    return y.astype(x.dtype) * g

def axial_rope_tables(row, col, dim):
    n_freq = dim // 4
    inv = ROPE_THETA ** (-jnp.arange(n_freq, dtype=jnp.float32) / n_freq)
    ang = jnp.concatenate([row[:, None] * inv[None, :], col[:, None] * inv[None, :]], axis=-1)
    return jnp.cos(ang), jnp.sin(ang)

def apply_rope(x, cos, sin):
    xf = x.astype(jnp.float32).reshape(x.shape[:-1] + (x.shape[-1] // 2, 2))
    xr, xi = xf[..., 0], xf[..., 1]
    c = cos[None, :, None, :]
    s = sin[None, :, None, :]
    out = jnp.stack([xr * c - xi * s, xr * s + xi * c], axis=-1)
    return out.reshape(x.shape).astype(x.dtype)

def block_attention(q, k, v, scale):
    b, s, kh, g, d = q.shape
    nb = s // Q_BLOCK
    qb = jnp.moveaxis(q.reshape(b, nb, Q_BLOCK, kh, g, d), 1, 0)

    def one_block(qblk):
        sc = jnp.einsum('bqhgd,bkhd->bhgqk', qblk, k).astype(jnp.float32) * scale
        p = jax.nn.softmax(sc, axis=-1).astype(v.dtype)
        return jnp.einsum('bhgqk,bkhe->bqhge', p, v)

    o = lax.map(one_block, qb)
    return jnp.moveaxis(o, 0, 1).reshape(b, s, kh, g, v.shape[-1])

def fourier_conv_mixer(h, w_in, conv_w, conv_b, conv_g, w_out):
    b, L, _ = h.shape
    p = h @ w_in
    pa, pu, pg = jnp.split(p, [A_WIDTH, A_WIDTH + B_WIDTH], axis=-1)
    fa = pa.astype(jnp.float32).reshape(b, L, A_GROUPS, A_GROUP_DIM)
    ya = jnp.fft.fft2(fa, axes=(1, 3), norm='ortho').real.reshape(b, L, A_WIDTH).astype(h.dtype)
    u = pu * jax.nn.sigmoid(pg)
    u = lax.conv_general_dilated(u, conv_w[:, None, :], (1,), [(CONV_PAD, CONV_PAD)],
                                 dimension_numbers=('NWC', 'WIO', 'NWC'),
                                 feature_group_count=B_WIDTH) + conv_b
    yb = jax.nn.silu(rmsnorm(u, conv_g))
    return jnp.concatenate([ya, yb], axis=-1) @ w_out

def cd_project(t, w_in, q_g, k_g, cq_g, ckv_g, w_uq, w_ukv):
    bt, L, _ = t.shape
    q, k, v, cq, ckv, kr = jnp.split(t @ w_in, CD_SPLITS, axis=-1)
    q = rmsnorm(q.reshape(bt, L, C_HEADS, C_HEAD_DIM), q_g)
    k = rmsnorm(k.reshape(bt, L, C_KV_HEADS, C_HEAD_DIM), k_g)
    v = v.reshape(bt, L, C_KV_HEADS, C_HEAD_DIM)
    qd = (rmsnorm(cq, cq_g) @ w_uq).reshape(bt, L, D_HEADS, D_NOPE + D_ROPE)
    kvd = (rmsnorm(ckv, ckv_g) @ w_ukv).reshape(bt, L, D_HEADS, D_NOPE + D_V)
    kd_rope = kr[:, :, None, :]
    return (q, k, v, qd[..., :D_NOPE], qd[..., D_NOPE:], kvd[..., :D_NOPE], kd_rope, kvd[..., D_NOPE:])

def cd_attend(q, qdn, qdr, k, v, kdn, kdr, vd):
    b, L = q.shape[:2]
    oc = block_attention(q.reshape(b, L, C_KV_HEADS, C_GROUP, C_HEAD_DIM), k, v, C_HEAD_DIM ** -0.5)
    qd = jnp.concatenate([qdn, qdr], axis=-1)[:, :, :, None, :]
    kd = jnp.concatenate([kdn, jnp.broadcast_to(kdr, kdn.shape[:-1] + (D_ROPE,))], axis=-1)
    od = block_attention(qd, kd, vd, (D_NOPE + D_ROPE) ** -0.5)
    return jnp.concatenate([oc.reshape(b, L, C_WIDTH), od.reshape(b, L, D_WIDTH)], axis=-1)

def attn_mla_mixer(h, hc, w_in, q_g, k_g, cq_g, ckv_g, w_uq, w_ukv, w_out, rope_c, rope_d, with_ctx_out):
    q, k, v, qdn, qdr, kdn, kdr, vd = cd_project(h, w_in, q_g, k_g, cq_g, ckv_g, w_uq, w_ukv)
    cq, ck, cv, cqdn, cqdr, ckdn, ckdr, cvd = cd_project(hc, w_in, q_g, k_g, cq_g, ckv_g, w_uq, w_ukv)
    q, k = apply_rope(q, *rope_c), apply_rope(k, *rope_c)
    qdr, kdr = apply_rope(qdr, *rope_d), apply_rope(kdr, *rope_d)
    cat = lambda a, b: jnp.concatenate([a, b], axis=1)
    y = cd_attend(q, qdn, qdr, cat(ck, k), cat(cv, v), cat(ckdn, kdn), cat(ckdr, kdr), cat(cvd, vd)) @ w_out
    yc = cd_attend(cq, cqdn, cqdr, ck, cv, ckdn, ckdr, cvd) @ w_out if with_ctx_out else None
    return y, yc

def routed_experts(h, e_idx, e_w, w_gate, w_up, w_down):
    n_tok, d = h.shape
    n_exp = w_gate.shape[0]
    n_asg = e_idx.shape[0] * e_idx.shape[1]
    n_blocks = (n_asg + n_exp * (EXPERT_BLOCK - 1) + EXPERT_BLOCK - 1) // EXPERT_BLOCK
    n_rows = n_blocks * EXPERT_BLOCK
    flat_e = e_idx.reshape(-1)
    flat_tok = jnp.arange(n_asg, dtype=jnp.int32) // e_idx.shape[1]
    flat_w = e_w.reshape(-1)
    order = jnp.argsort(flat_e)
    sorted_e = flat_e[order]
    counts = jnp.bincount(flat_e, length=n_exp)
    padded = (counts + EXPERT_BLOCK - 1) // EXPERT_BLOCK * EXPERT_BLOCK
    padded_end = jnp.cumsum(padded)
    start = jnp.cumsum(counts) - counts
    dest = (padded_end - padded)[sorted_e] + jnp.arange(n_asg, dtype=jnp.int32) - start[sorted_e]
    row_tok = jnp.full((n_rows,), n_tok, jnp.int32).at[dest].set(flat_tok[order])
    row_w = jnp.zeros((n_rows,), h.dtype).at[dest].set(flat_w[order])
    block_exp = jnp.minimum(jnp.searchsorted(padded_end, jnp.arange(n_blocks, dtype=jnp.int32) * EXPERT_BLOCK,
                                             side='right'), n_exp - 1)
    h_pad = jnp.concatenate([h, jnp.zeros((1, d), h.dtype)], axis=0)
    xb = h_pad[row_tok].reshape(n_blocks, EXPERT_BLOCK, d)

    def expert_block(args):
        xblk, e = args
        return (jax.nn.silu(xblk @ w_gate[e]) * (xblk @ w_up[e])) @ w_down[e]

    yb = lax.map(expert_block, (xb, block_exp)).reshape(n_rows, d)
    return jnp.zeros((n_tok + 1, d), h.dtype).at[row_tok].add(yb * row_w[:, None])[:n_tok]

def hier_moe(h, grp_w, grp_b, exp_w, exp_b, w_gate, w_up, w_down):
    n = h.shape[0]
    g_logit = (h @ grp_w).astype(jnp.float32) + grp_b.astype(jnp.float32)
    g_idx = jnp.argmax(g_logit, axis=-1).astype(jnp.int32)
    g_prob = jnp.take_along_axis(jax.nn.softmax(g_logit, axis=-1), g_idx[:, None], axis=-1)
    e_logit = ((h @ exp_w).astype(jnp.float32) + exp_b.astype(jnp.float32)).reshape(n, N_GROUPS, EXPERTS_PER_GROUP)
    e_logit = jnp.take_along_axis(e_logit, g_idx[:, None, None], axis=1)[:, 0]
    top_v, top_i = lax.top_k(e_logit, TOP_K)
    w = (g_prob * jax.nn.softmax(top_v, axis=-1)).astype(h.dtype)
    e_idx = g_idx[:, None] * EXPERTS_PER_GROUP + top_i.astype(jnp.int32)
    return routed_experts(h, e_idx, w, w_gate, w_up, w_down)

def second_inputs(seed: int = 0) -> dict:
    key = jax.random.key(seed)
    ks = jax.random.split(key, 29)
    f32 = jnp.float32
    nrm = lambda k, shape, s: jax.random.normal(k, shape, f32) * s
    gain = lambda k, shape: 1.0 + 0.05 * jax.random.normal(k, shape, f32)
    ne, no = N_EVEN, N_ODD
    return {
        'x': nrm(ks[0], (BATCH, SEQ, D_MODEL), 1.0),
        'c': nrm(ks[1], (BATCH, D_MODEL), 1.0),
        'ctx': nrm(ks[2], (BATCH, CTX_LEN, D_MODEL), 1.0),
        'c_ctx': nrm(ks[3], (D_MODEL,), 1.0),
        'mod_w': nrm(ks[4], (DEPTH, D_MODEL, N_MOD * D_MODEL), MOD_INIT * D_MODEL ** -0.5),
        'mod_b': nrm(ks[5], (DEPTH, N_MOD * D_MODEL), 0.02),
        'norm_mix_g': gain(ks[6], (DEPTH, D_MODEL)),
        'norm_ffn_g': gain(ks[7], (DEPTH, D_MODEL)),
        'w_in_ab': nrm(ks[8], (ne, D_MODEL, AB_IN), D_MODEL ** -0.5),
        'conv_w': nrm(ks[9], (ne, CONV_WIDTH, B_WIDTH), CONV_WIDTH ** -0.5),
        'conv_b': nrm(ks[10], (ne, B_WIDTH), 0.02),
        'conv_norm_g': gain(ks[11], (ne, B_WIDTH)),
        'w_out_ab': nrm(ks[12], (ne, AB_MIX, D_MODEL), AB_MIX ** -0.5),
        'w_in_cd': nrm(ks[13], (no, D_MODEL, CD_IN), D_MODEL ** -0.5),
        'q_norm_g': gain(ks[14], (no, C_HEAD_DIM)),
        'k_norm_g': gain(ks[15], (no, C_HEAD_DIM)),
        'cq_norm_g': gain(ks[16], (no, Q_LORA)),
        'ckv_norm_g': gain(ks[17], (no, KV_LORA)),
        'w_uq': nrm(ks[18], (no, Q_LORA, D_HEADS * (D_NOPE + D_ROPE)), Q_LORA ** -0.5),
        'w_ukv': nrm(ks[19], (no, KV_LORA, D_HEADS * (D_NOPE + D_V)), KV_LORA ** -0.5),
        'w_out_cd': nrm(ks[20], (no, CD_MIX, D_MODEL), CD_MIX ** -0.5),
        'router_grp_w': nrm(ks[21], (DEPTH, D_MODEL, N_GROUPS), D_MODEL ** -0.5),
        'router_grp_b': nrm(ks[22], (DEPTH, N_GROUPS), ROUTER_BIAS_INIT),
        'router_exp_w': nrm(ks[23], (DEPTH, D_MODEL, N_EXPERTS), D_MODEL ** -0.5),
        'router_exp_b': nrm(ks[24], (DEPTH, N_EXPERTS), ROUTER_BIAS_INIT),
        'exp_w_gate': nrm(ks[25], (DEPTH, N_EXPERTS, D_MODEL, EXPERT_FF), D_MODEL ** -0.5),
        'exp_w_up': nrm(ks[26], (DEPTH, N_EXPERTS, D_MODEL, EXPERT_FF), D_MODEL ** -0.5),
        'exp_w_down': nrm(ks[27], (DEPTH, N_EXPERTS, EXPERT_FF, D_MODEL), EXPERT_FF ** -0.5),
        'final_norm_g': gain(ks[28], (D_MODEL,)),
    }

def second_block(x, c, ctx, c_ctx, mod_w, mod_b, norm_mix_g, norm_ffn_g, w_in_ab, conv_w, conv_b,
              conv_norm_g, w_out_ab, w_in_cd, q_norm_g, k_norm_g, cq_norm_g, ckv_norm_g, w_uq, w_ukv,
              w_out_cd, router_grp_w, router_grp_b, router_exp_w, router_exp_b, exp_w_gate, exp_w_up,
              exp_w_down, final_norm_g):
    b, s, d = x.shape
    rows = s // GRID_W
    row_pos = jnp.repeat(jnp.arange(rows, dtype=jnp.float32), GRID_W)
    col_pos = jnp.tile(jnp.arange(GRID_W, dtype=jnp.float32), rows)
    rope_c = axial_rope_tables(row_pos, col_pos, C_HEAD_DIM)
    rope_d = axial_rope_tables(row_pos, col_pos, D_ROPE)
    silu_c = jax.nn.silu(c)
    silu_cc = jax.nn.silu(c_ctx)
    xc = ctx
    for layer in range(DEPTH):
        last = layer == DEPTH - 1
        j = layer // 2
        sh1, sc1, g1, sh2, sc2, g2 = jnp.split((silu_c @ mod_w[layer] + mod_b[layer])[:, None, :], N_MOD, axis=-1)
        csh1, csc1, cg1, csh2, csc2, cg2 = jnp.split(silu_cc @ mod_w[layer] + mod_b[layer], N_MOD)
        h = rmsnorm(x, norm_mix_g[layer]) * (1.0 + sc1) + sh1
        if layer % 2 == 0:
            ab = (w_in_ab[j], conv_w[j], conv_b[j], conv_norm_g[j], w_out_ab[j])
            x = x + g1 * fourier_conv_mixer(h, *ab)
            if not last:
                hc = rmsnorm(xc, norm_mix_g[layer]) * (1.0 + csc1) + csh1
                xc = xc + cg1 * fourier_conv_mixer(hc, *ab)
        else:
            hc = rmsnorm(xc, norm_mix_g[layer]) * (1.0 + csc1) + csh1
            y, yc = attn_mla_mixer(h, hc, w_in_cd[j], q_norm_g[j], k_norm_g[j], cq_norm_g[j], ckv_norm_g[j],
                                   w_uq[j], w_ukv[j], w_out_cd[j], rope_c, rope_d, not last)
            x = x + g1 * y
            if not last:
                xc = xc + cg1 * yc
        moe = (router_grp_w[layer], router_grp_b[layer], router_exp_w[layer], router_exp_b[layer],
               exp_w_gate[layer], exp_w_up[layer], exp_w_down[layer])
        h2 = rmsnorm(x, norm_ffn_g[layer]) * (1.0 + sc2) + sh2
        if last:
            x = x + g2 * hier_moe(h2.reshape(b * s, d), *moe).reshape(x.shape)
        else:
            hc2 = rmsnorm(xc, norm_ffn_g[layer]) * (1.0 + csc2) + csh2
            out = hier_moe(jnp.concatenate([h2.reshape(b * s, d), hc2.reshape(-1, d)], axis=0), *moe)
            x = x + g2 * out[: b * s].reshape(x.shape)
            xc = xc + cg2 * out[b * s:].reshape(xc.shape)
    return rmsnorm(x, final_norm_g)


def setup_inputs(seed=0):
    out = dict(first_inputs(seed))
    for name, value in second_inputs(seed + 1).items():
        if name != "x":
            out[name + "_2"] = value
    return out


def reference(
    x, lru_w_in, lru_b_in, lru_conv_w, lru_conv_b, lru_w_gates, lru_b_gates, lru_a_param,
    lru_w_out, lru_b_out, kv_w, attn_w_q, attn_w_out, ffn_w_up, ffn_conv_w, ffn_conv_b,
    ffn_w_down, ln_g, ln_b, c_2, ctx_2, c_ctx_2, mod_w_2, mod_b_2, norm_mix_g_2, norm_ffn_g_2,
    w_in_ab_2, conv_w_2, conv_b_2, conv_norm_g_2, w_out_ab_2, w_in_cd_2, q_norm_g_2, k_norm_g_2,
    cq_norm_g_2, ckv_norm_g_2, w_uq_2, w_ukv_2, w_out_cd_2, router_grp_w_2, router_grp_b_2,
    router_exp_w_2, router_exp_b_2, exp_w_gate_2, exp_w_up_2, exp_w_down_2, final_norm_g_2,
):
    x = first_block(
        x, lru_w_in, lru_b_in, lru_conv_w, lru_conv_b, lru_w_gates, lru_b_gates, lru_a_param,
        lru_w_out, lru_b_out, kv_w, attn_w_q, attn_w_out, ffn_w_up, ffn_conv_w, ffn_conv_b,
        ffn_w_down, ln_g, ln_b,
    )
    return second_block(
        x, c_2, ctx_2, c_ctx_2, mod_w_2, mod_b_2, norm_mix_g_2, norm_ffn_g_2, w_in_ab_2,
        conv_w_2, conv_b_2, conv_norm_g_2, w_out_ab_2, w_in_cd_2, q_norm_g_2, k_norm_g_2,
        cq_norm_g_2, ckv_norm_g_2, w_uq_2, w_ukv_2, w_out_cd_2, router_grp_w_2, router_grp_b_2,
        router_exp_w_2, router_exp_b_2, exp_w_gate_2, exp_w_up_2, exp_w_down_2, final_norm_g_2,
    )


_drawn_inputs = setup_inputs


def setup_inputs(seed=0):
    import zlib

    import numpy as np

    out = dict(_drawn_inputs(seed))
    spreads = {}
    factors = {'lru_b_in': 3.617,
     'lru_conv_b': 4.266,
     'lru_b_gates': 8.0,
     'lru_b_out': 6.014,
     'ffn_conv_b': 6.565,
     'ctx_2': 3.014,
     'norm_mix_g_2': 3.889,
     'conv_b_2': 7.22,
     'conv_norm_g_2': 5.1,
     'q_norm_g_2': 8.0,
     'k_norm_g_2': 8.0,
     'cq_norm_g_2': 8.0,
     'ckv_norm_g_2': 8.0,
     'router_grp_b_2': 8.0,
     'router_exp_b_2': 5.64}
    for name, (base, spread) in spreads.items():
        noise = np.random.default_rng([zlib.crc32(name.encode()), seed]).standard_normal(out[name].shape)
        drawn = base * np.exp(spread * noise) if base else spread * noise
        out[name] = __import__('jax').numpy.asarray(drawn.astype(out[name].dtype))
    for name, factor in factors.items():
        out[name] = (out[name] * factor).astype(out[name].dtype)
    return out
```

```python
from contextlib import ExitStack

import numpy as np

import concourse.bass as bass
from concourse import mybir

ALU = mybir.AluOpType
ACT = mybir.ActivationFunctionType
AX = mybir.AxisListType
F32 = mybir.dt.float32
BF16 = mybir.dt.bfloat16
I32 = mybir.dt.int32
ds = bass.ds

P = 128
D = 1024
KT = D // P
S = 256
N2 = 2 * S
NH = 8
FF = 3 * D
FT = FF // P
CH = 512
NJ = FF // CH
MJ = CH // P
SLOTS = 5
MSLOTS = 6
ALPHA = (2 * 2) ** 0.25
LN_EPS = 1e-5
RMS_EPS = 1e-6
NMOD = 6
NE = 32
NG = 4
EFF = 512
B = 128
NTOK = [2 * S, S]
NBLK = [2 * (((2 * n + NE * (B - 1)) // B + 1) // 2) for n in NTOK]
CONV = 31
PADC = CONV // 2
GRID_W = 64

VEC = {}
_at = 0
for _name, _cols in [
    ("lru_b_in", 16), ("lru_conv_w", 4 * 8), ("lru_conv_b", 8), ("lru_b_gates", 16), ("lru_a", 8),
    ("lru_b_out", 8), ("ffn_conv_w", 2 * 3 * 48), ("ffn_conv_b", 2 * 48), ("ln_g", 4 * 8),
    ("ln_b", 4 * 8), ("c", 16), ("mod_b", 2 * 48), ("norm_mix_g", 16), ("norm_ffn_g", 16),
    ("conv_w", CONV * 4), ("conv_b", 4), ("conv_norm_g", 4), ("q_g", 1), ("k_g", 1), ("cq_g", 3),
    ("ckv_g", 2), ("final_g", 8),
]:
    VEC[_name] = _at
    _at += _cols
NVEC = _at

TAB = {}
_at = 0
for _name, _cols in [
    ("ident", 128), ("suffix", 128), ("before", 128), ("ones", 128), ("swap", 128), ("dft_d", 256),
    ("cos_l", 512), ("sin_l", 512), ("cos_c", 256), ("sin_c", 256), ("cos_d", 256), ("sin_d", 256),
    ("mask", 512), ("iota", 64), ("thresh", 4),
]:
    TAB[_name] = _at
    _at += _cols
NTAB = _at


def tables():
    t = np.zeros((P, NTAB), np.float32)
    p = np.arange(P)
    put = lambda name, a: t.__setitem__((slice(0, a.shape[0]), slice(TAB[name], TAB[name] + a.shape[1])), a)
    put("ident", np.eye(P))
    put("suffix", (p[:, None] >= p[None, :]).astype(np.float64))
    put("before", (p[:, None] < p[None, :]).astype(np.float64))
    put("ones", np.ones((P, P)))
    put("swap", (p[:, None] == (p[None, :] ^ 1)).astype(np.float64))
    ang = 2 * np.pi * np.outer(p, p) / P
    put("dft_d", np.concatenate([np.cos(ang), np.sin(ang)], 1) / np.sqrt(S * P))
    l = np.arange(S)
    ang = 2 * np.pi * (np.outer(l, l) % S) / S
    both = lambda a: a.reshape(2, P, S).transpose(1, 0, 2).reshape(P, 2 * S)
    put("cos_l", both(np.cos(ang)))
    put("sin_l", both(-np.sin(ang)))
    row, col = (l // GRID_W).astype(np.float32), (l % GRID_W).astype(np.float32)
    for name, dim in (("c", 128), ("d", 64)):
        nf = dim // 4
        inv = (np.float32(10000.0) ** (-np.arange(nf, dtype=np.float32) / np.float32(nf))).astype(np.float32)
        a = np.concatenate([inv[:, None] * row[None], inv[:, None] * col[None]], 0).astype(np.float64)
        cos, sin = np.repeat(np.cos(a), 2, 0), np.repeat(np.sin(a), 2, 0)
        sin[0::2] *= -1
        put("cos_" + name, cos)
        put("sin_" + name, sin)
    k = np.arange(S).reshape(2, P).T
    put("mask", (k[:, :, None] < l[None, None, :]).astype(np.float64).reshape(P, 2 * S))
    put("iota", np.tile(np.arange(64), (P, 1)).astype(np.float64))
    put("thresh", np.tile(np.arange(4) * B, (P, 1)).astype(np.float64))
    return t


class Chain:

    def __init__(self, eng, sem):
        self.eng, self.sem, self.n, self.turn, self.per, self.start = eng, sem, 0, None, 0, 0

    def mark(self, ins):
        self.n += 1
        ins.then_inc(self.sem, 1)
        return self.n

    def wait(self, n):
        if self.turn is None:
            self.eng.wait_ge(self.sem, n)
        else:
            self.eng.wait_ge(self.sem, self.turn * self.per + n)

    def __call__(self, ins):
        self.wait(self.mark(ins))

    def loop(self, turn, per):
        self.turn, self.per, self.start = turn, per, self.n

    def end_loop(self, turns=None):
        assert self.n - self.start == self.per, (self.n - self.start, self.per)
        self.turn = None
        if turns is not None:
            self.n = self.start + self.per * turns


def build(nc, a):
    ctx = ExitStack()
    with ctx:
        def sb(name, shape, dt=F32):
            return ctx.enter_context(nc.sbuf_tensor(name, shape, dt))

        def sem(name):
            return ctx.enter_context(nc.semaphore(name))

        def sems(name, n):
            return [sem(f"{name}{i}") for i in range(n)]

        ring = sb("ring", [P, MSLOTS, KT * CH])
        X = sb("X", [P, KT, N2])
        H = sb("H", [P, KT, N2])
        S1 = sb("S1", [P, KT, N2])
        S2 = sb("S2", [P, KT, N2])
        S3 = sb("S3", [P, KT, N2])
        vec = sb("vec", [P, NVEC])
        tab = sb("tab", [P, NTAB])
        std = sb("std", [P, 2, N2])
        modv = sb("modv", [P, 2, 48, 2])
        gsv = sb("gsv", [P, 4, KT, 2])
        cs = sb("cs", [P, 16])
        sp = sb("sp", [P, 8, 8])
        rw = sb("rw", [P, 2, KT, 36])
        rb = sb("rb", [1, 2, 36])
        zb = sb("zb", [P, CH], BF16)
        rt = sb("rt", [P, 1024])
        dst = sb("dst", [P, 4, 2], I32)
        tok = sb("tok", [P, 4], I32)
        zi = sb("zi", [P, NBLK[0]], I32)
        ix = sb("ix", [P, 2], I32)
        plan = sb("plan", [1, 2, 64], I32)
        T = ctx.enter_context(nc.psum_tensor("T", [P, 8, 512], F32))

        def tabv(name, n, off=0, rows=P):
            return tab[0:rows, TAB[name] + off:TAB[name] + off + n]

        def vc(name, i=0, n=1):
            return vec[:, VEC[name] + i:VEC[name] + i + n]

        ident, ones = tabv("ident", P), tabv("ones", P)

        def flat(t):
            return t[:, :, :].rearrange("p a n -> p (a n)")

        def part(t, off, *dims):
            n = int(np.prod(dims))
            v = flat(t)[:, off:off + n]
            if len(dims) == 2:
                return v.rearrange("p (a b) -> p a b", a=dims[0])
            if len(dims) == 3:
                return v.rearrange("p (a b c) -> p a b c", a=dims[0], b=dims[1])
            return v

        x1 = X[:, :, 0:S]

        h_rows = [nc.dram_tensor(f"h_rows{l}", (NTOK[l], D), F32, kind="Internal").ap() for l in range(2)]
        y_rows = nc.dram_tensor("y_rows", (max(NBLK) * B, D), F32, kind="Internal").ap()
        row_tok = [nc.dram_tensor(f"row_tok{l}", (NBLK[l] * B, 1), I32, kind="Internal").ap() for l in range(2)]

        def cols(w, n0, n):
            return w[:, n0:n0 + n].rearrange("(k p) n -> p k n", p=P)

        chunks, c0 = [], {}

        def add(name, sources):
            c0[name] = len(chunks)
            chunks.extend(sources)

        add("lru_in", [cols(a["lru_w_in"], CH * i, CH) for i in range(4)])
        add("gates", [a["lru_w_gates"].rearrange("n p g -> p n g")])
        add("lru_out", [cols(a["lru_w_out"], CH * i, CH) for i in range(2)])
        add("ffn0", [None] * 5 * NJ)
        add("kv", [cols(a["kv_w"], CH * i, CH) for i in range(4)])
        add("q", [cols(a["attn_w_q"], CH * i, CH) for i in range(2)])
        add("attn_out", [cols(a["attn_w_out"], CH * i, CH) for i in range(2)])
        add("ffn1", [None] * 5 * NJ)
        add("in_ab", [cols(a["w_in_ab"], CH * i, CH) for i in (0, 2, 1)])
        add("out_ab", [cols(a["w_out_ab"], CH * i, CH) for i in range(2)])
        add("in_cd", [cols(a["w_in_cd"], CH * i, min(CH, 1728 - CH * i)) for i in range(4)])
        add("uq", [a["w_uq"].rearrange("(k p) n -> p k n", p=P)])
        add("ukv", [a["w_ukv"].rearrange("(k p) n -> p k n", p=P)])
        add("out_cd", [cols(a["w_out_cd"], CH * i, CH) for i in range(2)])
        before_moe = [c0["in_cd"], len(chunks)]

        def slot(c, k=KT, n=CH):
            return ring[:, c % SLOTS, 0:k * n].rearrange("p (k n) -> p k n", k=k)

        def mslot(s, k=KT, n=CH):
            return ring[:, s, 0:k * n].rearrange("p (k n) -> p k n", k=k)

        def loads(c):
            return c // SLOTS + 1

        w_landed = sems("w_landed", SLOTS)

        full, free = sems("bank_full", 4), sems("bank_free", 4)
        u0, n_units = {}, 0
        for name, n in [("lru_in", 8), ("gates", 8), ("lru_out", 4), ("k", 4), ("v", 4), ("q", 4),
                        ("att", 3 * NH), ("attn_out", 4), ("in_ab", 12), ("dft1", 8), ("dft2", 4), ("out_ab", 8),
                        ("rows0", 8), ("logit0", 1), ("rank0", 2), ("comb0", 8),
                        ("in_cd", 11), ("ss", 6), ("rope_c", 3), ("uq", 4), ("ukv", 8), ("rope_d", 3),
                        ("soft", 48), ("out_cd", 4),
                        ("rows1", 4), ("logit1", 1), ("rank1", 2), ("comb1", 4)]:
            u0[name] = n_units
            n_units += n

        def bank(u, n=2 * S):
            return T[:, u % 4, 0:n]

        def pair(u):
            return T[:, u % 4, :].rearrange("p (a n) -> p a n", a=2)

        def take(pe, u):
            if u >= 4:
                pe.wait_ge(free[u % 4], u // 4)

        def got(eng, u):
            eng.wait_ge(full[u % 4], u // 4 + 1)

        def read(eng, u):
            eng.wait_ge(free[u % 4], u // 4 + 1)

        last_unit = {}
        last_unit.update({
            c0["lru_in"] + j: u0["lru_in"] + 2 * j + 1 for j in range(4)})
        last_unit.update({c0["gates"]: u0["gates"] + 7})
        last_unit.update({c0["lru_out"] + j: u0["lru_out"] + 2 * j + 1 for j in range(2)})
        last_unit.update({c0["kv"] + j: (u0["k"] + 2 * j + 1 if j < 2 else u0["v"] + 2 * j - 3) for j in range(4)})
        last_unit.update({c0["q"] + j: u0["q"] + 2 * j + 1 for j in range(2)})
        last_unit.update({c0["attn_out"] + j: u0["attn_out"] + 2 * j + 1 for j in range(2)})
        last_unit.update({c0["in_ab"] + j: u0["in_ab"] + 4 * j + 3 for j in range(3)})
        last_unit.update({c0["out_ab"] + j: u0["out_ab"] + 4 * j + 3 for j in range(2)})
        last_unit.update({c0["in_cd"] + j: u0["in_cd"] + (1, 5, 8, 10)[j] for j in range(4)})
        last_unit.update({c0["uq"]: u0["uq"] + 3, c0["ukv"]: u0["ukv"] + 7})
        last_unit.update({c0["out_cd"] + j: u0["out_cd"] + 2 * j + 1 for j in range(2)})

        def pipelined(n, base):
            order = [("a", 0), ("a", 1)]
            for i in range(n):
                order.append(("b", i))
                if i >= 1:
                    order.append(("c", i - 1))
                if i + 2 < n:
                    order.append(("a", i + 2))
            order.append(("c", n - 1))
            return order, {key: base + j for j, key in enumerate(order)}

        s_const, s_zero, s_in = sem("s_const"), sem("s_zero"), sem("s_in")
        s_c, s_cs = sem("s_c"), sem("s_cs")
        s_sp = sem("s_sp")
        xbr_ready, a_ready = sem("xbr_ready"), sem("a_ready")
        m2_ready, mult_ready, hy_ready = sem("m2_ready"), sem("mult_ready"), sem("hy_ready")
        ln_src, ln_mean, ln_xc, ln_sq, ln_var = sem("ln_src"), sem("ln_mean"), sem("ln_xc"), sem("ln_sq"), sem("ln_var")
        ln_std, ln_nrm, x_ready = sem("ln_std"), sem("ln_nrm"), sem("x_ready")
        f_full, f_id, f_conv, f_gelu = sem("f_full"), sem("f_id"), sem("f_conv"), sem("f_gelu")
        g_ready, g_used, acc_ready = sem("g_ready"), sem("g_used"), sem("acc_ready")
        mod_acc_ready, mod_sum, mod_out = sem("mod_acc_ready"), sem("mod_sum"), sem("mod_out")
        at_ln, at_l, at_e, at_w0, at_w = sem("at_ln"), sem("at_l"), sem("at_e"), sem("at_w0"), sem("at_w")
        gs_ready = sem("gs_ready")
        n_sq, n_ms, n_std, n_nrm, h_ready = sem("n_sq"), sem("n_ms"), sem("n_std"), sem("n_nrm"), sem("h_ready")
        yc_ready, yn_ready, yb_ready = sem("yc_ready"), sem("yn_ready"), sem("yb_ready")
        act_own, dve_own, pool_own = sem("act_own"), sem("dve_own"), sem("pool_own")
        s_out = sem("s_out")
        r = {k: sem(k) for k in (
            "rows_st", "ge", "gx", "m_ready", "dest", "planned", "zeroed", "scat", "m_full", "sg", "hT", "xT", "tr",
            "y_full", "m_act", "gathers", "y_all", "done", "cb")}
        for k, n in (("landed", MSLOTS), ("xg", 2), ("y_st", 2), ("ixl", 2), ("cg", 4)):
            r[k] = sems(k, n)
        cd_sq, cd_qk, cd_n, cd_rot = sem("cd_sq"), sem("cd_qk"), sem("cd_n"), sem("cd_rot")
        so_m, so_n = sem("so_m"), sem("so_n")
        block = ctx.enter_context(nc.Block())

        N_CONST = 8
        att_order, att_u = pipelined(NH, u0["att"])
        so_order, so_u = pipelined(16, u0["soft"])

        def turns(eng, l):
            n = [eng.value_load(plan[0:1, j, 0:1], min_val=1, max_val=NBLK[j] // 2) for j in range(l + 1)]
            return (0, n[0]) if l == 0 else (n[0], n[0] + n[1])

        def turn_of_layer(i, t0, l):
            return i if l == 0 else nc.s_assert_within(i - t0, 0, NBLK[l] // 2 - 1, skip_runtime_bounds_check_because=
                                                       "the loop runs from t0 over at most that many turns")

        ybr, xp, xbr, gi, gr, av = (part(S1, 0, 8, S), part(S1, 2048, 8, S), part(S2, 0, 8, S),
                                    part(S2, 2048, 8, S), part(S3, 0, 8, S), part(S3, 2048, 8, S))
        m2, uu, hs = part(H, 0, 8, S), part(H, 2048, 8, S), part(S1, 2048, 8, S)
        hy, lo = part(S3, 0, 8, S), part(S2, 2048, 8, S)
        lns, lxc, lsq = part(H, 0, 8, S), part(S3, 2048, 8, S), part(S3, 0, 8, S)
        hab, gT = part(S1, 0, 2, 2, S), part(S1, 1024, 2, S)
        macc = part(S1, 1536, 2, 2, CH)
        kT, vv, qT, oT = part(S1, 0, 8, S), part(S1, 2048, 2, D), part(S2, 0, 8, S), part(S2, 2048, 8, S)
        zs, ze, zl, zw = part(S3, 0, 2, 512), part(S3, 1024, 2, 512), part(S3, 2048, 2, 512), part(S3, 3072, 2, 512)
        U = part(S2, 0, 4, 2, S + 2 * PADC)
        fa = part(H, 0, 4, 4, 256)
        hrow = part(S2, 0, 4, D)
        xg, yb = part(S3, 0, 2, D), part(S3, 2048, 2, D)
        xgT, hT, sg = part(S1, 0, 2, 8 * P), part(S1, 2048, 2, 4 * P), part(S1, 3072, 4, P)
        qk, vC, cq = part(S1, 0, 4, 512), part(S1, 2048, 4, 256), part(S1, 3072, 3, S)
        ckv, kr, qn, qr = part(S2, 0, 2, 512), part(S2, 1024, 512), part(S2, 1536, 4, S), part(S2, 2560, 4, S)
        cdsq, cdr = part(S3, 0, 4, 512), part(H, 2048, 4, 512)
        kn, vD = part(S3, 0, 4, 512), part(S3, 2048, 4, 512)
        rtmp = part(H, 0, 4, 512)
        pp, pt, oo = part(H, 0, 2, 512), part(H, 1024, 2, 512), part(H, 2048, 8, S)

        def kt8(t, k, n=S):
            return t[:, k, 0:n]

        TT = [NTOK[l] // P for l in range(2)]

        nsq0 = [0, 4, 6, 10, 14, 18]
        ACT_F = ACT.Identity

        @block.sync
        def _(sp_):
            def released(c, i=None):
                for l in range(2):
                    j = c - c0[f"ffn{l}"]
                    if 0 <= j < 5 * NJ:
                        t = j // 5 if i is None else i
                        if j % 5 < 2:
                            sp_.wait_ge(f_full, 4 * t + (24 * l + 4))
                        elif j % 5 < 4:
                            sp_.wait_ge(mod_acc_ready, t + (NJ * l + 1))
                        else:
                            sp_.wait_ge(g_used, 4 * t + (24 * l + 6))
                        return
                u = last_unit[c]
                sp_.wait_ge(full[u % 4], u // 4 + 1)

            def static(c):
                if c >= SLOTS:
                    released(c - SLOTS)
                src = chunks[c]
                k, n = src.shape[1], src.shape[2]
                sp_.dma_start(slot(c, k, n), src).then_inc(w_landed[c % SLOTS], 16)

            def ffn(l):
                base = c0[f"ffn{l}"]
                up, down, mw = a["ffn_w_up"][l], a["ffn_w_down"][l], a["mod_w"][l]
                up = up.rearrange("(k p) n -> p k n", p=P)
                mw = mw.rearrange("(k p) n -> p k n", p=P)
                down = down.rearrange("(f p) n -> p f n", p=P)

                def turn(i):
                    return [up[:, :, ds(i * CH, CH)], up[:, :, ds(i * CH + FF, CH)], mw[:, :, ds(i * 2 * CH, CH)],
                            mw[:, :, ds(i * 2 * CH + CH, CH)], down[:, ds(i * MJ, MJ), :]]

                for j, src in enumerate(turn(0)):
                    released(base + j - SLOTS)
                    sp_.dma_start(slot(base + j, src.shape[1], src.shape[2]), src)\
                        .then_inc(w_landed[(base + j) % SLOTS], 16)
                with sp_.Fori(1, NJ) as i:
                    for j, src in enumerate(turn(i)):
                        released(base + j, i - 1)
                        sp_.dma_start(slot(base + j, src.shape[1], src.shape[2]), src)\
                            .then_inc(w_landed[(base + j) % SLOTS], 16)

            def moe(l):
                for c in range(before_moe[l] - SLOTS, before_moe[l]):
                    released(c)
                sp_.wait_ge(r["planned"], l + 1)
                t0, t1 = turns(sp_, l)
                with sp_.Fori(t0, t1) as i:
                    at = turn_of_layer(i, t0, l)
                    for s in range(2):
                        e = sp_.value_load(plan[0:1, l, ds(at * 2 + (1 + s), 1)], min_val=0, max_val=NE - 1)
                        for j, w in enumerate((a["exp_w_gate"], a["exp_w_up"], a["exp_w_down"])):
                            src = w[l][ds(e, 1)].rearrange("e (k p) n -> p (e k) n", p=P)
                            m = 3 * s + j
                            if j < 2:
                                sp_.wait_ge(r["m_full"], 8 * i + (4 * s + 4))
                            else:
                                sp_.wait_ge(r["y_full"], 4 * i + (2 * s + 2))
                            sp_.dma_start(mslot(m, src.shape[1], src.shape[2]), src).then_inc(r["landed"][m], 16)
                sp_.wait_ge(r["done"], l + 1)

            for c in range(0, c0["ffn0"]):
                static(c)
            ffn(0)
            for c in range(c0["kv"], c0["ffn1"]): static(c)
            ffn(1)
            for c in range(c0["in_ab"], c0["in_cd"]): static(c)
            moe(0)
            for c in range(c0["in_cd"], len(chunks)): static(c)
            moe(1)
            sp_.wait_ge(s_out, 16)

        @block.tensor
        def _(pe):
            def landed(c):
                pe.wait_ge(w_landed[c % SLOTS], 16 * loads(c))

            def dense(c, n_tiles, rhs, u, width, k_tiles=KT, n=CH, m0=0):
                w = slot(c, k_tiles, n)
                per = 512 // width
                for m in range(n_tiles):
                    if m % per == 0:
                        take(pe, u + m // per)
                    for k in range(k_tiles):
                        ins = pe.matmul(bank(u + m // per)[:, (m % per) * width:(m % per + 1) * width],
                                        w[:, k, (m0 + m) * P:(m0 + m + 1) * P], rhs(k),
                                        start=(k == 0), stop=(k == k_tiles - 1))
                    if m % per == per - 1 or m == n_tiles - 1:
                        ins.then_inc(full[(u + m // per) % 4], 1)

            def layer_norm(i):
                if i == 2:
                    read(pe, u0["attn_out"] + 3)
                else:
                    pe.wait_ge(ln_src, (1, 2, None, 3)[i])
                for k in range(KT):
                    ins = pe.matmul(T[:, 6, 0:S], ones, kt8(lns, k), start=(k == 0), stop=(k == KT - 1))
                ins.then_inc(ln_mean, 1)
                for k in range(KT):
                    if k % 2 == 0:
                        pe.wait_ge(ln_sq, 4 * i + k // 2 + 1)
                    ins = pe.matmul(T[:, 7, 0:S], ones, kt8(lsq, k), start=(k == 0), stop=(k == KT - 1))
                ins.then_inc(ln_var, 1)

            def ffn(l):
                base = c0[f"ffn{l}"]
                pe.wait_ge(x_ready, 8 * (2 * l + 1))
                for b in range(4):
                    ins = pe.matmul(T[:, 4 + b, :], zb[:, 0:P], zb[:, :], start=True, stop=False,
                                    skip_group_check=True)
                if l == 0:
                    ins.then_inc(g_used, 2)
                wa, wb, wd = slot(base), slot(base + 1), slot(base + 4, MJ, D)

                with pe.Fori(0, NJ) as i:
                    def up(m):
                        t = 4 * i + (24 * l + m + 1)
                        pe.wait_ge(f_conv, t)
                        for h, w in ((0, wa), (1, wb)):
                            for k in range(KT):
                                ins = pe.matmul(T[:, m % 2, h * S:(h + 1) * S], w[:, k, m * P:(m + 1) * P],
                                                x1[:, k, :], start=(k == 0), stop=(k == KT - 1))
                        ins.then_inc(f_full, 1)

                    def down(m):
                        pe.wait_ge(g_ready, 4 * i + (24 * l + m + 3))
                        for d in range(KT):
                            ins = pe.matmul(T[:, 4 + d // 2, (d % 2) * S:(d % 2 + 1) * S], wd[:, m, d * P:(d + 1) * P],
                                            gT[:, m % 2, :], start=False, stop=False, skip_group_check=True)
                        ins.then_inc(g_used, 1)

                    for j in range(2):
                        c = base + j
                        pe.wait_ge(w_landed[c % SLOTS], 16 * i + 16 * loads(c))
                    up(0)
                    up(1)
                    pe.wait_ge(w_landed[(base + 4) % SLOTS], 16 * i + 16 * loads(base + 4))
                    down(0)
                    up(2)
                    down(1)
                    up(3)
                    down(2)
                    pe.wait_ge(mod_acc_ready, i + (NJ * l + 1))
                    pe.wait_ge(mod_out, i + (NJ * l + 1))
                    for m in range(8):
                        for v in range(2):
                            ins = pe.matmul(T[:, 2, 2 * m + v:2 * m + v + 1],
                                            macc[:, m // 4, v, (m % 4) * P:(m % 4 + 1) * P], ones[:, 0:1],
                                            start=True, stop=True)
                    ins.then_inc(mod_sum, 1)
                    down(3)
                for b in range(4):
                    ins = pe.matmul(T[:, 4 + b, :], zb[:, 0:P], zb[:, :], start=False, stop=True,
                                    skip_group_check=True)
                ins.then_inc(acc_ready, 1)

            def norm(r, k_tiles=KT, n=N2, sq=S1, off=0):
                for k in range(k_tiles):
                    if k % 2 == 0:
                        pe.wait_ge(n_sq, nsq0[r] + k // 2 + 1)
                    ins = pe.matmul(T[:, 7, 0:n], ones, sq[:, off + k, 0:n], start=(k == 0), stop=(k == k_tiles - 1))
                ins.then_inc(n_ms, 1)

            def route(l):
                tt = TT[l]
                for t in range(tt):
                    for hf in range(2):
                        u = u0[f"rows{l}"] + 2 * t + hf
                        take(pe, u)
                        for k in range(4):
                            ins = pe.transpose(bank(u)[:, k * P:(k + 1) * P],
                                               H[:, 4 * hf + k, t * P:(t + 1) * P], ident)
                        ins.then_inc(full[u % 4], 1)
                u = u0[f"logit{l}"]
                take(pe, u)
                for t in range(tt):
                    for k in range(KT):
                        pe.matmul(bank(u)[:, t * 36:(t + 1) * 36], H[:, k, t * P:(t + 1) * P], rw[:, l, k, :],
                                  start=(k == 0), stop=False)
                    ins = pe.matmul(bank(u)[:, t * 36:(t + 1) * 36], ones[0:1, :], rb[0:1, l, :],
                                    start=False, stop=True)
                ins.then_inc(full[u % 4], 1)
                pe.wait_ge(r["m_ready"], l + 1)
                m_ = rt[:, 0:tt * NE].rearrange("p (t e) -> p t e", t=tt)
                u = u0[f"rank{l}"]
                take(pe, u)
                for t in range(tt):
                    for s in range(t + 1):
                        ins = pe.matmul(bank(u)[:, t * NE:(t + 1) * NE], tabv("before", P) if s == t else ones,
                                        m_[:, s, :], start=(s == 0), stop=(s == t))
                ins.then_inc(full[u % 4], 1)
                u += 1
                take(pe, u)
                for t in range(tt):
                    ins = pe.matmul(bank(u)[:, 0:NE], ones, m_[:, t, :], start=(t == 0), stop=(t == tt - 1))
                ins.then_inc(full[u % 4], 1)

            def experts(l):
                pe.wait_ge(r["planned"], l + 1)
                t0, t1 = turns(pe, l)
                if l == 0:
                    pe.sem_inc(r["tr"], 2)
                    pe.sem_inc(r["m_full"], 8)
                    pe.sem_inc(r["y_full"], 4)
                with pe.Fori(t0, t1) as i:
                    for s in range(2):
                        wg, wu, wd = mslot(3 * s), mslot(3 * s + 1), mslot(3 * s + 2, MJ, D)
                        pe.wait_ge(r["xT"], 2 * i + (s + 1))
                        pe.wait_ge(r["xg"][s], 16 * i + 16)
                        for k in range(KT):
                            ins = pe.transpose(T[:, 6 + k // 4, (k % 4) * P:(k % 4 + 1) * P],
                                               xg[:, s, k * P:(k + 1) * P], ident)
                        ins.then_inc(r["tr"], 1)
                        pe.wait_ge(r["landed"][3 * s], 16 * i + 16)
                        pe.wait_ge(r["landed"][3 * s + 1], 16 * i + 16)
                        pe.wait_ge(r["xT"], 2 * i + (s + 2))
                        for m in range(MJ):
                            pe.wait_ge(r["hT"], 8 * i + (4 * s + m + 1))
                            for h, w in ((0, wg), (1, wu)):
                                for k in range(KT):
                                    ins = pe.matmul(T[:, m, h * P:(h + 1) * P], w[:, k, m * P:(m + 1) * P],
                                                    xgT[:, s, k * P:(k + 1) * P], start=(k == 0), stop=(k == KT - 1))
                            ins.then_inc(r["m_full"], 1)
                        pe.wait_ge(r["landed"][3 * s + 2], 16 * i + 16)
                        pe.wait_ge(r["m_act"], 4 * i + (2 * s + 2))
                        for n in range(2):
                            for m in range(MJ):
                                if n == 0:
                                    pe.wait_ge(r["hT"], 8 * i + (4 * s + m + 5))
                                ins = pe.matmul(T[:, 4 + n, :], hT[:, s, m * P:(m + 1) * P],
                                                wd[:, m, n * 512:(n + 1) * 512], start=(m == 0), stop=(m == MJ - 1))
                            ins.then_inc(r["y_full"], 1)
                pe.sem_inc(r["done"], 1)

            def combine(l):
                tt = TT[l]
                pe.wait_ge(r["cb"], 4 + 2 * l)
                per = 4 // tt
                for k in range(KT):
                    u = u0[f"comb{l}"] + k // per
                    if k % per == 0:
                        take(pe, u)
                    for t in range(tt):
                        c = (k % per) * tt + t
                        ins = pe.transpose(bank(u)[:, c * P:(c + 1) * P],
                                           part(S1, 0, 4, D)[:, t, k * P:(k + 1) * P], ident)
                    if k % per == per - 1:
                        ins.then_inc(full[u % 4], 1)

            pe.wait_ge(s_const, 16 * N_CONST)
            pe.wait_ge(s_zero, 1)
            for c in range(4):
                landed(c)
                dense(c, 4, lambda k: x1[:, k, :], u0["lru_in"] + 2 * c, S)
            landed(4)
            for h in range(8):
                u = u0["gates"] + h
                take(pe, u)
                pe.wait_ge(xbr_ready, h + 1)
                for j in range(2):
                    ins = pe.matmul(pair(u)[:, j, :], slot(4, 8, 2 * P)[:, h, j * P:(j + 1) * P], kt8(xbr, h),
                                    start=True, stop=True)
                ins.then_inc(full[u % 4], 1)
            pe.wait_ge(hy_ready, 8)
            for j in range(2):
                landed(5 + j)
                dense(5 + j, 4, lambda k: kt8(hy, k), u0["lru_out"] + 2 * j, S)
            layer_norm(0)
            ffn(0)
            layer_norm(1)
            pe.wait_ge(x_ready, 16)
            for j in range(2):
                landed(c0["kv"] + j)
                dense(c0["kv"] + j, 4, lambda k: x1[:, k, :], u0["k"] + 2 * j, S)
            for j in range(2):
                c = c0["kv"] + 2 + j
                landed(c)
                for t in range(2):
                    u = u0["v"] + 2 * j + t
                    take(pe, u)
                    for k in range(KT):
                        ins = pe.matmul(bank(u), x1[:, k, t * P:(t + 1) * P], slot(c)[:, k, :],
                                        start=(k == 0), stop=(k == KT - 1))
                    ins.then_inc(full[u % 4], 1)
            for j in range(2):
                landed(c0["q"] + j)
                dense(c0["q"] + j, 4, lambda k: x1[:, k, :], u0["q"] + 2 * j, S)
            read(pe, u0["q"] + 3)
            read(pe, u0["v"] + 3)
            for what, h in att_order:
                u = att_u[what, h]
                take(pe, u)
                if what == "a":
                    for t in range(2):
                        ins = pe.matmul(pair(u)[:, t, :], kT[:, h, t * P:(t + 1) * P], qT[:, h, :],
                                        start=True, stop=True)
                elif what == "b":
                    pe.wait_ge(at_l, h + 1)
                    ll = zl[:, h % 2, :].rearrange("p (t q) -> p t q", t=2)
                    pe.matmul(pair(u)[:, 0, :], tabv("suffix", P), ll[:, 0, :], start=True, stop=False)
                    pe.matmul(pair(u)[:, 0, :], ones, ll[:, 1, :], start=False, stop=True)
                    ins = pe.matmul(pair(u)[:, 1, :], tabv("suffix", P), ll[:, 1, :], start=True, stop=True)
                else:
                    pe.wait_ge(at_w, h + 1)
                    ww = zw[:, h % 2, :].rearrange("p (t q) -> p t q", t=2)
                    for t in range(2):
                        ins = pe.matmul(bank(u, S), vv[:, t, h * P:(h + 1) * P], ww[:, t, :],
                                        start=(t == 0), stop=(t == 1))
                ins.then_inc(full[u % 4], 1)
            read(pe, att_u["c", NH - 1])
            for j in range(2):
                c = c0["attn_out"] + j
                landed(c)
                dense(c, 4, lambda k: kt8(oT, k), u0["attn_out"] + 2 * j, S)
            layer_norm(2)
            ffn(1)
            layer_norm(3)
            norm(0)
            pe.wait_ge(h_ready, 8)
            for j in range(3):
                c = c0["in_ab"] + j
                landed(c)
                dense(c, 4, lambda k: H[:, k, :], u0["in_ab"] + 4 * j, N2)
            read(pe, u0["in_ab"] + 3)
            for g in range(4):
                for st in range(2):
                    u = u0["dft1"] + 2 * g + st
                    take(pe, u)
                    for t in range(2):
                        ins = pe.matmul(pair(u)[:, t, :], S1[:, g, (2 * st + t) * P:(2 * st + t + 1) * P],
                                        tabv("dft_d", 256), start=True, stop=True)
                    ins.then_inc(full[u % 4], 1)
            for g in range(4):
                u = u0["dft2"] + g
                take(pe, u)
                read(pe, u0["dft1"] + 7)
                for st in range(2):
                    for t in range(2):
                        pe.matmul(pair(u)[:, st, :], fa[:, 2 * st + t, g, 0:P], tabv("cos_l", S, t * S),
                                  start=(t == 0), stop=False)
                        ins = pe.matmul(pair(u)[:, st, :], fa[:, 2 * st + t, g, P:2 * P],
                                        tabv("sin_l", S, t * S), start=False, stop=(t == 1))
                ins.then_inc(full[u % 4], 1)
            norm(1, 4, sq=S1, off=4)
            read(pe, u0["dft2"] + 3)
            pe.wait_ge(yb_ready, 4)
            for j in range(2):
                c = c0["out_ab"] + j
                landed(c)
                dense(c, 4, lambda k: S1[:, k, :] if k < 4 else S3[:, k - 4, :], u0["out_ab"] + 4 * j, N2)
            norm(2, sq=S2)
            pe.wait_ge(h_ready, 16)
            route(0)
            experts(0)
            combine(0)
            norm(3, sq=S2)
            pe.wait_ge(h_ready, 24)
            u, c = u0["in_cd"], c0["in_cd"]
            landed(c)
            dense(c, 4, lambda k: H[:, k, 0:S], u, S)
            landed(c + 1)
            dense(c + 1, 2, lambda k: H[:, k, :], u + 2, N2)
            for t in range(4):
                if t % 2 == 0:
                    take(pe, u + 4 + t // 2)
                for k in range(KT):
                    ins = pe.matmul(pair(u + 4 + t // 2)[:, t % 2, :], H[:, k, t * P:(t + 1) * P],
                                    slot(c + 1)[:, k, 256:512], start=(k == 0), stop=(k == KT - 1))
                if t % 2 == 1:
                    ins.then_inc(full[(u + 4 + t // 2) % 4], 1)
            landed(c + 2)
            dense(c + 2, 3, lambda k: H[:, k, 0:S], u + 6, S)
            dense(c + 2, 1, lambda k: H[:, k, :], u + 8, N2, m0=3)
            landed(c + 3)
            dense(c + 3, 1, lambda k: H[:, k, :], u + 9, N2, n=192)
            take(pe, u + 10)
            for k in range(KT):
                ins = pe.matmul(bank(u + 10)[0:64, :], slot(c + 3, KT, 192)[:, k, P:192], H[:, k, :],
                                start=(k == 0), stop=(k == KT - 1))
            ins.then_inc(full[(u + 10) % 4], 1)
            u = u0["ss"]
            pe.wait_ge(cd_sq, 1)
            for j in range(4):
                take(pe, u + j)
                pe.matmul(bank(u + j), ones, cdsq[:, j, :], start=True, stop=True).then_inc(full[(u + j) % 4], 1)
            take(pe, u + 4)
            pe.wait_ge(cd_sq, 2)
            for k in range(3):
                ins = pe.matmul(bank(u + 4, S), ones, part(S3, 2048, 3, S)[:, k, :], start=(k == 0), stop=(k == 2))
            ins.then_inc(full[(u + 4) % 4], 1)
            take(pe, u + 5)
            for k in range(2):
                ins = pe.matmul(bank(u + 5), ones, part(S3, 3072, 2, 512)[:, k, :], start=(k == 0), stop=(k == 1))
            ins.then_inc(full[(u + 5) % 4], 1)
            u = u0["rope_c"]
            pe.wait_ge(cd_qk, 1)
            for j in range(3):
                take(pe, u + j)
                rhs = qk[:, j, :] if j < 2 else qk[:, 2:4, 0:S]
                out = bank(u + j) if j < 2 else pair(u + j)
                pe.matmul(out, tabv("swap", P), rhs, start=True, stop=True).then_inc(full[(u + j) % 4], 1)
            u, c = u0["uq"], c0["uq"]
            landed(c)
            pe.wait_ge(cd_n, 1)
            wq = slot(c, 3, 768)
            for h in range(4):
                if h % 2 == 0:
                    take(pe, u + h // 2)
                for k in range(3):
                    ins = pe.matmul(pair(u + h // 2)[:, h % 2, :], wq[:, k, h * 192:h * 192 + P], cq[:, k, :],
                                    start=(k == 0), stop=(k == 2))
                if h % 2 == 1:
                    ins.then_inc(full[(u + h // 2) % 4], 1)
            for h in range(4):
                if h % 2 == 0:
                    take(pe, u + 2 + h // 2)
                for k in range(3):
                    ins = pe.matmul(pair(u + 2 + h // 2)[0:64, h % 2, :], wq[:, k, h * 192 + P:(h + 1) * 192],
                                    cq[:, k, :], start=(k == 0), stop=(k == 2))
                if h % 2 == 1:
                    ins.then_inc(full[(u + 2 + h // 2) % 4], 1)
            u, c = u0["ukv"], c0["ukv"]
            landed(c)
            pe.wait_ge(cd_n, 2)
            wk = slot(c, 2, D)
            for h in range(4):
                take(pe, u + h)
                for k in range(2):
                    ins = pe.matmul(bank(u + h), wk[:, k, h * 256:h * 256 + P], ckv[:, k, :],
                                    start=(k == 0), stop=(k == 1))
                ins.then_inc(full[(u + h) % 4], 1)
            for t in range(4):
                take(pe, u + 4 + t)
                for k in range(2):
                    ins = pe.matmul(bank(u + 4 + t).rearrange("p (h d) -> p h d", h=4),
                                    ckv[:, k, t * P:(t + 1) * P],
                                    wk[:, k, :].rearrange("p (h d) -> p h d", h=4)[:, :, P:256],
                                    start=(k == 0), stop=(k == 1))
                ins.then_inc(full[(u + 4 + t) % 4], 1)
            u = u0["rope_d"]
            read(pe, u0["uq"] + 3)
            for j in range(3):
                take(pe, u + j)
                rhs = part(S2, 2560 + 512 * j, 512)[0:64, :] if j < 2 else kr[0:64, 0:S]
                pe.matmul(bank(u + j, 512 if j < 2 else S)[0:64, :], tabv("swap", 64, rows=64), rhs,
                          start=True, stop=True).then_inc(full[(u + j) % 4], 1)
            pe.wait_ge(cd_rot, 2)
            read(pe, u0["ukv"] + 7)
            for what, n in so_order:
                u, h, t = so_u[what, n], n // 2, n % 2
                take(pe, u)
                if what == "a":
                    if h < 4:
                        ins = pe.matmul(bank(u), part(S1, h * S, S)[:, t * P:(t + 1) * P], qk[:, 2 + h // 2, :],
                                        start=True, stop=True)
                    else:
                        pe.matmul(bank(u), qn[:, h - 4, t * P:(t + 1) * P], kn[:, h - 4, :], start=True, stop=False)
                        ins = pe.matmul(bank(u), qr[0:64, h - 4, t * P:(t + 1) * P], kr[0:64, :],
                                        start=False, stop=True)
                elif what == "b":
                    pe.wait_ge(so_n, n + 1)
                    for k in range(4):
                        ins = pe.transpose(bank(u)[:, k * P:(k + 1) * P], pp[:, n % 2, k * P:(k + 1) * P], ident)
                else:
                    read(pe, so_u["b", n])
                    for k in range(4):
                        v = (vC[:, k, (h // 2) * P:(h // 2 + 1) * P] if h < 4 else
                             vD[:, k, (h - 4) * P:(h - 3) * P])
                        ins = pe.matmul(bank(u, P), v, pt[:, n % 2, k * P:(k + 1) * P],
                                        start=(k == 0), stop=(k == 3))
                ins.then_inc(full[u % 4], 1)
            read(pe, so_u["c", 15])
            for j in range(2):
                c = c0["out_cd"] + j
                landed(c)
                dense(c, 4, lambda k: kt8(oo, k), u0["out_cd"] + 2 * j, S)
            norm(4, n=S)
            pe.wait_ge(h_ready, 32)
            route(1)
            experts(1)
            combine(1)
            norm(5, n=S, sq=S2)


        @block.scalar
        def _(act):
            own = Chain(act, act_own)
            A = nc.scalar.activation

            def layer_norm(i):
                for j in range(4):
                    if j == 0:
                        act.wait_ge(ln_xc, i + 1)
                    A(lsq[:, 2 * j:2 * j + 2, :], lxc[:, 2 * j:2 * j + 2, :], ACT.Square).then_inc(ln_sq, 1)
                act.wait_ge(ln_var, i + 1)
                A(std[:, 0, 0:S], T[:, 7, 0:S], ACT.Sqrt, scale=1.0 / D, bias=LN_EPS).then_inc(ln_std, 1)
                for k in range(KT):
                    act.wait_ge(ln_nrm, 8 * i + k + 1)
                    A(x1[:, k, :], lns[:, k, :], ACT_F, bias=vc("ln_b", 8 * i + k)).then_inc(x_ready, 1)

            def ffn(l):
                with act.Fori(0, NJ) as i:
                    for m in range(4):
                        bi = i * 4
                        for h in range(2):
                            cw = 3 * 48 * l + 2 * 48 + 24 * h + m
                            cb = 48 * l + 24 * h + m
                            if h == 0:
                                act.wait_ge(g_ready, 4 * i + (24 * l + m + 1))
                                act.wait_ge(f_full, 4 * i + (24 * l + m + 1))
                            A(hab[:, m % 2, h, :], T[:, m % 2, h * S:(h + 1) * S], ACT_F,
                              scale=vec[:, ds(bi + (VEC["ffn_conv_w"] + cw), 1)],
                              bias=vec[:, ds(bi + (VEC["ffn_conv_b"] + cb), 1)]).then_inc(f_id, 1)
                        act.wait_ge(f_conv, 4 * i + (24 * l + m + 3))
                        A(hab[:, m % 2, 0, :], hab[:, m % 2, 0, :], ACT.Gelu_apprx_tanh).then_inc(f_gelu, 1)

            def norm(r, src, k_tiles=KT, n=N2, sq=S1, off=0, wait=None, shift=None):
                for j in range(k_tiles // 2):
                    if wait is not None:
                        wait(2 * j + 1)
                    A(sq[:, off + 2 * j:off + 2 * j + 2, 0:n], src[:, 2 * j:2 * j + 2, 0:n],
                      ACT.Square).then_inc(n_sq, 1)
                act.wait_ge(n_ms, r + 1)
                A(std[:, 0, 0:n], T[:, 7, 0:n], ACT.Sqrt, scale=1.0 / (k_tiles * P), bias=RMS_EPS).then_inc(n_std, 1)
                if shift is not None:
                    l, w, q = shift
                    streams = n // S
                    for k in range(KT):
                        act.wait_ge(n_nrm, 8 * q + k + 1)
                        for v in range(streams):
                            ins = A(H[:, k, v * S:(v + 1) * S], H[:, k, v * S:(v + 1) * S], ACT_F,
                                    bias=modv[:, l, 24 * w + k, v:v + 1])
                        ins.then_inc(h_ready, 1)

            def evac(u, out, n=512, rows=P, in_=None, scale=1.0, func=ACT_F, bias=0.0):
                got(act, u)
                A(out, bank(u, n)[0:rows, :] if in_ is None else in_, func, scale=scale, bias=bias)\
                    .then_inc(free[u % 4], 1)

            def route(l):
                tt = TT[l]
                for t in range(tt):
                    u = u0[f"rows{l}"] + 2 * t
                    evac(u, hrow[:, t, 0:512])
                act.wait_ge(r["ge"], l + 1)
                A(rt[:, 512:512 + 5 * tt], rt[:, 512:512 + 5 * tt], ACT.Exp).then_inc(r["gx"], 1)

            def experts(l):
                nc.scalar.preload_act_table(ACT.Silu)
                act.wait_ge(r["planned"], l + 1)
                t0, t1 = turns(act, l)
                if l == 0:
                    for s in range(2):
                        act.sem_inc(r["y_st"][s], 16)
                    act.sem_inc(r["m_act"], 2)
                with act.Fori(t0, t1) as i:
                    at = turn_of_layer(i, t0, l)
                    for s in range(2):
                        for m in range(MJ):
                            act.wait_ge(r["hT"], 8 * i + (4 * s + m + 1))
                            act.wait_ge(r["m_full"], 8 * i + (4 * s + m + 9))
                            A(sg[:, m, :], T[:, m, 0:P], ACT.Silu).then_inc(r["sg"], 1)
                        act.wait_ge(r["y_st"][s], 16 * i + 16)
                        for n in range(2):
                            act.wait_ge(r["y_full"], 4 * i + (2 * s + n + 5))
                            A(yb[:, s, n * 512:(n + 1) * 512], T[:, 4 + n, :], ACT.Copy).then_inc(r["m_act"], 1)
                        act.wait_ge(r["m_act"], 4 * i + (2 * s + 4))
                        act.dma_start(y_rows[ds(at * (2 * B) + s * B, B), :], yb[:, s, :]).then_inc(r["y_st"][s], 16)
                for s in range(2):
                    act.wait_ge(r["y_st"][s], t1 * 16 + 16)
                act.sem_inc(r["y_all"], 1)

            act.wait_ge(s_sp, 1)
            A(sp[:, 1, :], sp[:, 0, :], ACT.Exp, scale=-1.0).then_inc(s_sp, 1)
            act.wait_ge(s_const, 16 * N_CONST)
            A(cs[:, :], vc("c", 0, 16), ACT.Sigmoid).then_inc(s_cs, 1)
            for u in range(8):
                got(act, u)
                for j in range(2):
                    m = 2 * u + j
                    if m < 8:
                        ins = A(ybr[:, m, :], pair(u)[:, j, :], ACT.Gelu_apprx_tanh, bias=vc("lru_b_in", m))
                    else:
                        ins = A(xp[:, m - 8, :], pair(u)[:, j, :], ACT_F, bias=vc("lru_b_in", m))
                ins.then_inc(free[u % 4], 1)
            for h in range(8):
                u = u0["gates"] + h
                got(act, u)
                A(gi[:, h, :], pair(u)[:, 0, :], ACT.Sigmoid, bias=vc("lru_b_gates", h))
                A(gr[:, h, :], pair(u)[:, 1, :], ACT.Sigmoid, bias=vc("lru_b_gates", 8 + h))\
                    .then_inc(free[u % 4], 1)
            read(act, u0["gates"] + 7)
            act.wait_ge(s_sp, 3)
            for k in range(8):
                A(av[:, k, :], gr[:, k, :], ACT.Exp, scale=sp[:, 6, k:k + 1])
                A(m2[:, k, :], gr[:, k, :], ACT.Exp, scale=sp[:, 7, k:k + 1]).then_inc(a_ready, 1)
            act.wait_ge(m2_ready, 1)
            A(m2[:, :, :], m2[:, :, :], ACT.Sqrt).then_inc(mult_ready, 1)
            for j in range(4):
                u = u0["lru_out"] + j
                got(act, u)
                for h in range(2):
                    ins = A(lo[:, 2 * j + h, :], pair(u)[:, h, :], ACT_F, bias=vc("lru_b_out", 2 * j + h))
                ins.then_inc(free[u % 4], 1)
            layer_norm(0)
            ffn(0)
            layer_norm(1)
            for j in range(4):
                evac(u0["k"] + j, kT[:, 2 * j:2 * j + 2, :], in_=pair(u0["k"] + j))
            for j in range(4):
                evac(u0["q"] + j, qT[:, 2 * j:2 * j + 2, :], in_=pair(u0["q"] + j))
            nc.scalar.preload_act_table_set("natural_log_exp_and_others")
            for h in range(NH + 2):
                if h < NH:
                    if h >= 2:
                        act.wait_ge(at_w, h - 1)
                    evac(att_u["a", h], zs[:, h % 2, :], scale=float(P) ** -0.5)
                    read(act, att_u["a", h])
                    own(A(ze[:, h % 2, :], zs[:, h % 2, :], ACT.Abs))
                    own(A(ze[:, h % 2, :], ze[:, h % 2, :], ACT.Exp, scale=-1.0))
                    A(ze[:, h % 2, :], ze[:, h % 2, :], ACT.Ln, bias=1.0).then_inc(at_ln, 1)
                if 1 <= h <= NH:
                    act.wait_ge(at_e, h)
                    A(zw[:, (h - 1) % 2, :], zw[:, (h - 1) % 2, :], ACT.Exp).then_inc(at_w0, 1)
                if h >= 2:
                    evac(att_u["c", h - 2], oT[:, h - 2, :], n=S)
            layer_norm(2)
            ffn(1)
            layer_norm(3)
            act.wait_ge(gs_ready, 1)
            act.wait_ge(x_ready, 32)
            norm(0, X, shift=(0, 0, 0))
            for m in range(4):
                evac(u0["in_ab"] + m, S1[:, m, :])
            for m in range(4):
                evac(u0["in_ab"] + 4 + m, S1[:, 4 + m, :], func=ACT.Sigmoid)
            for g in range(4):
                for st in range(2):
                    u = u0["dft1"] + 2 * g + st
                    evac(u, fa[:, 2 * st:2 * st + 2, g, :], in_=pair(u))
            for g in range(4):
                evac(u0["dft2"] + g, S1[:, g, :])
            norm(1, S3, 4, sq=S1, off=4, wait=lambda k: act.wait_ge(yc_ready, 1))
            for m in range(4):
                act.wait_ge(yn_ready, m + 1)
                A(S3[:, m, :], S3[:, m, :], ACT.Silu).then_inc(yb_ready, 1)
            norm(2, X, sq=S2, wait=lambda k: read(act, u0["out_ab"] + k), shift=(0, 1, 1))
            route(0)
            experts(0)
            norm(3, X, sq=S2, wait=lambda k: read(act, u0["comb0"] + k), shift=(1, 0, 2))
            u = u0["in_cd"]
            for j in range(2):
                evac(u + j, part(S1, 512 * j, 512))
            for j in range(2):
                evac(u + 2 + j, qk[:, 2 + j, :])
            for j in range(2):
                evac(u + 4 + j, part(S1, 2048 + 512 * j, 512))
            evac(u + 6, part(S1, 3072, 512))
            evac(u + 7, part(S1, 3584, 256), n=256)
            for j in range(2):
                evac(u + 8 + j, ckv[:, j, :])
            evac(u + 10, kr[0:64, :], rows=64)
            read(act, u + 3)
            A(flat(S3)[:, 0:2048], flat(S1)[:, 0:2048], ACT.Square).then_inc(cd_sq, 1)
            read(act, u + 10)
            A(part(S3, 2048, 768), part(S1, 3072, 768), ACT.Square)
            A(part(S3, 3072, 1024), part(S2, 0, 1024), ACT.Square).then_inc(cd_sq, 1)
            u = u0["ss"]
            for j in range(4):
                evac(u + j, cdr[:, j, :], func=ACT.Sqrt, scale=1.0 / P, bias=RMS_EPS)
            evac(u + 4, std[:, 0, 0:S], n=S, func=ACT.Sqrt, scale=1.0 / 384, bias=RMS_EPS)
            evac(u + 5, std[:, 1, :], func=ACT.Sqrt, scale=1.0 / 256, bias=RMS_EPS)
            u = u0["uq"]
            for j in range(2):
                evac(u + j, part(S2, 1536 + 512 * j, 512))
            for j in range(2):
                evac(u + 2 + j, part(S2, 2560 + 512 * j, 512)[0:64, :], rows=64)
            u = u0["ukv"]
            for j in range(4):
                evac(u + j, kn[:, j, :])
            for j in range(4):
                evac(u + 4 + j, vD[:, j, :])
            for n in range(16 + 2):
                if n < 16:
                    h = n // 2
                    scale = float(P) ** -0.5 if h < 4 else 192.0 ** -0.5
                    got(act, so_u["a", n])
                    act.wait_ge(so_m, n + 1)
                    if n >= 2:
                        got(act, so_u["b", n - 2])
                    A(pp[:, n % 2, :], bank(so_u["a", n]), ACT.Exp, scale=scale, bias=rt[:, 2 * n:2 * n + 1],
                      accum_out=rt[:, 64 + 2 * n:65 + 2 * n]).then_inc(free[so_u["a", n] % 4], 1)
                if n >= 2:
                    h, t = (n - 2) // 2, n % 2
                    evac(so_u["c", n - 2], oo[:, h, t * P:(t + 1) * P], n=P)
            norm(4, X, n=S, wait=lambda k: read(act, u0["out_cd"] + k // 2), shift=(1, 1, 3))
            route(1)
            experts(1)
            norm(5, X, n=S, sq=S2, wait=lambda k: read(act, u0["comb1"] + k // 2))

        @block.vector
        def _(dve):
            own = Chain(dve, dve_own)
            V = nc.vector
            STT = V.scalar_tensor_tensor

            def layer_norm(i):
                dve.wait_ge(ln_mean, i + 1)
                STT(out=lxc, in0=T[:, 6:7, 0:S].to_broadcast([P, KT, S]), scalar=-1.0 / D, in1=lns,
                    op0=ALU.mult, op1=ALU.add).then_inc(ln_xc, 1)
                dve.wait_ge(ln_std, i + 1)
                own(V.reciprocal(std[:, 1, 0:S], std[:, 0, 0:S]))
                dve.wait_ge(ln_xc, i + 1)
                for k in range(KT):
                    STT(out=lns[:, k, :], in0=lxc[:, k, :], scalar=vc("ln_g", 8 * i + k), in1=std[:, 1, 0:S],
                        op0=ALU.mult, op1=ALU.mult).then_inc(ln_nrm, 1)

            def residual(units, i):
                for j, u in enumerate(units):
                    got(dve, u)
                    for h in range(2):
                        k = 2 * j + h
                        ins = STT(out=lns[:, k, :], in0=x1[:, k, :], scalar=ALPHA, in1=pair(u)[:, h, :],
                                  op0=ALU.mult, op1=ALU.add)
                    ins.then_inc(free[u % 4], 1)

            def ffn(l):
                base = c0[f"ffn{l}"]
                if l == 0:
                    dve.sem_inc(f_conv, 2)
                    dve.sem_inc(g_ready, 2)
                    dve.sem_inc(mod_out, 1)
                    dve.wait_ge(s_cs, 2)
                own.loop(None, 0)
                with dve.Fori(0, NJ) as i:
                    own.loop(i, 4 * 3 + 31)

                    def mod_steps(first, n):
                        for q in range(first, first + n):
                            k, j, v = q // 4, (q // 2) % 2, q % 2
                            c = base + 2 + j
                            if k == 0 and v == 0:
                                dve.wait_ge(w_landed[c % SLOTS], 16 * i + 16 * loads(c))
                            w, sc = slot(c)[:, k, :], cs[:, 8 * v + k:8 * v + k + 1]
                            if k == 0:
                                ins = V.tensor_scalar(macc[:, j, v, :], w, sc, None, ALU.mult)
                            else:
                                own.wait(last[j, v])
                                ins = STT(out=macc[:, j, v, :], in0=w, scalar=sc, in1=macc[:, j, v, :],
                                          op0=ALU.mult, op1=ALU.add)
                            if q == 31:
                                ins.then_inc(mod_acc_ready, 1)
                            else:
                                last[j, v] = own.mark(ins)

                    last = {}
                    for m in range(4):
                        t = 4 * i + (24 * l + m)
                        b = m % 2

                        def tap(h, w, shift):
                            cw = 3 * 48 * l + w * 48 + 24 * h + m
                            return STT(out=hab[:, b, h, shift:S], in0=T[:, b, h * S:(h + 1) * S - shift],
                                       scalar=vec[:, ds(i * 4 + (VEC["ffn_conv_w"] + cw), 1)],
                                       in1=hab[:, b, h, shift:S], op0=ALU.mult, op1=ALU.add)

                        dve.wait_ge(f_id, 8 * i + (48 * l + 2 * m + 2))
                        n1 = own.mark(tap(0, 1, 1))
                        n2 = own.mark(tap(1, 1, 1))
                        own.wait(n1)
                        n3 = own.mark(tap(0, 0, 2))
                        own.wait(n2)
                        tap(1, 0, 2).then_inc(f_conv, 1)
                        dve.wait_ge(f_gelu, t + 1)
                        dve.wait_ge(g_used, t + 1)
                        V.tensor_tensor(gT[:, b, :], hab[:, b, 0, :], hab[:, b, 1, :], ALU.mult).then_inc(g_ready, 1)
                        if m < 3:
                            mod_steps((0, 12, 24)[m], (12, 12, 8)[m])
                    dve.wait_ge(mod_sum, i + (NJ * l + 1))
                    V.tensor_tensor(modv[:, l, ds(i * 8, 8), :], T[:, 2, 0:16].rearrange("p (m v) -> p m v", v=2),
                                    vec[:, ds(i * 8 + (VEC["mod_b"] + 48 * l), 8)].unsqueeze(2)
                                    .to_broadcast([P, 8, 2]), ALU.add).then_inc(mod_out, 1)
                own.end_loop(NJ)
                dve.wait_ge(acc_ready, l + 1)
                for k in range(KT):
                    ins = STT(out=lns[:, k, :], in0=x1[:, k, :], scalar=ALPHA,
                              in1=T[:, 4 + k // 2, (k % 2) * S:(k % 2 + 1) * S], op0=ALU.mult, op1=ALU.add)
                ins.then_inc(ln_src, 1)

            def norm(r, gain, n=N2, out=H, q=None):
                dve.wait_ge(n_std, r + 1)
                own(V.reciprocal(std[:, 1, 0:n], std[:, 0, 0:n]))
                for k in range(KT):
                    for v in range(n // S):
                        ins = STT(out=out[:, k, v * S:(v + 1) * S], in0=X[:, k, v * S:(v + 1) * S],
                                  scalar=gain(k, v), in1=std[:, 1, v * S:(v + 1) * S], op0=ALU.mult, op1=ALU.mult)
                    ins.then_inc(n_nrm, 1)

            def add_gated(u, k, l, which, width, half_=None):
                for v in range(width // S):
                    src = bank(u)[:, v * S:(v + 1) * S] if half_ is None else pair(u)[:, half_, :]
                    ins = STT(out=X[:, k, v * S:(v + 1) * S], in0=src, scalar=modv[:, l, which * 8 + k, v:v + 1],
                              in1=X[:, k, v * S:(v + 1) * S], op0=ALU.mult, op1=ALU.add)
                return ins

            def route(l):
                tt = TT[l]
                for t in range(tt):
                    u = u0[f"rows{l}"] + 2 * t + 1
                    got(dve, u)
                    V.tensor_copy(hrow[:, t, 512:1024], bank(u)).then_inc(free[u % 4], 1)
                n = tt * NE
                v3 = lambda off, w: rt[:, off:off + tt * w].rearrange("p (t e) -> p t e", t=tt)
                M, oh1, oh2, tmp = v3(0, NE), v3(128, NE), v3(256, NE), v3(384, NE)
                ge, gap = v3(512, 4), v3(512 + 4 * tt, 1)
                lg, t4, ohg = v3(544, 36), v3(688, 4), v3(704, 4)
                gm, gi_, m1, i1, m2_, w1, w2, gp = (v3(720 + 4 * j, 1) for j in range(8))
                cnt, nb, ends, st = (rt[:, 752 + 32 * j:784 + 32 * j] for j in range(4))
                bc = lambda x, w: x.to_broadcast([P, tt, w])
                iota = lambda w: tab[:, TAB["iota"]:TAB["iota"] + w].unsqueeze(1).to_broadcast([P, tt, w])
                u = u0[f"logit{l}"]
                got(dve, u)
                ins = V.tensor_copy(lg, bank(u, tt * 36).rearrange("p (t e) -> p t e", t=tt))
                ins.then_inc(free[u % 4], 1)
                read(dve, u)
                G, E = lg[:, :, 0:4], lg[:, :, 4:36]
                own(V.tensor_reduce(gm, G, AX.X, ALU.max))
                own(V.tensor_tensor(ge, G, bc(gm, 4), ALU.subtract))
                own(V.tensor_tensor(t4, G, bc(gm, 4), ALU.is_equal))
                own(STT(out=t4, in0=t4, scalar=-100.0, in1=iota(4), op0=ALU.mult, op1=ALU.add))
                own(V.tensor_reduce(gi_, t4, AX.X, ALU.min))
                own(V.tensor_tensor(ohg, t4, bc(gi_, 4), ALU.is_equal))
                own(V.tensor_scalar(ohg, ohg, -1.0, 1e30, ALU.add, ALU.mult))
                E4 = E.rearrange("p t (g e) -> p t g e", g=4)
                own(V.tensor_tensor(E4, E4, ohg.unsqueeze(3).to_broadcast([P, tt, 4, 8]), ALU.add))
                for m_, i_, oh in ((m1, i1, oh1), (m2_, i1, oh2)):
                    own(V.tensor_reduce(m_, E, AX.X, ALU.max))
                    own(V.tensor_tensor(tmp, E, bc(m_, NE), ALU.is_equal))
                    own(STT(out=tmp, in0=tmp, scalar=-100.0, in1=iota(NE), op0=ALU.mult, op1=ALU.add))
                    own(V.tensor_reduce(i_, tmp, AX.X, ALU.min))
                    own(V.tensor_tensor(oh, tmp, bc(i_, NE), ALU.is_equal))
                    if oh is oh1:
                        own(STT(out=E, in0=oh, scalar=-2e30, in1=E, op0=ALU.mult, op1=ALU.add))
                V.tensor_tensor(M, oh1, oh2, ALU.add).then_inc(r["m_ready"], 1)
                V.tensor_tensor(gap, m2_, m1, ALU.subtract).then_inc(r["ge"], 1)
                dve.wait_ge(r["gx"], l + 1)
                own(V.tensor_reduce(gp, ge, AX.X, ALU.add))
                own(V.tensor_scalar(w1, gap, 1.0, None, ALU.add))
                own(V.tensor_tensor(w1, w1, gp, ALU.mult))
                own(V.reciprocal(w1, w1))
                own(V.tensor_tensor(w2, w1, gap, ALU.mult))
                u = u0[f"rank{l}"]
                got(dve, u + 1)
                nth = NTOK[l] // B
                V.tensor_copy(cnt, bank(u + 1, NE)).then_inc(free[(u + 1) % 4], 1)
                read(dve, u + 1)
                own(V.tensor_tensor(tmp_th(nth), cnt.unsqueeze(2).to_broadcast([P, NE, nth]),
                                tab[:, TAB["thresh"]:TAB["thresh"] + nth].unsqueeze(1).to_broadcast([P, NE, nth]),
                                ALU.is_gt))
                own(V.tensor_reduce(nb.unsqueeze(2), tmp_th(nth), AX.X, ALU.add))
                own(V.tensor_tensor_scan(ends, ones[:, 0:NE], nb, 0.0, ALU.mult, ALU.add))
                own(V.tensor_tensor(st, ends, nb, ALU.subtract))
                own(V.tensor_scalar(st, st, float(B), None, ALU.mult))
                got(dve, u)
                V.tensor_tensor(tmp, bank(u, n).rearrange("p (t e) -> p t e", t=tt),
                                st.unsqueeze(1).to_broadcast([P, tt, NE]), ALU.add).then_inc(free[u % 4], 1)
                read(dve, u)
                own(V.tensor_tensor(oh1, oh1, tmp, ALU.mult))
                own(V.tensor_tensor(oh2, oh2, tmp, ALU.mult))
                own(V.tensor_reduce(gm, oh1, AX.X, ALU.add))
                own(V.tensor_reduce(gi_, oh2, AX.X, ALU.add))
                own(V.tensor_copy(dst[:, 0:tt, 0:1], gm))
                V.tensor_copy(dst[:, 0:tt, 1:2], gi_).then_inc(r["dest"], 1)
                nb_ = NBLK[l]
                cmp_ = flat(H)[0:1, 0:nb_ * NE].rearrange("p (b e) -> p b e", b=nb_)
                io = tab[0:1, TAB["iota"]:TAB["iota"] + nb_]
                fl = rt[0:1, 880:880 + nb_ + 1]
                dve.wait_ge(r["rows_st"], 16 * (l + 1))
                own(V.tensor_tensor(cmp_, ends[0:1, :].unsqueeze(1).to_broadcast([1, nb_, NE]),
                                    io.unsqueeze(2).to_broadcast([1, nb_, NE]), ALU.is_le))
                own(V.tensor_reduce(fl[:, 1:nb_ + 1].unsqueeze(2), cmp_, AX.X, ALU.add))
                own(V.tensor_scalar(fl[:, 1:nb_ + 1], fl[:, 1:nb_ + 1], float(NE - 1), None, ALU.min))
                own(V.tensor_scalar(cmp_[:, 0, 0:nb_ // 2], io[:, 0:nb_ // 2], 2.0, ends[0:1, NE - 1:NE], ALU.mult,
                                    ALU.is_lt))
                own(V.tensor_reduce(fl[:, 0:1], cmp_[:, 0, 0:nb_ // 2], AX.X, ALU.add))
                V.tensor_copy(plan[0:1, l, 0:nb_ + 1], fl).then_inc(r["planned"], 1)

            def tmp_th(nth):
                return rt[:, 384:384 + NE * nth].rearrange("p (e j) -> p e j", e=NE)

            def experts(l):
                dve.wait_ge(r["planned"], l + 1)
                t0, t1 = turns(dve, l)
                if l == 0:
                    dve.sem_inc(r["hT"], 4)
                    dve.sem_inc(r["xT"], 1)
                with dve.Fori(t0, t1) as i:
                    for s in range(2):
                        dve.wait_ge(r["tr"], 2 * i + (s + 3))
                        V.tensor_copy(xgT[:, s, :].rearrange("p (a n) -> p a n", a=2), T[:, 6:8, :])\
                            .then_inc(r["xT"], 1)
                        for m in range(MJ):
                            dve.wait_ge(r["sg"], 8 * i + (4 * s + m + 1))
                            V.tensor_tensor(hT[:, s, m * P:(m + 1) * P], sg[:, m, :], T[:, m, P:2 * P], ALU.mult)\
                                .then_inc(r["hT"], 1)

            def combine(l):
                tt = TT[l]
                v3 = lambda off: rt[:, off:off + tt]
                w1, w2 = v3(740), v3(744)
                g0, g1 = part(S1, 0, 4, D), part(S2, 0, 4, D)
                for t in range(tt):
                    dve.wait_ge(r["cg"][t], 32 * (l + 1))
                    own(V.tensor_scalar(g0[:, t, :], g0[:, t, :], w1[:, t:t + 1], None, ALU.mult))
                    STT(out=g0[:, t, :], in0=g1[:, t, :], scalar=w2[:, t:t + 1], in1=g0[:, t, :],
                        op0=ALU.mult, op1=ALU.add).then_inc(r["cb"], 1)
                per = 4 // tt
                for k in range(KT):
                    u = u0[f"comb{l}"] + k // per
                    got(dve, u)
                    ins = add_gated(u, k, l, 5, tt * P, None if per == 1 else k % 2)
                    if k % per == per - 1:
                        ins.then_inc(free[u % 4], 1)

            V.memset(zb[:, :], 0.0).then_inc(s_zero, 1)
            dve.wait_ge(s_const, 16 * N_CONST)
            STT(out=sp[:, 0, :], in0=vc("lru_a", 0, 8), scalar=-1.0, in1=vc("lru_a", 0, 8), op0=ALU.mult, op1=ALU.max)\
                .then_inc(s_sp, 1)
            dve.wait_ge(s_sp, 2)
            e, t_, t2, q_ = sp[:, 1, :], sp[:, 2, :], sp[:, 3, :], sp[:, 4, :]
            own(V.tensor_scalar(t_, e, 2.0, None, ALU.add))
            own(V.reciprocal(t_, t_))
            own(V.tensor_tensor(t_, t_, e, ALU.mult))
            own(V.tensor_tensor(t2, t_, t_, ALU.mult))
            own(V.memset(q_, 1.0 / 17))
            for n in (15, 13, 11, 9, 7, 5, 3, 1):
                own(V.tensor_tensor(q_, q_, t2, ALU.mult))
                own(V.tensor_scalar(q_, q_, 1.0 / n, None, ALU.add))
            own(V.tensor_tensor(q_, q_, t_, ALU.mult))
            own(V.tensor_scalar(t_, vc("lru_a", 0, 8), -1.0, 0.0, ALU.mult, ALU.max))
            own(STT(out=q_, in0=q_, scalar=2.0, in1=t_, op0=ALU.mult, op1=ALU.add))
            own(V.tensor_scalar(sp[:, 6, :], q_, -8.0, None, ALU.mult))
            V.tensor_scalar(sp[:, 7, :], q_, -16.0, None, ALU.mult).then_inc(s_sp, 1)
            dve.wait_ge(s_cs, 1)
            V.tensor_tensor(cs[:, :], cs[:, :], vc("c", 0, 16), ALU.mult).then_inc(s_cs, 1)
            for k in range(8):
                read(dve, 4 + k // 2)
                cw = lambda t: vc("lru_conv_w", 8 * t + k)
                own(V.tensor_scalar(xbr[:, k, :], xp[:, k, :], cw(3), vc("lru_conv_b", k), ALU.mult, ALU.add))
                for t in (2, 1, 0):
                    sh = 3 - t
                    ins = STT(out=xbr[:, k, sh:S], in0=xp[:, k, 0:S - sh], scalar=cw(t), in1=xbr[:, k, sh:S],
                              op0=ALU.mult, op1=ALU.add)
                    if t:
                        own(ins)
                ins.then_inc(xbr_ready, 1)
            dve.wait_ge(a_ready, 8)
            own(V.tensor_scalar(m2, m2, -1.0, 1.0, ALU.mult, ALU.add))
            V.tensor_scalar(m2, m2, 2.0 ** -100, None, ALU.max).then_inc(m2_ready, 1)
            dve.wait_ge(xbr_ready, 8)
            own(V.tensor_tensor(gi, gi, xbr, ALU.mult))
            dve.wait_ge(mult_ready, 1)
            own(V.memset(m2[:, :, 0:1], 1.0))
            own(V.tensor_tensor(uu, m2, gi, ALU.mult))
            for k in range(8):
                own(V.tensor_tensor_scan(hs[:, k, :], av[:, k, :], uu[:, k, :], 0.0, ALU.mult, ALU.add))
                V.tensor_tensor(hy[:, k, :], hs[:, k, :], ybr[:, k, :], ALU.mult).then_inc(hy_ready, 1)
            for k in range(8):
                read(dve, u0["lru_out"] + k // 2)
                ins = STT(out=lns[:, k, :], in0=x1[:, k, :], scalar=ALPHA, in1=lo[:, k, :], op0=ALU.mult,
                          op1=ALU.add)
            ins.then_inc(ln_src, 1)
            layer_norm(0)
            ffn(0)
            layer_norm(1)
            for j in range(4):
                u = u0["v"] + j
                got(dve, u)
                V.tensor_copy(vv[:, j % 2, (j // 2) * 512:(j // 2 + 1) * 512], bank(u))\
                    .then_inc(free[u % 4], 1)
            mask = tabv("mask", 512)
            for h in range(NH + 1):
                if h < NH:
                    b = h % 2
                    dve.wait_ge(at_ln, h + 1)
                    if h >= 2:
                        got(dve, att_u["b", h - 2])
                    own(STT(out=zl[:, b, :], in0=zs[:, b, :], scalar=0.0, in1=ze[:, b, :],
                            op0=ALU.max, op1=ALU.add))
                    STT(out=zl[:, b, :], in0=zl[:, b, :], scalar=-1.0, in1=mask, op0=ALU.mult, op1=ALU.mult)\
                        .then_inc(at_l, 1)
                if h >= 1:
                    b = (h - 1) % 2
                    dve.wait_ge(at_w0, h)
                    V.tensor_tensor(zw[:, b, :], zw[:, b, :], mask, ALU.mult).then_inc(at_w, 1)
                if h < NH:
                    b = h % 2
                    u = att_u["b", h]
                    got(dve, u)
                    if h >= 2:
                        got(dve, att_u["c", h - 2])
                    ins = V.tensor_tensor(zw[:, b, :], bank(u), zs[:, b, :], ALU.add)
                    ins.then_inc(free[u % 4], 1)
                    read(dve, u)
                    V.tensor_scalar(zw[:, b, :], zw[:, b, :], 0.0, None, ALU.min).then_inc(at_e, 1)
            residual([u0["attn_out"] + j for j in range(4)], 2)
            layer_norm(2)
            ffn(1)
            layer_norm(3)
            dve.wait_ge(mod_out, 13)
            for q in range(4):
                l, w = q // 2, q % 2
                gain = vc(("norm_mix_g", "norm_ffn_g")[w], 8 * l, 8).unsqueeze(2).to_broadcast([P, 8, 2])
                own(V.tensor_scalar(gsv[:, q, :, :], modv[:, l, 24 * w + 8:24 * w + 16, :], 1.0, None, ALU.add))
                ins = V.tensor_tensor(gsv[:, q, :, :], gsv[:, q, :, :], gain, ALU.mult)
                own(ins)
            dve.sem_inc(gs_ready, 1)
            norm(0, lambda k, v: gsv[:, 0, k, v:v + 1])
            own(V.memset(flat(S2)[:, 0:4 * 2 * (S + 2 * PADC)], 0.0))
            for m in range(4):
                u = u0["in_ab"] + 8 + m
                got(dve, u)
                read(dve, u0["in_ab"] + 4 + m)
                ins = V.tensor_tensor(U[:, m, :, PADC:PADC + S], pair(u),
                                      S1[:, 4 + m, :].rearrange("p (a n) -> p a n", a=2), ALU.mult)
                ins.then_inc(free[u % 4], 1)
            read(dve, u)
            last = {}
            for t in range(CONV):
                for m in range(4):
                    y = S3[:, m, :].rearrange("p (a n) -> p a n", a=2)
                    w = vc("conv_w", 4 * t + m)
                    if t == 0:
                        ins = V.tensor_scalar(y, U[:, m, :, 0:S], w, vc("conv_b", m), ALU.mult, ALU.add)
                    else:
                        own.wait(last[m])
                        ins = STT(out=y, in0=U[:, m, :, t:t + S], scalar=w, in1=y, op0=ALU.mult, op1=ALU.add)
                    last[m] = own.mark(ins)
            for m in range(4):
                own.wait(last[m])
            dve.sem_inc(yc_ready, 1)
            dve.wait_ge(n_std, 2)
            own(V.reciprocal(std[:, 1, :], std[:, 0, :]))
            for m in range(4):
                STT(out=S3[:, m, :], in0=S3[:, m, :], scalar=vc("conv_norm_g", m), in1=std[:, 1, :],
                    op0=ALU.mult, op1=ALU.mult).then_inc(yn_ready, 1)
            for k in range(KT):
                u = u0["out_ab"] + k
                got(dve, u)
                add_gated(u, k, 0, 2, N2).then_inc(free[u % 4], 1)
            norm(2, lambda k, v: gsv[:, 1, k, v:v + 1])
            route(0)
            experts(0)
            combine(0)
            norm(3, lambda k, v: gsv[:, 2, k, v:v + 1])
            read(dve, u0["ss"] + 3)
            own(V.reciprocal(cdr, cdr))
            own(STT(out=part(S1, 0, 1024), in0=part(S1, 0, 1024), scalar=vc("q_g"), in1=part(H, 2048, 1024),
                    op0=ALU.mult, op1=ALU.mult))
            STT(out=part(S1, 1024, 1024), in0=part(S1, 1024, 1024), scalar=vc("k_g"), in1=part(H, 3072, 1024),
                op0=ALU.mult, op1=ALU.mult).then_inc(cd_qk, 1)
            read(dve, u0["ss"] + 5)
            own(V.reciprocal(std[:, 0, 0:S], std[:, 0, 0:S]))
            own(V.reciprocal(std[:, 1, :], std[:, 1, :]))
            for k in range(3):
                ins = STT(out=cq[:, k, :], in0=cq[:, k, :], scalar=vc("cq_g", k), in1=std[:, 0, 0:S],
                          op0=ALU.mult, op1=ALU.mult)
            ins.then_inc(cd_n, 1)
            for k in range(2):
                ins = STT(out=ckv[:, k, :], in0=ckv[:, k, :], scalar=vc("ckv_g", k), in1=std[:, 1, :],
                          op0=ALU.mult, op1=ALU.mult)
            ins.then_inc(cd_n, 1)
            u = u0["rope_c"]
            dve.wait_ge(cd_qk, 1)
            for j in range(3):
                got(dve, u + j)
                x_ = part(S1, 512 * j, 2, S) if j < 2 else qk[:, 2:4, 0:S]
                t1 = rtmp[:, j, :].rearrange("p (a n) -> p a n", a=2)
                cos = tabv("cos_c", S).unsqueeze(1).to_broadcast([P, 2, S])
                sin = tabv("sin_c", S).unsqueeze(1).to_broadcast([P, 2, S])
                ins = V.tensor_tensor(t1, pair(u + j), sin, ALU.mult)
                ins.then_inc(free[(u + j) % 4], 1)
                read(dve, u + j)
                own(V.tensor_tensor(x_, x_, cos, ALU.mult))
                ins = V.tensor_tensor(x_, x_, t1, ALU.add)
                if j < 2:
                    own(ins)
            ins.then_inc(cd_rot, 1)
            u = u0["rope_d"]
            for j in range(3):
                got(dve, u + j)
                w = 2 if j < 2 else 1
                x_ = (part(S2, 2560 + 512 * j, 2, S) if j < 2 else part(S2, 1024, 1, S))[0:64]
                t1 = rtmp[0:64, 3, 0:w * S].rearrange("p (a n) -> p a n", a=w)
                cos = tabv("cos_d", S, rows=64).unsqueeze(1).to_broadcast([64, w, S])
                sin = tabv("sin_d", S, rows=64).unsqueeze(1).to_broadcast([64, w, S])
                ins = V.tensor_tensor(t1, bank(u + j, w * S)[0:64, :].rearrange("p (a n) -> p a n", a=w), sin,
                                      ALU.mult)
                ins.then_inc(free[(u + j) % 4], 1)
                read(dve, u + j)
                own(V.tensor_tensor(x_, x_, cos, ALU.mult))
                ins = V.tensor_tensor(x_, x_, t1, ALU.add)
                if j < 2:
                    own(ins)
            ins.then_inc(cd_rot, 1)
            for n in range(16 + 1):
                if n < 16:
                    scale = float(P) ** -0.5 if n // 2 < 4 else 192.0 ** -0.5
                    got(dve, so_u["a", n])
                    own(V.reduce_max(rt[:, 128 + n:129 + n], bank(so_u["a", n]), AX.X))
                    V.tensor_scalar(rt[:, 2 * n:2 * n + 1], rt[:, 128 + n:129 + n], -scale, None, ALU.mult)\
                        .then_inc(so_m, 1)
                if n >= 1:
                    i = n - 1
                    read(dve, so_u["a", i])
                    own(V.reciprocal(rt[:, 64 + 2 * i:65 + 2 * i], rt[:, 64 + 2 * i:65 + 2 * i]))
                    V.tensor_scalar(pp[:, i % 2, :], pp[:, i % 2, :], rt[:, 64 + 2 * i:65 + 2 * i], None,
                                    ALU.mult).then_inc(so_n, 1)
                    got(dve, so_u["b", i])
                    if i >= 2:
                        got(dve, so_u["c", i - 2])
                    V.tensor_copy(pt[:, i % 2, :], bank(so_u["b", i]))\
                        .then_inc(free[so_u["b", i] % 4], 1)
            for j in range(4):
                u = u0["out_cd"] + j
                got(dve, u)
                for h in range(2):
                    ins = add_gated(u, 2 * j + h, 1, 2, S, h)
                ins.then_inc(free[u % 4], 1)
            norm(4, lambda k, v: gsv[:, 3, k, v:v + 1], n=S)
            route(1)
            experts(1)
            combine(1)
            norm(5, lambda k, v: vc("final_g", k), n=S)

        @block.gpsimd
        def _(pool):
            own = Chain(pool, pool_own)
            for j, (dst_, src) in enumerate([
                (x1, a["xT"].rearrange("(k p) n -> p k n", p=P)),
                (X[:, :, S:N2], a["ctxT"].rearrange("(k p) n -> p k n", p=P)),
                (vec[:, :], a["vec"]), (tab[:, :], a["tab"]),
                (rw[:, 0], a["router_w"][0].rearrange("(k p) n -> p k n", p=P)),
                (rw[:, 1], a["router_w"][1].rearrange("(k p) n -> p k n", p=P)),
                (rb[:, 0], a["router_b"][0:1]), (rb[:, 1], a["router_b"][1:2]),
            ]):
                pool.dma_start(dst_, src).then_inc(s_const, 16)
            own(pool.memset(zi[:, :], 0))
            for l in range(2):
                pool.dma_start(row_tok[l].rearrange("(p b) o -> p (b o)", p=P), zi[:, 0:NBLK[l]])\
                    .then_inc(r["zeroed"], 16)
            own(pool.iota(tok[:, :], pattern=[[P, 4]], base=0, channel_multiplier=1))

            pool.wait_ge(s_zero, 1)
            pool.wait_ge(x_ready, 8)
            zv = zb[:, :].bitcast(F32)
            y_init = y_rows.rearrange("(q p b) (a n) -> q p (b a) n", q=4, p=P, n=CH // 2)
            for q in range(4):
                pool.dma_start(y_init[q], zv.unsqueeze(1).to_broadcast([P, y_init.shape[2], CH // 2]))\
                    .then_inc(r["zeroed"], 16)

            def moe(l):
                tt = TT[l]
                for j in (2, 1):
                    read(pool, u0[f"rows{l}"] + 2 * tt - j)
                pool.dma_start(h_rows[l].rearrange("(t p) n -> p t n", p=P), hrow[:, 0:tt, :])\
                    .then_inc(r["rows_st"], 16)
                pool.wait_ge(r["zeroed"], 16 * 6)
                pool.wait_ge(r["dest"], l + 1)
                for t in range(tt):
                    for k in range(2):
                        pool.indirect_dma_start(row_tok[l], bass.IndirectOffsetOnAxis(ap=dst[:, t, k:k + 1], axis=0),
                                                tok[:, t:t + 1], None).then_inc(r["scat"], 16)
                pool.wait_ge(r["scat"], 128 + 64 * l)
                pool.wait_ge(r["rows_st"], 16 * (l + 1))
                pool.wait_ge(r["planned"], l + 1)
                t0, t1 = turns(pool, l)
                with pool.Fori(t0, t1) as i:
                    at = turn_of_layer(i, t0, l)
                    for s in range(2):
                        pool.wait_ge(r["tr"], 2 * i + (s + 1))
                        pool.dma_start(ix[:, s:s + 1], row_tok[l][ds(at * (2 * B) + s * B, B), :]).then_inc(r["ixl"][s], 16)
                        pool.wait_ge(r["ixl"][s], 16 * i + 16)
                        pool.sem_inc(r["gathers"], 1)
                        pool.indirect_dma_start(xg[:, s, :], None, h_rows[l],
                                                bass.IndirectOffsetOnAxis(ap=ix[:, s:s + 1], axis=0))\
                            .then_inc(r["xg"][s], 16)
                pool.wait_ge(r["y_all"], l + 1)
                g = [part(S1, 0, 4, D), part(S2, 0, 4, D)]
                for t in range(tt):
                    for k in range(2):
                        pool.indirect_dma_start(g[k][:, t, :], None, y_rows,
                                                bass.IndirectOffsetOnAxis(ap=dst[:, t, k:k + 1], axis=0))\
                            .then_inc(r["cg"][t], 16)

            moe(0)
            moe(1)
            pool.wait_ge(n_nrm, 8 * 5)
            src = H[:, :, 0:S]
            pool.dma_start(a["out"].rearrange("(k p) n -> p k n", p=P), src).then_inc(s_out, 16)
            pool.wait_ge(s_out, 16)


def kernel(**inputs):
    import numpy as _np
    import concourse.bacc as _bacc
    from concourse import mybir as _mybir
    from concourse.bass_utils import run_bass_kernel_spmd as _run

    g = {k: _np.ascontiguousarray(v) for k, v in inputs.items()}

    def tiles(v):
        return v.reshape(-1, 128).T

    vec = _np.concatenate([tiles(v) for v in (
        g["lru_b_in"], g["lru_conv_w"], g["lru_conv_b"],
        g["lru_b_gates"].reshape(8, 2, 128).transpose(1, 0, 2), g["lru_a_param"], g["lru_b_out"],
        g["ffn_conv_w"], g["ffn_conv_b"], g["ln_g"], g["ln_b"], g["c_2"], g["c_ctx_2"], g["mod_b_2"],
        g["norm_mix_g_2"], g["norm_ffn_g_2"], g["conv_w_2"], g["conv_b_2"], g["conv_norm_g_2"],
        g["q_norm_g_2"], g["k_norm_g_2"], g["cq_norm_g_2"], g["ckv_norm_g_2"], g["final_norm_g_2"])], 1)
    arrays = {
        "xT": g["x"][0].T, "ctxT": g["ctx_2"][0].T, "vec": vec, "tab": tables(),
        "router_w": _np.concatenate([g["router_grp_w_2"], g["router_exp_w_2"]], 2),
        "router_b": _np.concatenate([g["router_grp_b_2"], g["router_exp_b_2"]], 1),
        "lru_w_in": g["lru_w_in"][0], "lru_w_gates": g["lru_w_gates"][0], "lru_w_out": g["lru_w_out"][0],
        "kv_w": g["kv_w"], "attn_w_q": g["attn_w_q"][0], "attn_w_out": g["attn_w_out"][0],
        "ffn_w_up": g["ffn_w_up"], "ffn_w_down": g["ffn_w_down"], "mod_w": g["mod_w_2"],
        "w_in_ab": g["w_in_ab_2"][0], "w_out_ab": g["w_out_ab_2"][0], "w_in_cd": g["w_in_cd_2"][0],
        "w_uq": g["w_uq_2"][0], "w_ukv": g["w_ukv_2"][0], "w_out_cd": g["w_out_cd_2"][0],
        "exp_w_gate": g["exp_w_gate_2"], "exp_w_up": g["exp_w_up_2"], "exp_w_down": g["exp_w_down_2"],
    }
    arrays = {k: _np.ascontiguousarray(v) for k, v in arrays.items()}
    nc = _bacc.Bacc("TRN2", target_bir_lowering=False, num_devices=1)
    aps = {k: nc.dram_tensor("in_" + k, v.shape, _mybir.dt.from_np(v.dtype), kind="ExternalInput").ap()
           for k, v in arrays.items()}
    aps["out"] = nc.dram_tensor("out", (1024, 256), _mybir.dt.float32, kind="ExternalOutput").ap()
    build(nc, aps)
    r = _run(nc, [{"in_" + k: v for k, v in arrays.items()}], core_ids=[0])
    return _np.ascontiguousarray(r.results[0]["out"].T)[None]
```

```python
from contextlib import ExitStack

import numpy as np

import concourse.bass as bass
from concourse import mybir

ALU = mybir.AluOpType
ACT = mybir.ActivationFunctionType
AX = mybir.AxisListType
F32 = mybir.dt.float32
BF16 = mybir.dt.bfloat16
I32 = mybir.dt.int32
ds = bass.ds

P = 128
D = 1024
KT = D // P
S = 256
N2 = 2 * S
NH = 8
FF = 3 * D
FT = FF // P
CH = 512
NJ = FF // CH
MJ = CH // P
SLOTS = 6
MSLOTS = 6
ALPHA = (2 * 2) ** 0.25
LN_EPS = 1e-5
RMS_EPS = 1e-6
NMOD = 6
NE = 32
NG = 4
EFF = 512
B = 64
NTOK = [2 * S, S]
NBLK = [2 * (((2 * n + NE * B) // B + 1) // 2) for n in NTOK]
CONV = 31
PADC = CONV // 2
GRID_W = 64

VEC = {}
_at = 0
for _name, _cols in [
    ("lru_b_in", 16), ("lru_conv_w", 4 * 8), ("lru_conv_b", 8), ("lru_b_gates", 16), ("lru_a", 8),
    ("lru_b_out", 8), ("ffn_conv_w", 2 * 3 * 48), ("ffn_conv_b", 2 * 48), ("ln_g", 4 * 8),
    ("ln_b", 4 * 8), ("c", 16), ("mod_b", 2 * 48), ("norm_mix_g", 16), ("norm_ffn_g", 16),
    ("conv_w", CONV * 4), ("conv_b", 4), ("conv_norm_g", 4), ("q_g", 1), ("k_g", 1), ("cq_g", 3),
    ("ckv_g", 2), ("final_g", 8),
]:
    VEC[_name] = _at
    _at += _cols
NVEC = _at

TAB = {}
_at = 0
for _name, _cols in [
    ("ident", 128), ("suffix", 128), ("before", 128), ("ones", 128), ("swap", 128), ("dft_d", 256),
    ("cos_l", 512), ("sin_l", 512), ("cos_c", 256), ("sin_c", 256), ("cos_d", 256), ("sin_d", 256),
    ("mask", 512), ("iota", 128), ("thresh", 8),
]:
    TAB[_name] = _at
    _at += _cols
NTAB = _at


def tables():
    t = np.zeros((P, NTAB), np.float32)
    p = np.arange(P)
    put = lambda name, a: t.__setitem__((slice(0, a.shape[0]), slice(TAB[name], TAB[name] + a.shape[1])), a)
    put("ident", np.eye(P))
    put("suffix", (p[:, None] >= p[None, :]).astype(np.float64))
    put("before", (p[:, None] < p[None, :]).astype(np.float64))
    put("ones", np.ones((P, P)))
    put("swap", (p[:, None] == (p[None, :] ^ 1)).astype(np.float64))
    ang = 2 * np.pi * np.outer(p, p) / P
    put("dft_d", np.concatenate([np.cos(ang), np.sin(ang)], 1) / np.sqrt(S * P))
    l = np.arange(S)
    ang = 2 * np.pi * (np.outer(l, l) % S) / S
    both = lambda a: a.reshape(2, P, S).transpose(1, 0, 2).reshape(P, 2 * S)
    put("cos_l", both(np.cos(ang)))
    put("sin_l", both(-np.sin(ang)))
    row, col = (l // GRID_W).astype(np.float32), (l % GRID_W).astype(np.float32)
    for name, dim in (("c", 128), ("d", 64)):
        nf = dim // 4
        inv = (np.float32(10000.0) ** (-np.arange(nf, dtype=np.float32) / np.float32(nf))).astype(np.float32)
        a = np.concatenate([inv[:, None] * row[None], inv[:, None] * col[None]], 0).astype(np.float64)
        cos, sin = np.repeat(np.cos(a), 2, 0), np.repeat(np.sin(a), 2, 0)
        sin[0::2] *= -1
        put("cos_" + name, cos)
        put("sin_" + name, sin)
    k = np.arange(S).reshape(2, P).T
    put("mask", (k[:, :, None] < l[None, None, :]).astype(np.float64).reshape(P, 2 * S))
    put("iota", np.tile(p, (P, 1)).astype(np.float64))
    put("thresh", np.tile(np.arange(8) * B, (P, 1)).astype(np.float64))
    return t


class Chain:

    def __init__(self, eng, sem):
        self.eng, self.sem, self.n, self.turn, self.per, self.start = eng, sem, 0, None, 0, 0

    def mark(self, ins):
        self.n += 1
        ins.then_inc(self.sem, 1)
        return self.n

    def wait(self, n):
        if self.turn is None:
            self.eng.wait_ge(self.sem, n)
        else:
            self.eng.wait_ge(self.sem, self.turn * self.per + n)

    def __call__(self, ins):
        self.wait(self.mark(ins))

    def loop(self, turn, per):
        self.turn, self.per, self.start = turn, per, self.n

    def end_loop(self, turns=None):
        assert self.n - self.start == self.per, (self.n - self.start, self.per)
        self.turn = None
        if turns is not None:
            self.n = self.start + self.per * turns


def build(nc, a):
    ctx = ExitStack()
    with ctx:
        def sb(name, shape, dt=F32):
            return ctx.enter_context(nc.sbuf_tensor(name, shape, dt))

        def sem(name):
            return ctx.enter_context(nc.semaphore(name))

        def sems(name, n):
            return [sem(f"{name}{i}") for i in range(n)]

        ring = sb("ring", [P, MSLOTS, KT * CH])
        X = sb("X", [P, KT, N2])
        H = sb("H", [P, KT, N2])
        S1 = sb("S1", [P, KT, N2])
        S2 = sb("S2", [P, KT, N2])
        S3 = sb("S3", [P, KT, N2])
        vec = sb("vec", [P, NVEC])
        tab = sb("tab", [P, NTAB])
        std = sb("std", [P, 2, N2])
        modv = sb("modv", [P, 2, 48, 2])
        gsv = sb("gsv", [P, 4, KT, 2])
        cs = sb("cs", [P, 16])
        sp = sb("sp", [P, 8, 8])
        rw = sb("rw", [P, 2, KT, 36])
        rb = sb("rb", [1, 2, 36])
        zb = sb("zb", [P, CH], BF16)
        rt = sb("rt", [P, 1024])
        dst = sb("dst", [P, 4, 2], I32)
        plan = sb("plan", [1, 2, 64], I32)
        T = ctx.enter_context(nc.psum_tensor("T", [P, 8, 512], F32))

        def tabv(name, n, off=0, rows=P):
            return tab[0:rows, TAB[name] + off:TAB[name] + off + n]

        def vc(name, i=0, n=1):
            return vec[:, VEC[name] + i:VEC[name] + i + n]

        ident, ones = tabv("ident", P), tabv("ones", P)

        def flat(t):
            return t[:, :, :].rearrange("p a n -> p (a n)")

        def part(t, off, *dims):
            n = int(np.prod(dims))
            v = flat(t)[:, off:off + n]
            if len(dims) == 2:
                return v.rearrange("p (a b) -> p a b", a=dims[0])
            if len(dims) == 3:
                return v.rearrange("p (a b c) -> p a b c", a=dims[0], b=dims[1])
            return v

        x1 = X[:, :, 0:S]

        y_rows = nc.dram_tensor("y_rows", (max(NBLK) * B, D), F32, kind="Internal").ap()

        def cols(w, n0, n):
            return w[:, n0:n0 + n].rearrange("(k p) n -> p k n", p=P)

        chunks, c0 = [], {}
        slot_of, nth, prev, _users = [], [], [], {}

        def add(name, sources, slots):
            c0[name] = len(chunks)
            for src, s_ in zip(sources, slots, strict=True):
                c = len(chunks)
                chunks.append(src)
                slot_of.append(s_)
                users = _users.setdefault(s_, [])
                prev.append(users[-1] if users else None)
                users.append(c)
                nth.append(len(users))

        def ffn_slots(a0, a1):
            return [x for j in range(NJ) for x in ((a0, a1)[j % 2], (a0, a1)[j % 2] + 1, 4, 4, 5)]

        add("lru_in", [cols(a["lru_w_in"], CH * i, CH) for i in range(4)], (0, 1, 2, 3))
        add("gates", [a["lru_w_gates"].rearrange("n p g -> p n g")], (4,))
        add("lru_out", [cols(a["lru_w_out"], CH * i, CH) for i in range(2)], (5, 3))
        add("ffn0", [None] * 5 * NJ, ffn_slots(0, 2))
        add("kv", [cols(a["kv_w"], CH * i, CH) for i in range(4)], (0, 1, 2, 3))
        add("q", [cols(a["attn_w_q"], CH * i, CH) for i in range(2)], (4, 5))
        add("attn_out", [cols(a["attn_w_out"], CH * i, CH) for i in range(2)], (0, 1))
        add("ffn1", [None] * 5 * NJ, ffn_slots(2, 0))
        add("in_ab", [cols(a["w_in_ab"], CH * i, CH) for i in (2, 1, 0)], (2, 3, 4))
        add("out_ab", [cols(a["w_out_ab"], CH * i, CH) for i in range(2)], (0, 1))
        add("in_cd", [cols(a["w_in_cd"], CH * i, min(CH, 1728 - CH * i)) for i in range(4)], (0, 1, 2, 3))
        add("uq", [a["w_uq"].rearrange("(k p) n -> p k n", p=P)], (4,))
        add("ukv", [a["w_ukv"].rearrange("(k p) n -> p k n", p=P)], (5,))
        add("out_cd", [cols(a["w_out_cd"], CH * i, CH) for i in range(2)], (0, 1))
        before_moe = [c0["in_cd"], len(chunks)]

        def slot(c, k=KT, n=CH):
            return ring[:, slot_of[c], 0:k * n].rearrange("p (k n) -> p k n", k=k)

        def mslot(s, k=KT, n=CH):
            return ring[:, s, 0:k * n].rearrange("p (k n) -> p k n", k=k)

        w_landed = sems("w_landed", SLOTS)

        full, free = sems("bank_full", 4), sems("bank_free", 4)
        u0, n_units = {}, 0
        for name, n in [("lru_in", 8), ("gates", 8), ("lru_out", 4), ("k", 4), ("v", 4), ("q", 4),
                        ("att", 3 * NH), ("attn_out", 4), ("in_ab", 12), ("dft1", 8), ("dft2", 4), ("out_ab", 8),
                        ("rows0", 8), ("logit0", 1), ("rank0", 2), ("comb0", 8),
                        ("in_cd", 11), ("ss", 6), ("uq", 4), ("ukv", 8), ("rope_c", 3), ("rope_d", 3),
                        ("soft", 48), ("out_cd", 4),
                        ("rows1", 4), ("logit1", 1), ("rank1", 2), ("comb1", 4)]:
            u0[name] = n_units
            n_units += n

        def bank(u, n=2 * S):
            return T[:, u % 4, 0:n]

        def pair(u):
            return T[:, u % 4, :].rearrange("p (a n) -> p a n", a=2)

        def take(pe, u):
            if u >= 4:
                pe.wait_ge(free[u % 4], u // 4)

        def got(eng, u):
            eng.wait_ge(full[u % 4], u // 4 + 1)

        def read(eng, u):
            eng.wait_ge(free[u % 4], u // 4 + 1)

        last_unit = {}
        last_unit.update({
            c0["lru_in"] + j: u0["lru_in"] + 2 * j + 1 for j in range(4)})
        last_unit.update({c0["gates"]: u0["gates"] + 7})
        last_unit.update({c0["lru_out"] + j: u0["lru_out"] + 2 * j + 1 for j in range(2)})
        last_unit.update({c0["kv"] + j: (u0["k"] + 2 * j + 1 if j < 2 else u0["v"] + 2 * j - 3) for j in range(4)})
        last_unit.update({c0["q"] + j: u0["q"] + 2 * j + 1 for j in range(2)})
        last_unit.update({c0["attn_out"] + j: u0["attn_out"] + 2 * j + 1 for j in range(2)})
        last_unit.update({c0["in_ab"] + j: u0["in_ab"] + 4 * j + 3 for j in range(3)})
        last_unit.update({c0["out_ab"] + j: u0["out_ab"] + 4 * j + 3 for j in range(2)})
        last_unit.update({c0["in_cd"] + j: u0["in_cd"] + (1, 5, 8, 10)[j] for j in range(4)})
        last_unit.update({c0["uq"]: u0["uq"] + 3, c0["ukv"]: u0["ukv"] + 7})
        last_unit.update({c0["out_cd"] + j: u0["out_cd"] + 2 * j + 1 for j in range(2)})

        def pipelined(n, base):
            order = [("a", 0), ("a", 1)]
            for i in range(n):
                order.append(("b", i))
                if i >= 1:
                    order.append(("c", i - 1))
                if i + 2 < n:
                    order.append(("a", i + 2))
            order.append(("c", n - 1))
            return order, {key: base + j for j, key in enumerate(order)}

        s_const, s_tab, s_late, s_zero = sem("s_const"), sem("s_tab"), sem("s_late"), sem("s_zero")
        s_cs = sem("s_cs")
        s_sp = sem("s_sp")
        xbr_ready, a_ready = sem("xbr_ready"), sem("a_ready")
        m2_ready, mult_ready, hy_ready = sem("m2_ready"), sem("mult_ready"), sem("hy_ready")
        ln_src, ln_mean, ln_xc, ln_sq, ln_var = sem("ln_src"), sem("ln_mean"), sem("ln_xc"), sem("ln_sq"), sem("ln_var")
        ln_std, ln_nrm, x_ready = sem("ln_std"), sem("ln_nrm"), sem("x_ready")
        f_full, f_id, f_conv, f_gelu = sem("f_full"), sem("f_id"), sem("f_conv"), sem("f_gelu")
        g_ready, g_used, acc_ready = sem("g_ready"), sem("g_used"), sem("acc_ready")
        mod_acc_ready, mod_sum, mod_out = sem("mod_acc_ready"), sem("mod_sum"), sem("mod_out")
        mod_row, mod_turned = sem("mod_row"), sem("mod_turned")
        at_ln, at_l, at_e, at_w0, at_w = sem("at_ln"), sem("at_l"), sem("at_e"), sem("at_w0"), sem("at_w")
        gs_ready = sem("gs_ready")
        n_sq, n_ms, n_std, n_nrm, h_ready = sem("n_sq"), sem("n_ms"), sem("n_std"), sem("n_nrm"), sem("h_ready")
        ln_rs, ln_bc, n_rs, n_bc = sem("ln_rs"), sem("ln_bc"), sem("n_rs"), sem("n_bc")
        cv_ready, cv_used = sem("cv_ready"), sem("cv_used")
        yc_ready, yn_ready, yb_ready = sem("yc_ready"), sem("yn_ready"), sem("yb_ready")
        act_own, dve_own, pool_own = sem("act_own"), sem("dve_own"), sem("pool_own")
        s_out = sem("s_out")
        r = {k: sem(k) for k in (
            "ge", "gx", "m_ready", "dest", "planned", "zeroed", "m_full", "sg", "hm", "hT_full", "hT", "xT", "tr",
            "y_full", "m_act", "oh", "oh_own", "xT_all", "y_all", "cb")}
        for k, n in (("landed", MSLOTS), ("y_st", 2), ("cg", 4)):
            r[k] = sems(k, n)
        cd_sq, cd_qk, cd_n, cd_rot = sem("cd_sq"), sem("cd_qk"), sem("cd_n"), sem("cd_rot")
        so_m, so_n = sem("so_m"), sem("so_n")
        block = ctx.enter_context(nc.Block())

        N_CONST, N_LATE = 2, 5
        att_order, att_u = pipelined(NH, u0["att"])
        so_order, so_u = pipelined(16, u0["soft"])

        def turns(eng, l):
            n = [eng.value_load(plan[0:1, j, 0:1], min_val=1, max_val=NBLK[j] // 2) for j in range(l + 1)]
            return (0, n[0]) if l == 0 else (n[0], n[0] + n[1])

        def turn_of_layer(i, t0, l):
            return i if l == 0 else nc.s_assert_within(i - t0, 0, NBLK[l] // 2 - 1, skip_runtime_bounds_check_because=
                                                       "the loop runs from t0 over at most that many turns")

        ybr, xp, xbr, gi, gr, av = (part(S1, 0, 8, S), part(S1, 2048, 8, S), part(S2, 0, 8, S),
                                    part(S2, 2048, 8, S), part(S3, 0, 8, S), part(S3, 2048, 8, S))
        m2, uu, hs = part(H, 0, 8, S), part(H, 2048, 8, S), part(S1, 2048, 8, S)
        hy, lo = part(S3, 0, 8, S), part(S2, 2048, 8, S)
        lns, lxc, lsq = part(H, 0, 8, S), part(S3, 2048, 8, S), part(S3, 0, 8, S)
        hab, gT = part(S1, 0, 2, 2, S), part(S1, 1024, 2, S)
        macc, mrow = part(S1, 1536, 2, 2, CH), part(S1, 3584, CH)
        kT, vv, qT, oT = part(S1, 0, 8, S), part(S1, 2048, 2, D), part(S2, 0, 8, S), part(S2, 2048, 8, S)
        zs, ze, zl, zw = part(S3, 0, 2, 512), part(S3, 1024, 2, 512), part(S3, 2048, 2, 512), part(S3, 3072, 2, 512)
        U = part(S2, 0, 4, 2, S + 2 * PADC)
        fa = part(H, 0, 4, 4, 256)
        hrow = part(S2, 0, 4, D)
        yb = part(S3, 1024, 2, 512)
        xgT, sg, hm, hT = part(S1, 0, 8, P), part(S1, 1024, 2, 256), part(S1, 1536, 2, 256), part(S1, 2048, 2, 256)
        onehot = part(S1, 2560, 4, P)
        qk, vC, cq = part(S1, 0, 4, 512), part(S1, 2048, 4, 256), part(S1, 3072, 3, S)
        ckv, kr, qn, qr = part(S2, 0, 2, 512), part(S2, 1024, 512), part(S2, 1536, 4, S), part(S2, 2560, 4, S)
        cdsq, cdr = part(S3, 0, 4, 512), part(H, 2048, 4, 512)
        kn, vD = part(S3, 0, 4, 512), part(S3, 2048, 4, 512)
        rtmp = part(H, 0, 4, 512)
        pp, pt, oo = part(H, 0, 2, 512), part(H, 1024, 2, 512), part(H, 2048, 8, S)

        def kt8(t, k, n=S):
            return t[:, k, 0:n]

        TT = [NTOK[l] // P for l in range(2)]

        nsq0 = [0, 4, 6, 10, 14, 18]
        ACT_F = ACT.Identity

        @block.sync
        def _(sp_):
            def released(c, i=0):
                for l in range(2):
                    j = c - c0[f"ffn{l}"]
                    if 0 <= j < 5 * NJ:
                        t = j // 5
                        if j % 5 < 2:
                            sp_.wait_ge(f_full, i * 8 + (24 * l + 4 * t + 4))
                        elif j % 5 < 4:
                            sp_.wait_ge(mod_acc_ready, i * 4 + (2 * NJ * l + 2 * t + j % 5 - 1))
                        else:
                            sp_.wait_ge(g_used, i * 8 + (24 * l + 4 * t + 6))
                        return
                u = last_unit[c]
                sp_.wait_ge(full[u % 4], u // 4 + 1)

            def static(c):
                if prev[c] is not None:
                    released(prev[c])
                src = chunks[c]
                k, n = src.shape[1], src.shape[2]
                sp_.dma_start(slot(c, k, n), src).then_inc(w_landed[slot_of[c]], 16)

            def ffn(l):
                base = c0[f"ffn{l}"]
                up, down, mw = a["ffn_w_up"][l], a["ffn_w_down"][l], a["mod_w"][l]
                up = up.rearrange("(k p) n -> p k n", p=P)
                mw = mw.rearrange("(k p) n -> p k n", p=P)
                down = down.rearrange("(f p) n -> p f n", p=P)

                def load(i, p, j, peeled=False):
                    src = (up[:, :, ds(i * (2 * CH) + p * CH, CH)], up[:, :, ds(i * (2 * CH) + (p * CH + FF), CH)],
                           mw[:, :, ds(i * (4 * CH) + 2 * p * CH, CH)], mw[:, :, ds(i * (4 * CH) + (2 * p + 1) * CH, CH)],
                           down[:, ds(i * (2 * MJ) + p * MJ, MJ), :])[j]
                    c = base + 5 * p + j
                    if peeled:
                        released(prev[c])
                    else:
                        released(prev[c + 10], i - 1)
                    sp_.dma_start(slot(c, src.shape[1], src.shape[2]), src).then_inc(w_landed[slot_of[c]], 16)

                def pair_of_turns(i, peeled=False):
                    load(i, 0, 0, peeled)
                    if not peeled:
                        load(i - 1, 1, 3)
                    for p, j in ((0, 1), (0, 2), (0, 4), (1, 0), (0, 3), (1, 1), (1, 2), (1, 4)):
                        load(i, p, j, peeled)

                pair_of_turns(0, peeled=True)
                with sp_.Fori(1, NJ // 2) as i:
                    pair_of_turns(i)
                load(NJ // 2 - 1, 1, 3)

            def moe(l):
                for u in _users.values():
                    released(max(c for c in u if c < before_moe[l]))
                weights = (a["exp_w_gate"], a["exp_w_up"], a["exp_w_down"])

                def load(m, w):
                    src = w.rearrange("e (k p) n -> p (e k) n", p=P)
                    sp_.dma_start(mslot(m, src.shape[1], src.shape[2]), src).then_inc(r["landed"][m], 16)

                for j in range(3):
                    load(j, weights[j][l][0:1])
                sp_.wait_ge(r["planned"], l + 1)
                t0, t1 = turns(sp_, l)

                def expert(i, at, s):
                    e = sp_.value_load(plan[0:1, l, ds(at * 2 + (1 + s), 1)], min_val=0, max_val=NE - 1)
                    for j, w in enumerate(weights):
                        if j < 2:
                            sp_.wait_ge(r["m_full"], 2 * i + (s + 1))
                        else:
                            sp_.wait_ge(r["y_full"], 2 * i + (s + 1))
                        load(3 * s + j, w[l][ds(e, 1)])

                expert(t0, 0, 1)
                with sp_.Fori(t0 + 1, t1) as i:
                    at = turn_of_layer(i, t0, l)
                    for s in range(2):
                        expert(i, at, s)
                if l == 0:
                    sp_.wait_ge(r["y_full"], t1 * 2 + 2)
                    for t in range(TT[0]):
                        sp_.wait_ge(r["cg"][t], 32)

            for c in range(0, c0["ffn0"]):
                static(c)
            ffn(0)
            for c in range(c0["kv"], c0["ffn1"]): static(c)
            ffn(1)
            for c in range(c0["in_ab"], c0["in_cd"]): static(c)
            moe(0)
            for c in range(c0["in_cd"], len(chunks)): static(c)
            moe(1)
            sp_.wait_ge(s_out, 16)

        @block.tensor
        def _(pe):
            def landed(c):
                pe.wait_ge(w_landed[slot_of[c]], 16 * nth[c])

            def dense(c, n_tiles, rhs, u, width, k_tiles=KT, n=CH, m0=0, ready=None):
                w = slot(c, k_tiles, n)
                per = 512 // width
                for m in range(n_tiles):
                    if m % per == 0:
                        take(pe, u + m // per)
                    for k in range(k_tiles):
                        if m == 0 and ready is not None:
                            pe.wait_ge(ready[0], ready[1] + k + 1)
                        ins = pe.matmul(bank(u + m // per)[:, (m % per) * width:(m % per + 1) * width],
                                        w[:, k, (m0 + m) * P:(m0 + m + 1) * P], rhs(k),
                                        start=(k == 0), stop=(k == k_tiles - 1))
                    if m % per == per - 1 or m == n_tiles - 1:
                        ins.then_inc(full[(u + m // per) % 4], 1)

            def quarter_sums(x, n, start, stop):
                for q in range(4):
                    ins = pe.matmul(T[32 * q:32 * q + 32, 7, 0:n // 4], ones[:, 0:32], x[:, q * n // 4:(q + 1) * n // 4],
                                    start=start, stop=stop)
                return ins

            def spread(n):
                for q in range(4):
                    ins = pe.matmul(T[:, 6, q * n // 4:(q + 1) * n // 4], ident[:, 32 * q:32 * q + 1].to_broadcast([P, P]),
                                    std[:, 1, 0:n // 4], start=True, stop=True)
                return ins

            def layer_norm(i):
                if i == 2:
                    read(pe, u0["attn_out"] + 3)
                else:
                    pe.wait_ge(ln_src, (1, 2, None, 3)[i])
                for k in range(KT):
                    ins = pe.matmul(T[:, 6, 0:S], ones, kt8(lns, k), start=(k == 0), stop=(k == KT - 1))
                ins.then_inc(ln_mean, 1)
                for k in range(KT):
                    if k % 2 == 0:
                        pe.wait_ge(ln_sq, 4 * i + k // 2 + 1)
                    ins = quarter_sums(kt8(lsq, k), S, k == 0, k == KT - 1)
                ins.then_inc(ln_var, 1)
                pe.wait_ge(ln_rs, i + 1)
                spread(S).then_inc(ln_bc, 1)

            def ffn(l):
                base = c0[f"ffn{l}"]
                pe.wait_ge(ln_nrm, 8 * (2 * l + 1))
                for b in range(4):
                    ins = pe.matmul(T[:, 4 + b, :], zb[:, 0:P], zb[:, :], start=True, stop=False,
                                    skip_group_check=True)
                if l == 0:
                    ins.then_inc(g_used, 2)
                with pe.Fori(0, NJ // 2) as i:
                  for p in range(2):
                    ca, cb, cd = (base + 5 * p + j for j in (0, 1, 4))
                    wa, wb, wd = slot(ca), slot(cb), slot(cd, MJ, D)

                    def up(m):
                        pe.wait_ge(f_conv, i * 8 + (4 * p + 24 * l + m + 1))
                        for h, w in ((0, wa), (1, wb)):
                            for k in range(KT):
                                if p == 0 and m == 0 and h == 0:
                                    pe.wait_ge(x_ready, 16 * l + k + 1)
                                ins = pe.matmul(T[:, m % 2, h * S:(h + 1) * S], w[:, k, m * P:(m + 1) * P],
                                                x1[:, k, :], start=(k == 0), stop=(k == KT - 1))
                        ins.then_inc(f_full, 1)

                    def down(m):
                        pe.wait_ge(g_ready, i * 8 + (4 * p + 24 * l + m + 3))
                        for d in range(KT):
                            ins = pe.matmul(T[:, 4 + d // 2, (d % 2) * S:(d % 2 + 1) * S], wd[:, m, d * P:(d + 1) * P],
                                            gT[:, m % 2, :], start=False, stop=False, skip_group_check=True)
                        ins.then_inc(g_used, 1)

                    pe.wait_ge(w_landed[slot_of[ca]], i * 16 + 16 * nth[ca])
                    pe.wait_ge(w_landed[slot_of[cb]], i * 16 + 16 * nth[cb])
                    up(0)
                    up(1)
                    pe.wait_ge(w_landed[slot_of[cd]], i * 32 + 16 * nth[cd])
                    down(0)
                    up(2)
                    down(1)
                    up(3)
                    down(2)
                    pe.wait_ge(mod_acc_ready, i * 4 + (2 * p + 2 * NJ * l + 2))
                    pe.wait_ge(mod_out, i * 2 + (p + NJ * l + 1))
                    for q in range(4):
                        ins = pe.matmul(T[32 * q:32 * q + 32, 2, :], ones[:, 0:32], macc[:, q // 2, q % 2, :],
                                        start=True, stop=True)
                    ins.then_inc(mod_sum, 1)
                    down(3)
                    pe.wait_ge(mod_row, i * 2 + (p + NJ * l + 1))
                    for m in range(4):
                        ins = pe.transpose(T[:, 3, m * P:(m + 1) * P], mrow[:, m * P:(m + 1) * P], ident)
                    ins.then_inc(mod_turned, 1)
                for b in range(4):
                    ins = pe.matmul(T[:, 4 + b, :], zb[:, 0:P], zb[:, :], start=False, stop=True,
                                    skip_group_check=True)
                ins.then_inc(acc_ready, 1)

            def norm(r, k_tiles=KT, n=N2, sq=S1, off=0):
                for k in range(k_tiles):
                    if k % 2 == 0:
                        pe.wait_ge(n_sq, nsq0[r] + k // 2 + 1)
                    ins = quarter_sums(sq[:, off + k, 0:n], n, k == 0, k == k_tiles - 1)
                ins.then_inc(n_ms, 1)
                pe.wait_ge(n_rs, r + 1)
                spread(n).then_inc(n_bc, 1)

            def route(l):
                tt = TT[l]
                for t in range(tt):
                    for hf in range(2):
                        u = u0[f"rows{l}"] + 2 * t + hf
                        take(pe, u)
                        for k in range(4):
                            ins = pe.transpose(bank(u)[:, k * P:(k + 1) * P],
                                               H[:, 4 * hf + k, t * P:(t + 1) * P], ident)
                        ins.then_inc(full[u % 4], 1)
                u = u0[f"logit{l}"]
                take(pe, u)
                for t in range(tt):
                    for k in range(KT):
                        pe.matmul(bank(u)[:, t * 36:(t + 1) * 36], H[:, k, t * P:(t + 1) * P], rw[:, l, k, :],
                                  start=(k == 0), stop=False)
                    ins = pe.matmul(bank(u)[:, t * 36:(t + 1) * 36], ones[0:1, :], rb[0:1, l, :],
                                    start=False, stop=True)
                ins.then_inc(full[u % 4], 1)
                pe.wait_ge(r["m_ready"], l + 1)
                m_ = rt[:, 0:tt * NE].rearrange("p (t e) -> p t e", t=tt)
                u = u0[f"rank{l}"]
                take(pe, u)
                for t in range(tt):
                    for s in range(t + 1):
                        ins = pe.matmul(bank(u)[:, t * NE:(t + 1) * NE], tabv("before", P) if s == t else ones,
                                        m_[:, s, :], start=(s == 0), stop=(s == t))
                ins.then_inc(full[u % 4], 1)
                u += 1
                take(pe, u)
                for t in range(tt):
                    ins = pe.matmul(bank(u)[:, 0:NE], ones, m_[:, t, :], start=(t == 0), stop=(t == tt - 1))
                ins.then_inc(full[u % 4], 1)

            def experts(l):
                pe.wait_ge(r["planned"], l + 1)
                t0, t1 = turns(pe, l)
                if l == 0:
                    pe.sem_inc(r["m_full"], 2)
                    pe.sem_inc(r["y_full"], 2)

                def turn_tokens(i):
                    pe.wait_ge(r["xT"], i + (l + 1))
                    pe.wait_ge(r["oh"], i + (l + 1))
                    for k in range(KT):
                        for t in range(TT[l]):
                            ins = pe.matmul(T[:, 6 + k // 4, (k % 4) * P:(k % 4 + 1) * P],
                                            hrow[:, t, k * P:(k + 1) * P], onehot[:, t, :],
                                            start=(t == 0), stop=(t == TT[l] - 1))
                    ins.then_inc(r["tr"], 1)

                for j in range(1, 5):
                    if 2 * TT[l] >= j:
                        read(pe, u0[f"rows{l}"] + 2 * TT[l] - j)

                turn_tokens(t0)
                with pe.Fori(t0, t1) as i:
                    for s in range(2):
                        pe.wait_ge(r["landed"][3 * s], 16 * i + 16)
                        pe.wait_ge(r["landed"][3 * s + 1], 16 * i + 16)
                        pe.wait_ge(r["xT"], i + (l + 2))
                        for k in range(KT):
                            for c in range(2):
                                ins = pe.matmul(T[c * B:(c + 1) * B, s, :].rearrange("p (a n) -> p a n", a=2),
                                                xgT[:, k, s * B:(s + 1) * B],
                                                ring[:, 3 * s:3 * s + 2, k * CH + c * 256:k * CH + (c + 1) * 256],
                                                start=(k == 0), stop=(k == KT - 1))
                        ins.then_inc(r["m_full"], 1)
                        if s == 1:
                            turn_tokens(i + 1)
                        pe.wait_ge(r["hm"], 2 * i + (s + 1))
                        for j in range(2):
                            ins = pe.transpose(T[:, 2, j * P:(j + 1) * P], hm[:, s, j * P:(j + 1) * P], ident)
                        ins.then_inc(r["hT_full"], 1)
                        pe.wait_ge(r["landed"][3 * s + 2], 16 * i + 16)
                        pe.wait_ge(r["m_act"], 2 * i + (s + 1))
                        pe.wait_ge(r["hT"], 2 * i + (s + 1))
                        wd = mslot(3 * s + 2, MJ, D)
                        for f in range(MJ):
                            off = (f % 2) * P + (f // 2) * B
                            for n in range(2):
                                ins = pe.matmul(T[n * B:(n + 1) * B, 4 + s, :], hT[:, s, off:off + B],
                                                wd[:, f, n * 512:(n + 1) * 512], start=(f == 0), stop=(f == MJ - 1))
                        ins.then_inc(r["y_full"], 1)

            def combine(l):
                tt = TT[l]
                pe.wait_ge(r["cb"], 4 + 2 * l)
                per = 4 // tt
                for k in range(KT):
                    u = u0[f"comb{l}"] + k // per
                    if k % per == 0:
                        take(pe, u)
                    for t in range(tt):
                        c = (k % per) * tt + t
                        ins = pe.transpose(bank(u)[:, c * P:(c + 1) * P],
                                           part(S1, 0, 4, D)[:, t, k * P:(k + 1) * P], ident)
                    if k % per == per - 1:
                        ins.then_inc(full[u % 4], 1)

            pe.wait_ge(s_const, 16 * N_CONST)
            pe.wait_ge(s_zero, 1)
            for c in range(4):
                landed(c)
                dense(c, 4, lambda k: x1[:, k, :], u0["lru_in"] + 2 * c, S)
            landed(4)
            for h in range(8):
                u = u0["gates"] + h
                take(pe, u)
                pe.wait_ge(xbr_ready, h + 1)
                for j in range(2):
                    ins = pe.matmul(pair(u)[:, j, :], slot(4, 8, 2 * P)[:, h, j * P:(j + 1) * P], kt8(xbr, h),
                                    start=True, stop=True)
                ins.then_inc(full[u % 4], 1)
            for j in range(2):
                landed(5 + j)
                dense(5 + j, 4, lambda k: kt8(hy, k), u0["lru_out"] + 2 * j, S,
                      ready=(hy_ready, 0) if j == 0 else None)
            pe.wait_ge(s_tab, 16)
            layer_norm(0)
            ffn(0)
            layer_norm(1)
            for j in range(2):
                landed(c0["kv"] + j)
                dense(c0["kv"] + j, 4, lambda k: x1[:, k, :], u0["k"] + 2 * j, S,
                      ready=(x_ready, 8) if j == 0 else None)
            for j in range(2):
                c = c0["kv"] + 2 + j
                landed(c)
                for t in range(2):
                    u = u0["v"] + 2 * j + t
                    take(pe, u)
                    for k in range(KT):
                        ins = pe.matmul(bank(u), x1[:, k, t * P:(t + 1) * P], slot(c)[:, k, :],
                                        start=(k == 0), stop=(k == KT - 1))
                    ins.then_inc(full[u % 4], 1)
            for j in range(2):
                landed(c0["q"] + j)
                dense(c0["q"] + j, 4, lambda k: x1[:, k, :], u0["q"] + 2 * j, S)
            read(pe, u0["q"] + 3)
            read(pe, u0["v"] + 3)
            for what, h in att_order:
                u = att_u[what, h]
                take(pe, u)
                if what == "a":
                    for t in range(2):
                        ins = pe.matmul(pair(u)[:, t, :], kT[:, h, t * P:(t + 1) * P], qT[:, h, :],
                                        start=True, stop=True)
                elif what == "b":
                    pe.wait_ge(at_l, h + 1)
                    ll = zl[:, h % 2, :].rearrange("p (t q) -> p t q", t=2)
                    pe.matmul(pair(u)[:, 0, :], tabv("suffix", P), ll[:, 0, :], start=True, stop=False)
                    pe.matmul(pair(u)[:, 0, :], ones, ll[:, 1, :], start=False, stop=True)
                    ins = pe.matmul(pair(u)[:, 1, :], tabv("suffix", P), ll[:, 1, :], start=True, stop=True)
                else:
                    pe.wait_ge(at_w, h + 1)
                    ww = zw[:, h % 2, :].rearrange("p (t q) -> p t q", t=2)
                    for t in range(2):
                        ins = pe.matmul(bank(u, S), vv[:, t, h * P:(h + 1) * P], ww[:, t, :],
                                        start=(t == 0), stop=(t == 1))
                ins.then_inc(full[u % 4], 1)
            read(pe, att_u["c", NH - 1])
            for j in range(2):
                c = c0["attn_out"] + j
                landed(c)
                dense(c, 4, lambda k: kt8(oT, k), u0["attn_out"] + 2 * j, S)
            layer_norm(2)
            ffn(1)
            layer_norm(3)
            pe.wait_ge(s_late, 16 * N_LATE)
            norm(0)
            for j in range(3):
                c = c0["in_ab"] + j
                landed(c)
                dense(c, 4, lambda k: H[:, k, :], u0["in_ab"] + 4 * j, N2, ready=(h_ready, 0) if j == 0 else None)
            read(pe, u0["in_ab"] + 11)
            for g in range(4):
                for st in range(2):
                    u = u0["dft1"] + 2 * g + st
                    take(pe, u)
                    for t in range(2):
                        ins = pe.matmul(pair(u)[:, t, :], S1[:, g, (2 * st + t) * P:(2 * st + t + 1) * P],
                                        tabv("dft_d", 256), start=True, stop=True)
                    ins.then_inc(full[u % 4], 1)
            for g in range(4):
                u = u0["dft2"] + g
                take(pe, u)
                read(pe, u0["dft1"] + 7)
                for st in range(2):
                    for t in range(2):
                        pe.matmul(pair(u)[:, st, :], fa[:, 2 * st + t, g, 0:P], tabv("cos_l", S, t * S),
                                  start=(t == 0), stop=False)
                        ins = pe.matmul(pair(u)[:, st, :], fa[:, 2 * st + t, g, P:2 * P],
                                        tabv("sin_l", S, t * S), start=False, stop=(t == 1))
                ins.then_inc(full[u % 4], 1)
            c, u = c0["out_ab"], u0["out_ab"]
            landed(c)
            landed(c + 1)
            read(pe, u0["dft2"] + 3)

            def out_ab(m, tiles):
                for k in tiles:
                    if k >= 4:
                        pe.wait_ge(yb_ready, k - 3)
                    rhs = S1[:, k, :] if k < 4 else S3[:, k - 4, :]
                    ins = pe.matmul(bank(u + m), slot(c + m // 4)[:, k, (m % 4) * P:(m % 4 + 1) * P], rhs,
                                    start=(k == 0), stop=(k == KT - 1))
                return ins

            for m in range(4):
                take(pe, u + m)
                out_ab(m, range(4))
            norm(1, 4, sq=S1, off=4)
            for m in range(4):
                out_ab(m, range(4, 8)).then_inc(full[(u + m) % 4], 1)
            for m in range(4, 8):
                take(pe, u + m)
                out_ab(m, range(8)).then_inc(full[(u + m) % 4], 1)
            norm(2, sq=S2)
            pe.wait_ge(h_ready, 16)
            route(0)
            experts(0)
            combine(0)
            norm(3, sq=S2)
            u, c = u0["in_cd"], c0["in_cd"]
            landed(c)
            dense(c, 4, lambda k: H[:, k, 0:S], u, S, ready=(h_ready, 16))
            landed(c + 1)
            dense(c + 1, 2, lambda k: H[:, k, :], u + 2, N2)
            for t in range(4):
                if t % 2 == 0:
                    take(pe, u + 4 + t // 2)
                for k in range(KT):
                    ins = pe.matmul(pair(u + 4 + t // 2)[:, t % 2, :], H[:, k, t * P:(t + 1) * P],
                                    slot(c + 1)[:, k, 256:512], start=(k == 0), stop=(k == KT - 1))
                if t % 2 == 1:
                    ins.then_inc(full[(u + 4 + t // 2) % 4], 1)
            landed(c + 2)
            dense(c + 2, 3, lambda k: H[:, k, 0:S], u + 6, S)
            dense(c + 2, 1, lambda k: H[:, k, :], u + 8, N2, m0=3)
            landed(c + 3)
            dense(c + 3, 1, lambda k: H[:, k, :], u + 9, N2, n=192)
            take(pe, u + 10)
            for k in range(KT):
                ins = pe.matmul(bank(u + 10)[0:64, :], slot(c + 3, KT, 192)[:, k, P:192], H[:, k, :],
                                start=(k == 0), stop=(k == KT - 1))
            ins.then_inc(full[(u + 10) % 4], 1)
            u = u0["ss"]
            take(pe, u)
            pe.wait_ge(cd_sq, 1)
            for k in range(3):
                ins = pe.matmul(bank(u, S), ones, part(S3, 2048, 3, S)[:, k, :], start=(k == 0), stop=(k == 2))
            ins.then_inc(full[u % 4], 1)
            take(pe, u + 1)
            for k in range(2):
                ins = pe.matmul(bank(u + 1), ones, part(S3, 3072, 2, 512)[:, k, :], start=(k == 0), stop=(k == 1))
            ins.then_inc(full[(u + 1) % 4], 1)
            pe.wait_ge(cd_sq, 2)
            for j in range(4):
                take(pe, u + 2 + j)
                pe.matmul(bank(u + 2 + j), ones, cdsq[:, j, :], start=True, stop=True)\
                    .then_inc(full[(u + 2 + j) % 4], 1)
            u, c = u0["uq"], c0["uq"]
            landed(c)
            pe.wait_ge(cd_n, 1)
            wq = slot(c, 3, 768)
            for h in range(4):
                if h % 2 == 0:
                    take(pe, u + h // 2)
                for k in range(3):
                    ins = pe.matmul(pair(u + h // 2)[:, h % 2, :], wq[:, k, h * 192:h * 192 + P], cq[:, k, :],
                                    start=(k == 0), stop=(k == 2))
                if h % 2 == 1:
                    ins.then_inc(full[(u + h // 2) % 4], 1)
            for h in range(4):
                if h % 2 == 0:
                    take(pe, u + 2 + h // 2)
                for k in range(3):
                    ins = pe.matmul(pair(u + 2 + h // 2)[0:64, h % 2, :], wq[:, k, h * 192 + P:(h + 1) * 192],
                                    cq[:, k, :], start=(k == 0), stop=(k == 2))
                if h % 2 == 1:
                    ins.then_inc(full[(u + 2 + h // 2) % 4], 1)
            u, c = u0["ukv"], c0["ukv"]
            landed(c)
            pe.wait_ge(cd_n, 2)
            wk = slot(c, 2, D)
            for h in range(4):
                take(pe, u + h)
                for k in range(2):
                    ins = pe.matmul(bank(u + h), wk[:, k, h * 256:h * 256 + P], ckv[:, k, :],
                                    start=(k == 0), stop=(k == 1))
                ins.then_inc(full[(u + h) % 4], 1)
            for t in range(4):
                take(pe, u + 4 + t)
                for k in range(2):
                    ins = pe.matmul(bank(u + 4 + t).rearrange("p (h d) -> p h d", h=4),
                                    ckv[:, k, t * P:(t + 1) * P],
                                    wk[:, k, :].rearrange("p (h d) -> p h d", h=4)[:, :, P:256],
                                    start=(k == 0), stop=(k == 1))
                ins.then_inc(full[(u + 4 + t) % 4], 1)
            u = u0["rope_c"]
            pe.wait_ge(cd_qk, 1)
            for j in range(3):
                take(pe, u + j)
                rhs = qk[:, j, :] if j < 2 else qk[:, 2:4, 0:S]
                out = bank(u + j) if j < 2 else pair(u + j)
                pe.matmul(out, tabv("swap", P), rhs, start=True, stop=True).then_inc(full[(u + j) % 4], 1)
            u = u0["rope_d"]
            read(pe, u0["uq"] + 3)
            for j in range(3):
                take(pe, u + j)
                rhs = part(S2, 2560 + 512 * j, 512)[0:64, :] if j < 2 else kr[0:64, 0:S]
                pe.matmul(bank(u + j, 512 if j < 2 else S)[0:64, :], tabv("swap", 64, rows=64), rhs,
                          start=True, stop=True).then_inc(full[(u + j) % 4], 1)
            pe.wait_ge(cd_rot, 2)
            read(pe, u0["ukv"] + 7)
            for what, n in so_order:
                u, h, t = so_u[what, n], n // 2, n % 2
                take(pe, u)
                if what == "a":
                    if h < 4:
                        ins = pe.matmul(bank(u), part(S1, h * S, S)[:, t * P:(t + 1) * P], qk[:, 2 + h // 2, :],
                                        start=True, stop=True)
                    else:
                        pe.matmul(bank(u), qn[:, h - 4, t * P:(t + 1) * P], kn[:, h - 4, :], start=True, stop=False)
                        ins = pe.matmul(bank(u), qr[0:64, h - 4, t * P:(t + 1) * P], kr[0:64, :],
                                        start=False, stop=True)
                elif what == "b":
                    pe.wait_ge(so_n, n + 1)
                    for k in range(4):
                        ins = pe.transpose(bank(u)[:, k * P:(k + 1) * P], pp[:, n % 2, k * P:(k + 1) * P], ident)
                else:
                    read(pe, so_u["b", n])
                    for k in range(4):
                        v = (vC[:, k, (h // 2) * P:(h // 2 + 1) * P] if h < 4 else
                             vD[:, k, (h - 4) * P:(h - 3) * P])
                        ins = pe.matmul(bank(u, P), v, pt[:, n % 2, k * P:(k + 1) * P],
                                        start=(k == 0), stop=(k == 3))
                ins.then_inc(full[u % 4], 1)
            read(pe, so_u["c", 15])
            for j in range(2):
                c = c0["out_cd"] + j
                landed(c)
                dense(c, 4, lambda k: kt8(oo, k), u0["out_cd"] + 2 * j, S)
            norm(4, n=S)
            pe.wait_ge(h_ready, 32)
            route(1)
            experts(1)
            combine(1)
            norm(5, n=S, sq=S2)


        @block.scalar
        def _(act):
            own = Chain(act, act_own)
            A = nc.scalar.activation

            def layer_norm(i):
                for j in range(4):
                    act.wait_ge(ln_xc, 4 * i + j + 1)
                    A(lsq[:, 2 * j:2 * j + 2, :], lxc[:, 2 * j:2 * j + 2, :], ACT.Square).then_inc(ln_sq, 1)
                act.wait_ge(ln_var, i + 1)
                A(std[:, 0, 0:S // 4], T[:, 7, 0:S // 4], ACT.Sqrt, scale=1.0 / D, bias=LN_EPS).then_inc(ln_std, 1)
                for k in range(KT):
                    act.wait_ge(ln_nrm, 8 * i + k + 1)
                    A(x1[:, k, :], lns[:, k, :], ACT_F, bias=vc("ln_b", 8 * i + k)).then_inc(x_ready, 1)

            def ffn(l):
                with act.Fori(0, NJ // 2) as i:
                    for t, m in ((t, t % 4) for t in range(8)):
                        for h in range(2):
                            cw = 3 * 48 * l + 2 * 48 + 24 * h + t
                            cb = 48 * l + 24 * h + t
                            if h == 0:
                                act.wait_ge(g_ready, i * 8 + (24 * l + t + 1))
                                act.wait_ge(f_full, i * 8 + (24 * l + t + 1))
                            A(hab[:, m % 2, h, :], T[:, m % 2, h * S:(h + 1) * S], ACT_F,
                              scale=vec[:, ds(i * 8 + (VEC["ffn_conv_w"] + cw), 1)],
                              bias=vec[:, ds(i * 8 + (VEC["ffn_conv_b"] + cb), 1)]).then_inc(f_id, 1)
                        act.wait_ge(f_conv, i * 8 + (24 * l + t + 3))
                        A(hab[:, m % 2, 0, :], hab[:, m % 2, 0, :], ACT.Gelu_apprx_tanh).then_inc(f_gelu, 1)
                        if m == 3:
                            act.wait_ge(mod_sum, i * 2 + (t // 4 + NJ * l + 1))
                            A(mrow, T[:, 2, :], ACT.Copy).then_inc(mod_row, 1)

            def norm(r, src, k_tiles=KT, n=N2, sq=S1, off=0, wait=None, shift=None):
                for j in range(k_tiles // 2):
                    if wait is not None:
                        wait(2 * j + 1)
                    A(sq[:, off + 2 * j:off + 2 * j + 2, 0:n], src[:, 2 * j:2 * j + 2, 0:n],
                      ACT.Square).then_inc(n_sq, 1)
                act.wait_ge(n_ms, r + 1)
                A(std[:, 0, 0:n // 4], T[:, 7, 0:n // 4], ACT.Sqrt, scale=1.0 / (k_tiles * P), bias=RMS_EPS).then_inc(n_std, 1)
                if shift is not None:
                    l, w, q = shift
                    streams = n // S
                    for k in range(KT):
                        act.wait_ge(n_nrm, 8 * q + k + 1)
                        for v in range(streams):
                            ins = A(H[:, k, v * S:(v + 1) * S], H[:, k, v * S:(v + 1) * S], ACT_F,
                                    bias=modv[:, l, 24 * w + k, v:v + 1])
                        ins.then_inc(h_ready, 1)

            def evac(u, out, n=512, rows=P, in_=None, scale=1.0, func=ACT_F, bias=0.0):
                got(act, u)
                A(out, bank(u, n)[0:rows, :] if in_ is None else in_, func, scale=scale, bias=bias)\
                    .then_inc(free[u % 4], 1)

            def route(l):
                tt = TT[l]
                for t in range(tt):
                    u = u0[f"rows{l}"] + 2 * t
                    evac(u, hrow[:, t, 0:512])
                act.wait_ge(r["ge"], l + 1)
                A(rt[:, 512:512 + 5 * tt], rt[:, 512:512 + 5 * tt], ACT.Exp).then_inc(r["gx"], 1)

            def experts(l):
                nc.scalar.preload_act_table(ACT.Silu)
                act.wait_ge(r["planned"], l + 1)
                t0, t1 = turns(act, l)
                if l == 0:
                    for s in range(2):
                        act.sem_inc(r["y_st"][s], 32)
                    act.sem_inc(r["m_act"], 2)
                act.wait_ge(r["zeroed"], 16 * 4)
                with act.Fori(t0, t1) as i:
                    at = turn_of_layer(i, t0, l)
                    for s in range(2):
                        act.wait_ge(r["m_full"], 2 * i + (s + 3))
                        A(sg[:, s, :], T[:, s, 0:256], ACT.Silu).then_inc(r["sg"], 1)
                        act.wait_ge(r["y_st"][s], 32 * i + 32)
                        act.wait_ge(r["y_full"], 2 * i + (s + 3))
                        A(yb[:, s, :], T[:, 4 + s, :], ACT.Copy).then_inc(r["m_act"], 1)
                        act.wait_ge(r["m_act"], 2 * i + (s + 3))
                        for n in range(2):
                            act.dma_start(y_rows[ds(at * (2 * B) + s * B, B), n * 512:(n + 1) * 512],
                                          yb[n * B:(n + 1) * B, s, :]).then_inc(r["y_st"][s], 16)
                for s in range(2):
                    act.wait_ge(r["y_st"][s], t1 * 32 + 32)
                act.sem_inc(r["y_all"], 1)

            act.dma_start(x1, a["xT"].rearrange("(k p) n -> p k n", p=P)).then_inc(s_const, 16)
            act.dma_start(vec[:, :], a["vec"]).then_inc(s_const, 16)
            act.wait_ge(s_const, 16 * N_CONST)
            act.dma_start(tab[:, :], a["tab"]).then_inc(s_tab, 16)
            act.wait_ge(s_sp, 1)
            A(sp[:, 1, :], sp[:, 0, :], ACT.Exp, scale=-1.0).then_inc(s_sp, 1)
            act.wait_ge(s_const, 16 * N_CONST)
            A(cs[:, :], vc("c", 0, 16), ACT.Sigmoid).then_inc(s_cs, 1)
            for u in range(8):
                got(act, u)
                for j in range(2):
                    m = 2 * u + j
                    if m < 8:
                        ins = A(ybr[:, m, :], pair(u)[:, j, :], ACT.Gelu_apprx_tanh, bias=vc("lru_b_in", m))
                    else:
                        ins = A(xp[:, m - 8, :], pair(u)[:, j, :], ACT_F, bias=vc("lru_b_in", m))
                ins.then_inc(free[u % 4], 1)
            for h in range(8):
                u = u0["gates"] + h
                got(act, u)
                A(gi[:, h, :], pair(u)[:, 0, :], ACT.Sigmoid, bias=vc("lru_b_gates", h))
                A(gr[:, h, :], pair(u)[:, 1, :], ACT.Sigmoid, bias=vc("lru_b_gates", 8 + h))\
                    .then_inc(free[u % 4], 1)
            read(act, u0["gates"] + 7)
            act.wait_ge(s_sp, 3)
            for k in range(8):
                A(av[:, k, :], gr[:, k, :], ACT.Exp, scale=sp[:, 6, k:k + 1])
                A(m2[:, k, :], gr[:, k, :], ACT.Exp, scale=sp[:, 7, k:k + 1]).then_inc(a_ready, 1)
            act.wait_ge(m2_ready, 1)
            A(m2[:, :, :], m2[:, :, :], ACT.Sqrt).then_inc(mult_ready, 1)
            for j in range(4):
                u = u0["lru_out"] + j
                got(act, u)
                for h in range(2):
                    ins = A(lo[:, 2 * j + h, :], pair(u)[:, h, :], ACT_F, bias=vc("lru_b_out", 2 * j + h))
                ins.then_inc(free[u % 4], 1)
            layer_norm(0)
            ffn(0)
            layer_norm(1)
            for j in range(4):
                evac(u0["k"] + j, kT[:, 2 * j:2 * j + 2, :], in_=pair(u0["k"] + j))
            for j in range(4):
                evac(u0["q"] + j, qT[:, 2 * j:2 * j + 2, :], in_=pair(u0["q"] + j))
            nc.scalar.preload_act_table_set("natural_log_exp_and_others")
            for h in range(NH + 2):
                if h < NH:
                    if h >= 2:
                        act.wait_ge(at_w, h - 1)
                    evac(att_u["a", h], zs[:, h % 2, :], scale=float(P) ** -0.5)
                    read(act, att_u["a", h])
                    own(A(ze[:, h % 2, :], zs[:, h % 2, :], ACT.Abs))
                    own(A(ze[:, h % 2, :], ze[:, h % 2, :], ACT.Exp, scale=-1.0))
                    A(ze[:, h % 2, :], ze[:, h % 2, :], ACT.Ln, bias=1.0).then_inc(at_ln, 1)
                if 1 <= h <= NH:
                    act.wait_ge(at_e, h)
                    A(zw[:, (h - 1) % 2, :], zw[:, (h - 1) % 2, :], ACT.Exp).then_inc(at_w0, 1)
                if h >= 2:
                    evac(att_u["c", h - 2], oT[:, h - 2, :], n=S)
            layer_norm(2)
            ffn(1)
            layer_norm(3)
            act.wait_ge(gs_ready, 1)
            act.wait_ge(x_ready, 32)
            act.wait_ge(s_late, 16 * N_LATE)
            norm(0, X, shift=(0, 0, 0))
            for m in range(4):
                evac(u0["in_ab"] + m, S1[:, 4 + m, :], func=ACT.Sigmoid)

            def conv_products(taps):
                for t in taps:
                    out = S3[:, 4 + t % 4, :] if t else S3[:, 3, :]
                    if t >= 5:
                        act.wait_ge(cv_used, t - 4)
                    A(out.rearrange("p (a n) -> p a n", a=2), U[:, 3, :, t:t + S], ACT_F, scale=vc("conv_w", 4 * t + 3),
                      bias=vc("conv_b", 3) if t == 0 else 0.0).then_inc(cv_ready, 1)

            read(act, u0["in_ab"] + 7)
            for m in range(4):
                evac(u0["in_ab"] + 8 + m, S1[:, m, :])
                conv_products(range(5 * m, 5 * m + 5))
            for g in range(4):
                for st in range(2):
                    u = u0["dft1"] + 2 * g + st
                    evac(u, fa[:, 2 * st:2 * st + 2, g, :], in_=pair(u))
                conv_products(range(20 + 2 * g, 22 + 2 * g))
            for g in range(4):
                evac(u0["dft2"] + g, S1[:, g, :])
                conv_products(range(28 + g, min(29 + g, CONV)))
            norm(1, S3, 4, sq=S1, off=4, wait=lambda k: act.wait_ge(yc_ready, 2))
            for m in range(4):
                act.wait_ge(yn_ready, m + 1)
                A(S3[:, m, :], S3[:, m, :], ACT.Silu).then_inc(yb_ready, 1)
            norm(2, X, sq=S2, wait=lambda k: read(act, u0["out_ab"] + k), shift=(0, 1, 1))
            route(0)
            experts(0)
            norm(3, X, sq=S2, wait=lambda k: read(act, u0["comb0"] + k), shift=(1, 0, 2))
            u = u0["in_cd"]
            for j in range(2):
                evac(u + j, part(S1, 512 * j, 512))
            for j in range(2):
                evac(u + 2 + j, qk[:, 2 + j, :])
            for j in range(2):
                evac(u + 4 + j, part(S1, 2048 + 512 * j, 512))
            evac(u + 6, part(S1, 3072, 512))
            evac(u + 7, part(S1, 3584, 256), n=256)
            for j in range(2):
                evac(u + 8 + j, ckv[:, j, :])
            evac(u + 10, kr[0:64, :], rows=64)
            read(act, u + 10)
            A(part(S3, 2048, 768), part(S1, 3072, 768), ACT.Square)
            A(part(S3, 3072, 1024), part(S2, 0, 1024), ACT.Square).then_inc(cd_sq, 1)
            A(flat(S3)[:, 0:2048], flat(S1)[:, 0:2048], ACT.Square).then_inc(cd_sq, 1)
            u = u0["ss"]
            evac(u, std[:, 0, 0:S], n=S, func=ACT.Sqrt, scale=1.0 / 384, bias=RMS_EPS)
            evac(u + 1, std[:, 1, :], func=ACT.Sqrt, scale=1.0 / 256, bias=RMS_EPS)
            for j in range(4):
                evac(u + 2 + j, cdr[:, j, :], func=ACT.Sqrt, scale=1.0 / P, bias=RMS_EPS)
            u = u0["uq"]
            for j in range(2):
                evac(u + j, part(S2, 1536 + 512 * j, 512))
            for j in range(2):
                evac(u + 2 + j, part(S2, 2560 + 512 * j, 512)[0:64, :], rows=64)
            u = u0["ukv"]
            for j in range(4):
                evac(u + j, kn[:, j, :])
            for j in range(4):
                evac(u + 4 + j, vD[:, j, :])
            for n in range(16 + 2):
                if n < 16:
                    h = n // 2
                    scale = float(P) ** -0.5 if h < 4 else 192.0 ** -0.5
                    got(act, so_u["a", n])
                    act.wait_ge(so_m, n + 1)
                    if n >= 2:
                        got(act, so_u["b", n - 2])
                    A(pp[:, n % 2, :], bank(so_u["a", n]), ACT.Exp, scale=scale, bias=rt[:, 2 * n:2 * n + 1],
                      accum_out=rt[:, 64 + 2 * n:65 + 2 * n]).then_inc(free[so_u["a", n] % 4], 1)
                if n >= 2:
                    h, t = (n - 2) // 2, n % 2
                    evac(so_u["c", n - 2], oo[:, h, t * P:(t + 1) * P], n=P)
            norm(4, X, n=S, wait=lambda k: read(act, u0["out_cd"] + k // 2), shift=(1, 1, 3))
            route(1)
            experts(1)
            norm(5, X, n=S, sq=S2, wait=lambda k: read(act, u0["comb1"] + k // 2))

        @block.vector
        def _(dve):
            own = Chain(dve, dve_own)
            V = nc.vector
            STT = V.scalar_tensor_tensor

            def layer_norm(i):
                dve.wait_ge(ln_mean, i + 1)
                for j in range(4):
                    STT(out=lxc[:, 2 * j:2 * j + 2, :], in0=T[:, 6:7, 0:S].to_broadcast([P, 2, S]), scalar=-1.0 / D,
                        in1=lns[:, 2 * j:2 * j + 2, :], op0=ALU.mult, op1=ALU.add).then_inc(ln_xc, 1)
                dve.wait_ge(ln_std, i + 1)
                V.reciprocal(std[:, 1, 0:S // 4], std[:, 0, 0:S // 4]).then_inc(ln_rs, 1)
                dve.wait_ge(ln_bc, i + 1)
                dve.wait_ge(ln_xc, 4 * i + 4)
                for k in range(KT):
                    STT(out=lns[:, k, :], in0=lxc[:, k, :], scalar=vc("ln_g", 8 * i + k), in1=T[:, 6, 0:S],
                        op0=ALU.mult, op1=ALU.mult).then_inc(ln_nrm, 1)

            def residual(units, i):
                for j, u in enumerate(units):
                    got(dve, u)
                    for h in range(2):
                        k = 2 * j + h
                        ins = STT(out=lns[:, k, :], in0=x1[:, k, :], scalar=ALPHA, in1=pair(u)[:, h, :],
                                  op0=ALU.mult, op1=ALU.add)
                    ins.then_inc(free[u % 4], 1)

            def ffn(l):
                base = c0[f"ffn{l}"]
                if l == 0:
                    dve.sem_inc(f_conv, 2)
                    dve.sem_inc(g_ready, 2)
                    dve.sem_inc(mod_out, 1)
                    dve.wait_ge(s_cs, 2)
                with dve.Fori(0, NJ // 2) as i:
                    own.loop(i, 2 * (4 * 3 + 30))

                    def mod_steps(p, first, n):
                        for q in range(first, first + n):
                            j, k, v = q // 16, (q // 2) % 8, q % 2
                            c = base + 5 * p + 2 + j
                            if q % 16 == 0:
                                dve.wait_ge(w_landed[slot_of[c]], i * 64 + 16 * nth[c])
                            w, sc = slot(c)[:, k, :], cs[:, 8 * v + k:8 * v + k + 1]
                            if k == 0:
                                ins = V.tensor_scalar(macc[:, j, v, :], w, sc, None, ALU.mult)
                            else:
                                own.wait(last[j, v])
                                ins = STT(out=macc[:, j, v, :], in0=w, scalar=sc, in1=macc[:, j, v, :],
                                          op0=ALU.mult, op1=ALU.add)
                            if q % 16 == 15:
                                ins.then_inc(mod_acc_ready, 1)
                            else:
                                last[j, v] = own.mark(ins)

                    last = {}
                    for p, m in ((p, m) for p in range(2) for m in range(4)):
                        t = 4 * p + m
                        b = m % 2

                        def tap(h, w, shift):
                            cw = 3 * 48 * l + w * 48 + 24 * h + t
                            return STT(out=hab[:, b, h, shift:S], in0=T[:, b, h * S:(h + 1) * S - shift],
                                       scalar=vec[:, ds(i * 8 + (VEC["ffn_conv_w"] + cw), 1)],
                                       in1=hab[:, b, h, shift:S], op0=ALU.mult, op1=ALU.add)

                        if m == 0:
                            mod_steps(p, 0, 10)
                        dve.wait_ge(f_id, i * 16 + (48 * l + 2 * t + 2))
                        n1 = own.mark(tap(0, 1, 1))
                        n2 = own.mark(tap(1, 1, 1))
                        own.wait(n1)
                        n3 = own.mark(tap(0, 0, 2))
                        own.wait(n2)
                        tap(1, 0, 2).then_inc(f_conv, 1)
                        mod_steps(p, (10, 16, 24, 32)[m], (4, 4, 4, 0)[m])
                        dve.wait_ge(f_gelu, i * 8 + (24 * l + t + 1))
                        dve.wait_ge(g_used, i * 8 + (24 * l + t + 1))
                        V.tensor_tensor(gT[:, b, :], hab[:, b, 0, :], hab[:, b, 1, :], ALU.mult).then_inc(g_ready, 1)
                        mod_steps(p, (14, 20, 28, 32)[m], (2, 4, 4, 0)[m])
                        if m == 3:
                            dve.wait_ge(mod_turned, i * 2 + (p + NJ * l + 1))
                            bias = vec[:, ds(i * 16 + (8 * p + VEC["mod_b"] + 48 * l), 8)]
                            sums = T[:, 3, :].rearrange("p (m j v n) -> p j m v n", m=4, j=2, v=2)
                            for j in range(2):
                                ins = V.tensor_tensor(modv[:, l, ds(i * 16 + (8 * p + 4 * j), 4), :], sums[:, j, :, :, 0],
                                                      bias[:, 4 * j:4 * j + 4].unsqueeze(2).to_broadcast([P, 4, 2]),
                                                      ALU.add)
                            ins.then_inc(mod_out, 1)
                own.end_loop(NJ // 2)
                dve.wait_ge(acc_ready, l + 1)
                for k in range(KT):
                    ins = STT(out=lns[:, k, :], in0=x1[:, k, :], scalar=ALPHA,
                              in1=T[:, 4 + k // 2, (k % 2) * S:(k % 2 + 1) * S], op0=ALU.mult, op1=ALU.add)
                ins.then_inc(ln_src, 1)

            def norm(r, gain, n=N2, out=H, q=None):
                dve.wait_ge(n_std, r + 1)
                V.reciprocal(std[:, 1, 0:n // 4], std[:, 0, 0:n // 4]).then_inc(n_rs, 1)
                dve.wait_ge(n_bc, r + 1)
                for k in range(KT):
                    for v in range(n // S):
                        ins = STT(out=out[:, k, v * S:(v + 1) * S], in0=X[:, k, v * S:(v + 1) * S],
                                  scalar=gain(k, v), in1=T[:, 6, v * S:(v + 1) * S], op0=ALU.mult, op1=ALU.mult)
                    ins.then_inc(n_nrm, 1)

            def add_gated(u, k, l, which, width, half_=None):
                for v in range(width // S):
                    src = bank(u)[:, v * S:(v + 1) * S] if half_ is None else pair(u)[:, half_, :]
                    ins = STT(out=X[:, k, v * S:(v + 1) * S], in0=src, scalar=modv[:, l, which * 8 + k, v:v + 1],
                              in1=X[:, k, v * S:(v + 1) * S], op0=ALU.mult, op1=ALU.add)
                return ins

            def route(l):
                tt = TT[l]
                for t in range(tt):
                    u = u0[f"rows{l}"] + 2 * t + 1
                    got(dve, u)
                    V.tensor_copy(hrow[:, t, 512:1024], bank(u)).then_inc(free[u % 4], 1)
                n = tt * NE
                v3 = lambda off, w: rt[:, off:off + tt * w].rearrange("p (t e) -> p t e", t=tt)
                M, oh1, oh2, tmp = v3(0, NE), v3(128, NE), v3(256, NE), v3(384, NE)
                ge, gap = v3(512, 4), v3(512 + 4 * tt, 1)
                lg, t4, ohg = v3(544, 36), v3(688, 4), v3(704, 4)
                gm, gi_, m1, i1, m2_, w1, w2, gp = (v3(720 + 4 * j, 1) for j in range(8))
                cnt, nb, ends, st = (rt[:, 752 + 32 * j:784 + 32 * j] for j in range(4))
                bc = lambda x, w: x.to_broadcast([P, tt, w])
                iota = lambda w: tab[:, TAB["iota"]:TAB["iota"] + w].unsqueeze(1).to_broadcast([P, tt, w])
                u = u0[f"logit{l}"]
                got(dve, u)
                ins = V.tensor_copy(lg, bank(u, tt * 36).rearrange("p (t e) -> p t e", t=tt))
                ins.then_inc(free[u % 4], 1)
                read(dve, u)
                G, E = lg[:, :, 0:4], lg[:, :, 4:36]
                own(V.tensor_reduce(gm, G, AX.X, ALU.max))
                own(V.tensor_tensor(ge, G, bc(gm, 4), ALU.subtract))
                own(V.tensor_tensor(t4, G, bc(gm, 4), ALU.is_equal))
                own(STT(out=t4, in0=t4, scalar=-100.0, in1=iota(4), op0=ALU.mult, op1=ALU.add))
                own(V.tensor_reduce(gi_, t4, AX.X, ALU.min))
                own(V.tensor_tensor(ohg, t4, bc(gi_, 4), ALU.is_equal))
                own(V.tensor_scalar(ohg, ohg, -1.0, 1e30, ALU.add, ALU.mult))
                E4 = E.rearrange("p t (g e) -> p t g e", g=4)
                own(V.tensor_tensor(E4, E4, ohg.unsqueeze(3).to_broadcast([P, tt, 4, 8]), ALU.add))
                for m_, i_, oh in ((m1, i1, oh1), (m2_, i1, oh2)):
                    own(V.tensor_reduce(m_, E, AX.X, ALU.max))
                    own(V.tensor_tensor(tmp, E, bc(m_, NE), ALU.is_equal))
                    own(STT(out=tmp, in0=tmp, scalar=-100.0, in1=iota(NE), op0=ALU.mult, op1=ALU.add))
                    own(V.tensor_reduce(i_, tmp, AX.X, ALU.min))
                    own(V.tensor_tensor(oh, tmp, bc(i_, NE), ALU.is_equal))
                    if oh is oh1:
                        own(STT(out=E, in0=oh, scalar=-2e30, in1=E, op0=ALU.mult, op1=ALU.add))
                V.tensor_tensor(M, oh1, oh2, ALU.add).then_inc(r["m_ready"], 1)
                V.tensor_tensor(gap, m2_, m1, ALU.subtract).then_inc(r["ge"], 1)
                dve.wait_ge(r["gx"], l + 1)
                own(V.tensor_reduce(gp, ge, AX.X, ALU.add))
                own(V.tensor_scalar(w1, gap, 1.0, None, ALU.add))
                own(V.tensor_tensor(w1, w1, gp, ALU.mult))
                own(V.reciprocal(w1, w1))
                own(V.tensor_tensor(w2, w1, gap, ALU.mult))
                u = u0[f"rank{l}"]
                got(dve, u + 1)
                nth = NTOK[l] // B
                V.tensor_copy(cnt, bank(u + 1, NE)).then_inc(free[(u + 1) % 4], 1)
                read(dve, u + 1)
                own(V.tensor_tensor(tmp_th(nth), cnt.unsqueeze(2).to_broadcast([P, NE, nth]),
                                tab[:, TAB["thresh"]:TAB["thresh"] + nth].unsqueeze(1).to_broadcast([P, NE, nth]),
                                ALU.is_gt))
                own(V.tensor_reduce(nb.unsqueeze(2), tmp_th(nth), AX.X, ALU.add))
                own(V.tensor_scalar(nb, nb, 1.0, None, ALU.max))
                own(V.tensor_tensor_scan(ends, ones[:, 0:NE], nb, 0.0, ALU.mult, ALU.add))
                own(V.tensor_tensor(st, ends, nb, ALU.subtract))
                own(V.tensor_scalar(st, st, float(B), None, ALU.mult))
                got(dve, u)
                V.tensor_tensor(tmp, bank(u, n).rearrange("p (t e) -> p t e", t=tt),
                                st.unsqueeze(1).to_broadcast([P, tt, NE]), ALU.add).then_inc(free[u % 4], 1)
                read(dve, u)
                own(V.tensor_tensor(oh1, oh1, tmp, ALU.mult))
                own(V.tensor_tensor(oh2, oh2, tmp, ALU.mult))
                own(V.tensor_reduce(gm, oh1, AX.X, ALU.add))
                own(V.tensor_reduce(gi_, oh2, AX.X, ALU.add))
                own(V.tensor_copy(dst[:, 0:tt, 0:1], gm))
                V.tensor_copy(dst[:, 0:tt, 1:2], gi_).then_inc(r["dest"], 1)
                nb_ = NBLK[l]
                cmp_ = flat(H)[0:1, 0:nb_ * NE].rearrange("p (b e) -> p b e", b=nb_)
                io = tab[0:1, TAB["iota"]:TAB["iota"] + nb_]
                fl = rt[0:1, 880:880 + nb_ + 1]
                for j in range(1, 3):
                    read(dve, u0[f"rows{l}"] + 2 * tt - j)
                own(V.tensor_tensor(cmp_, ends[0:1, :].unsqueeze(1).to_broadcast([1, nb_, NE]),
                                    io.unsqueeze(2).to_broadcast([1, nb_, NE]), ALU.is_le))
                own(V.tensor_reduce(fl[:, 1:nb_ + 1].unsqueeze(2), cmp_, AX.X, ALU.add))
                own(V.tensor_scalar(fl[:, 1:nb_ + 1], fl[:, 1:nb_ + 1], float(NE - 1), None, ALU.min))
                own(V.tensor_scalar(cmp_[:, 0, 0:nb_ // 2], io[:, 0:nb_ // 2], 2.0, ends[0:1, NE - 1:NE], ALU.mult,
                                    ALU.is_lt))
                own(V.tensor_reduce(fl[:, 0:1], cmp_[:, 0, 0:nb_ // 2], AX.X, ALU.add))
                V.tensor_copy(plan[0:1, l, 0:nb_ + 1], fl).then_inc(r["planned"], 1)

            def tmp_th(nth):
                return rt[:, 384:384 + NE * nth].rearrange("p (e j) -> p e j", e=NE)

            def experts(l):
                dve.wait_ge(r["planned"], l + 1)
                t0, t1 = turns(dve, l)
                if l == 0:
                    dve.sem_inc(r["xT"], 1)

                rel = rt[:, 720:728]

                def rows(turn, n):
                    step = 4 // TT[l]
                    for t in range(TT[l]):
                        oh = onehot[:, t, :]
                        V.tensor_scalar(oh, tabv("iota", P), rel[:, t:t + 1], None, ALU.is_equal)\
                            .then_inc(r["oh_own"], step)
                        dve.wait_ge(r["oh_own"], (0 if turn is None else turn * 5) + (n + step * (t + 1)))
                        ins = STT(out=oh, in0=tabv("iota", P), scalar=rel[:, 4 + t:5 + t], in1=oh, op0=ALU.is_equal,
                                  op1=ALU.add)
                    ins.then_inc(r["oh"], 1)

                def tokens(i):
                    dve.wait_ge(r["tr"], i + (l + 1))
                    V.tensor_copy(part(S1, 0, 2, 512), T[:, 6:8, :]).then_inc(r["xT"], 1)

                rows(t0 if l else None, 4 * l)
                tokens(t0)
                with dve.Fori(t0, t1) as i:
                    V.tensor_scalar(rel, rel, -float(P), None, ALU.add).then_inc(r["oh_own"], 1)
                    dve.wait_ge(r["oh_own"], i * 5 + (4 * l + 5))
                    rows(i, 4 * l + 5)
                    for s in range(2):
                        dve.wait_ge(r["sg"], 2 * i + (s + 1))
                        V.tensor_tensor(hm[:, s, :], sg[:, s, :], T[:, s, 256:512], ALU.mult).then_inc(r["hm"], 1)
                        dve.wait_ge(r["hT_full"], 2 * i + (s + 1))
                        V.tensor_copy(hT[:, s, :], T[:, 2, 0:256]).then_inc(r["hT"], 1)
                    tokens(i + 1)
                dve.wait_ge(r["xT"], t1 + (l + 2))
                dve.sem_inc(r["xT_all"], 1)

            def combine(l):
                tt = TT[l]
                v3 = lambda off: rt[:, off:off + tt]
                w1, w2 = v3(740), v3(744)
                g0, g1 = part(S1, 0, 4, D), part(S2, 0, 4, D)
                for t in range(tt):
                    dve.wait_ge(r["cg"][t], 32 * (l + 1))
                    own(V.tensor_scalar(g0[:, t, :], g0[:, t, :], w1[:, t:t + 1], None, ALU.mult))
                    STT(out=g0[:, t, :], in0=g1[:, t, :], scalar=w2[:, t:t + 1], in1=g0[:, t, :],
                        op0=ALU.mult, op1=ALU.add).then_inc(r["cb"], 1)
                per = 4 // tt
                for k in range(KT):
                    u = u0[f"comb{l}"] + k // per
                    got(dve, u)
                    ins = add_gated(u, k, l, 5, tt * P, None if per == 1 else k % 2)
                    if k % per == per - 1:
                        ins.then_inc(free[u % 4], 1)

            V.memset(zb[:, :], 0.0).then_inc(s_zero, 1)
            dve.wait_ge(s_const, 16 * N_CONST)
            STT(out=sp[:, 0, :], in0=vc("lru_a", 0, 8), scalar=-1.0, in1=vc("lru_a", 0, 8), op0=ALU.mult, op1=ALU.max)\
                .then_inc(s_sp, 1)
            dve.wait_ge(s_sp, 2)
            e, t_, t2, q_ = sp[:, 1, :], sp[:, 2, :], sp[:, 3, :], sp[:, 4, :]
            own(V.tensor_scalar(t_, e, 2.0, None, ALU.add))
            own(V.reciprocal(t_, t_))
            own(V.tensor_tensor(t_, t_, e, ALU.mult))
            own(V.tensor_tensor(t2, t_, t_, ALU.mult))
            own(V.memset(q_, 1.0 / 17))
            for n in (15, 13, 11, 9, 7, 5, 3, 1):
                own(V.tensor_tensor(q_, q_, t2, ALU.mult))
                own(V.tensor_scalar(q_, q_, 1.0 / n, None, ALU.add))
            own(V.tensor_tensor(q_, q_, t_, ALU.mult))
            own(V.tensor_scalar(t_, vc("lru_a", 0, 8), -1.0, 0.0, ALU.mult, ALU.max))
            own(STT(out=q_, in0=q_, scalar=2.0, in1=t_, op0=ALU.mult, op1=ALU.add))
            own(V.tensor_scalar(sp[:, 6, :], q_, -8.0, None, ALU.mult))
            V.tensor_scalar(sp[:, 7, :], q_, -16.0, None, ALU.mult).then_inc(s_sp, 1)
            dve.wait_ge(s_cs, 1)
            V.tensor_tensor(cs[:, :], cs[:, :], vc("c", 0, 16), ALU.mult).then_inc(s_cs, 1)
            for k in range(8):
                read(dve, 4 + k // 2)
                cw = lambda t: vc("lru_conv_w", 8 * t + k)
                own(V.tensor_scalar(xbr[:, k, :], xp[:, k, :], cw(3), vc("lru_conv_b", k), ALU.mult, ALU.add))
                for t in (2, 1, 0):
                    sh = 3 - t
                    ins = STT(out=xbr[:, k, sh:S], in0=xp[:, k, 0:S - sh], scalar=cw(t), in1=xbr[:, k, sh:S],
                              op0=ALU.mult, op1=ALU.add)
                    if t:
                        own(ins)
                ins.then_inc(xbr_ready, 1)
            dve.wait_ge(xbr_ready, 8)
            dve.wait_ge(a_ready, 1)
            own(V.tensor_tensor(gi, gi, xbr, ALU.mult))
            for j in range(2):
                dve.wait_ge(a_ready, 4 * j + 4)
                h2 = m2[:, 4 * j:4 * j + 4, :]
                own(V.tensor_scalar(h2, h2, -1.0, 1.0, ALU.mult, ALU.add))
                ins = V.tensor_scalar(h2, h2, 2.0 ** -100, None, ALU.max)
            ins.then_inc(m2_ready, 1)
            dve.wait_ge(mult_ready, 1)
            own(V.memset(m2[:, :, 0:1], 1.0))
            own(V.tensor_tensor(uu, m2, gi, ALU.mult))
            for k in range(8):
                own(V.tensor_tensor_scan(hs[:, k, :], av[:, k, :], uu[:, k, :], 0.0, ALU.mult, ALU.add))
                V.tensor_tensor(hy[:, k, :], hs[:, k, :], ybr[:, k, :], ALU.mult).then_inc(hy_ready, 1)
            for k in range(8):
                read(dve, u0["lru_out"] + k // 2)
                ins = STT(out=lns[:, k, :], in0=x1[:, k, :], scalar=ALPHA, in1=lo[:, k, :], op0=ALU.mult,
                          op1=ALU.add)
            ins.then_inc(ln_src, 1)
            layer_norm(0)
            ffn(0)
            layer_norm(1)
            for j in range(4):
                u = u0["v"] + j
                got(dve, u)
                V.tensor_copy(vv[:, j % 2, (j // 2) * 512:(j // 2 + 1) * 512], bank(u))\
                    .then_inc(free[u % 4], 1)
            dve.wait_ge(s_tab, 16)
            mask = tabv("mask", 512)
            for h in range(NH + 1):
                if h < NH:
                    b = h % 2
                    dve.wait_ge(at_ln, h + 1)
                    if h >= 2:
                        got(dve, att_u["b", h - 2])
                    own(STT(out=zl[:, b, :], in0=zs[:, b, :], scalar=0.0, in1=ze[:, b, :],
                            op0=ALU.max, op1=ALU.add))
                    STT(out=zl[:, b, :], in0=zl[:, b, :], scalar=-1.0, in1=mask, op0=ALU.mult, op1=ALU.mult)\
                        .then_inc(at_l, 1)
                if h >= 1:
                    b = (h - 1) % 2
                    dve.wait_ge(at_w0, h)
                    V.tensor_tensor(zw[:, b, :], zw[:, b, :], mask, ALU.mult).then_inc(at_w, 1)
                if h < NH:
                    b = h % 2
                    u = att_u["b", h]
                    got(dve, u)
                    if h >= 2:
                        got(dve, att_u["c", h - 2])
                    ins = V.tensor_tensor(zw[:, b, :], bank(u), zs[:, b, :], ALU.add)
                    ins.then_inc(free[u % 4], 1)
                    read(dve, u)
                    V.tensor_scalar(zw[:, b, :], zw[:, b, :], 0.0, None, ALU.min).then_inc(at_e, 1)
            residual([u0["attn_out"] + j for j in range(4)], 2)
            layer_norm(2)
            ffn(1)
            layer_norm(3)
            dve.wait_ge(mod_out, 13)
            for q in range(4):
                l, w = q // 2, q % 2
                gain = vc(("norm_mix_g", "norm_ffn_g")[w], 8 * l, 8).unsqueeze(2).to_broadcast([P, 8, 2])
                own(V.tensor_scalar(gsv[:, q, :, :], modv[:, l, 24 * w + 8:24 * w + 16, :], 1.0, None, ALU.add))
                ins = V.tensor_tensor(gsv[:, q, :, :], gsv[:, q, :, :], gain, ALU.mult)
                own(ins)
            dve.sem_inc(gs_ready, 1)
            norm(0, lambda k, v: gsv[:, 0, k, v:v + 1])
            own(V.memset(flat(S2)[:, 0:4 * 2 * (S + 2 * PADC)], 0.0))
            for m in range(4):
                u = u0["in_ab"] + 4 + m
                got(dve, u)
                read(dve, u0["in_ab"] + m)
                ins = V.tensor_tensor(U[:, m, :, PADC:PADC + S], pair(u),
                                      S1[:, 4 + m, :].rearrange("p (a n) -> p a n", a=2), ALU.mult)
                ins.then_inc(free[u % 4], 1)
            read(dve, u)
            last = {}
            for t in range(CONV):
                for m in range(3):
                    y = S3[:, m, :].rearrange("p (a n) -> p a n", a=2)
                    w = vc("conv_w", 4 * t + m)
                    if t == 0:
                        ins = V.tensor_scalar(y, U[:, m, :, 0:S], w, vc("conv_b", m), ALU.mult, ALU.add)
                    else:
                        own.wait(last[m])
                        ins = STT(out=y, in0=U[:, m, :, t:t + S], scalar=w, in1=y, op0=ALU.mult, op1=ALU.add)
                    last[m] = own.mark(ins)
            for m in range(3):
                own.wait(last[m])
            dve.sem_inc(yc_ready, 1)
            dve.wait_ge(n_std, 2)
            V.reciprocal(std[:, 1, 0:P], std[:, 0, 0:P]).then_inc(n_rs, 1)
            dve.wait_ge(n_bc, 2)
            for m in range(4):
                STT(out=S3[:, m, :], in0=S3[:, m, :], scalar=vc("conv_norm_g", m), in1=T[:, 6, :],
                    op0=ALU.mult, op1=ALU.mult).then_inc(yn_ready, 1)
            for k in range(KT):
                u = u0["out_ab"] + k
                got(dve, u)
                add_gated(u, k, 0, 2, N2).then_inc(free[u % 4], 1)
            norm(2, lambda k, v: gsv[:, 1, k, v:v + 1])
            route(0)
            experts(0)
            combine(0)
            norm(3, lambda k, v: gsv[:, 2, k, v:v + 1])
            read(dve, u0["ss"] + 1)
            own(V.reciprocal(std[:, 0, 0:S], std[:, 0, 0:S]))
            for k in range(3):
                ins = STT(out=cq[:, k, :], in0=cq[:, k, :], scalar=vc("cq_g", k), in1=std[:, 0, 0:S],
                          op0=ALU.mult, op1=ALU.mult)
            ins.then_inc(cd_n, 1)
            own(V.reciprocal(std[:, 1, :], std[:, 1, :]))
            for k in range(2):
                ins = STT(out=ckv[:, k, :], in0=ckv[:, k, :], scalar=vc("ckv_g", k), in1=std[:, 1, :],
                          op0=ALU.mult, op1=ALU.mult)
            ins.then_inc(cd_n, 1)
            read(dve, u0["ss"] + 5)
            own(V.reciprocal(cdr, cdr))
            own(STT(out=part(S1, 0, 1024), in0=part(S1, 0, 1024), scalar=vc("q_g"), in1=part(H, 2048, 1024),
                    op0=ALU.mult, op1=ALU.mult))
            STT(out=part(S1, 1024, 1024), in0=part(S1, 1024, 1024), scalar=vc("k_g"), in1=part(H, 3072, 1024),
                op0=ALU.mult, op1=ALU.mult).then_inc(cd_qk, 1)
            u = u0["rope_c"]
            dve.wait_ge(cd_qk, 1)
            for j in range(3):
                got(dve, u + j)
                x_ = part(S1, 512 * j, 2, S) if j < 2 else qk[:, 2:4, 0:S]
                t1 = rtmp[:, j, :].rearrange("p (a n) -> p a n", a=2)
                cos = tabv("cos_c", S).unsqueeze(1).to_broadcast([P, 2, S])
                sin = tabv("sin_c", S).unsqueeze(1).to_broadcast([P, 2, S])
                ins = V.tensor_tensor(t1, pair(u + j), sin, ALU.mult)
                ins.then_inc(free[(u + j) % 4], 1)
                read(dve, u + j)
                own(V.tensor_tensor(x_, x_, cos, ALU.mult))
                ins = V.tensor_tensor(x_, x_, t1, ALU.add)
                if j < 2:
                    own(ins)
            ins.then_inc(cd_rot, 1)
            u = u0["rope_d"]
            for j in range(3):
                got(dve, u + j)
                w = 2 if j < 2 else 1
                x_ = (part(S2, 2560 + 512 * j, 2, S) if j < 2 else part(S2, 1024, 1, S))[0:64]
                t1 = rtmp[0:64, 3, 0:w * S].rearrange("p (a n) -> p a n", a=w)
                cos = tabv("cos_d", S, rows=64).unsqueeze(1).to_broadcast([64, w, S])
                sin = tabv("sin_d", S, rows=64).unsqueeze(1).to_broadcast([64, w, S])
                ins = V.tensor_tensor(t1, bank(u + j, w * S)[0:64, :].rearrange("p (a n) -> p a n", a=w), sin,
                                      ALU.mult)
                ins.then_inc(free[(u + j) % 4], 1)
                read(dve, u + j)
                own(V.tensor_tensor(x_, x_, cos, ALU.mult))
                ins = V.tensor_tensor(x_, x_, t1, ALU.add)
                if j < 2:
                    own(ins)
            ins.then_inc(cd_rot, 1)
            for n in range(16 + 1):
                i = n - 1
                if n >= 1:
                    read(dve, so_u["a", i])
                    own(V.reciprocal(rt[:, 64 + 2 * i:65 + 2 * i], rt[:, 64 + 2 * i:65 + 2 * i]))
                    V.tensor_scalar(pp[:, i % 2, :], pp[:, i % 2, :], rt[:, 64 + 2 * i:65 + 2 * i], None,
                                    ALU.mult).then_inc(so_n, 1)
                if n < 16:
                    scale = float(P) ** -0.5 if n // 2 < 4 else 192.0 ** -0.5
                    got(dve, so_u["a", n])
                    own(V.reduce_max(rt[:, 128 + n:129 + n], bank(so_u["a", n]), AX.X))
                    V.tensor_scalar(rt[:, 2 * n:2 * n + 1], rt[:, 128 + n:129 + n], -scale, None, ALU.mult)\
                        .then_inc(so_m, 1)
                if n >= 1:
                    got(dve, so_u["b", i])
                    if i >= 2:
                        got(dve, so_u["c", i - 2])
                    V.tensor_copy(pt[:, i % 2, :], bank(so_u["b", i]))\
                        .then_inc(free[so_u["b", i] % 4], 1)
            for j in range(4):
                u = u0["out_cd"] + j
                got(dve, u)
                for h in range(2):
                    ins = add_gated(u, 2 * j + h, 1, 2, S, h)
                ins.then_inc(free[u % 4], 1)
            norm(4, lambda k, v: gsv[:, 3, k, v:v + 1], n=S)
            route(1)
            experts(1)
            combine(1)
            norm(5, lambda k, v: vc("final_g", k), n=S)

        @block.gpsimd
        def _(pool):
            own = Chain(pool, pool_own)
            pool.wait_ge(s_tab, 16)
            for dst_, src in (
                (X[:, :, S:N2], a["ctxT"].rearrange("(k p) n -> p k n", p=P)),
                (rw[:, 0], a["router_w"][0].rearrange("(k p) n -> p k n", p=P)),
                (rw[:, 1], a["router_w"][1].rearrange("(k p) n -> p k n", p=P)),
                (rb[:, 0], a["router_b"][0:1]), (rb[:, 1], a["router_b"][1:2]),
            ):
                pool.dma_start(dst_, src).then_inc(s_late, 16)
            pool.wait_ge(s_zero, 1)
            pool.wait_ge(x_ready, 32)
            zv = zb[:, :].bitcast(F32)
            y_init = y_rows.rearrange("(q p b) (a n) -> q p (b a) n", q=4, p=P, n=CH // 2)
            for q in range(4):
                pool.dma_start(y_init[q], zv.unsqueeze(1).to_broadcast([P, y_init.shape[2], CH // 2]))\
                    .then_inc(r["zeroed"], 16)

            for t in range(1, CONV):
                pool.wait_ge(cv_ready, t + 1)
                ins = pool.tensor_tensor(S3[:, 3, :], S3[:, 3, :], S3[:, 4 + t % 4, :], ALU.add)
                if t < CONV - 1:
                    ins.then_inc(cv_used, 1)
                    pool.wait_ge(cv_used, t)
                    pool.wait_ge(cv_used, t)
                else:
                    ins.then_inc(yc_ready, 1)

            def moe(l):
                tt = TT[l]
                pool.wait_ge(r["zeroed"], 16 * 4)
                pool.wait_ge(r["dest"], l + 1)
                pool.wait_ge(r["xT_all"], l + 1)
                pool.wait_ge(r["y_all"], l + 1)
                g = [part(S1, 0, 4, D), part(S2, 0, 4, D)]
                for t in range(tt):
                    for k in range(2):
                        pool.indirect_dma_start(g[k][:, t, :], None, y_rows,
                                                bass.IndirectOffsetOnAxis(ap=dst[:, t, k:k + 1], axis=0))\
                            .then_inc(r["cg"][t], 16)

            moe(0)
            moe(1)
            pool.wait_ge(n_nrm, 8 * 5)
            src = H[:, :, 0:S]
            pool.dma_start(a["out"].rearrange("(k p) n -> p k n", p=P), src).then_inc(s_out, 16)
            pool.wait_ge(s_out, 16)


def kernel(**inputs):
    import numpy as _np
    import concourse.bacc as _bacc
    from concourse import mybir as _mybir
    from concourse.bass_utils import run_bass_kernel_spmd as _run

    g = {k: _np.ascontiguousarray(v) for k, v in inputs.items()}

    def tiles(v):
        return v.reshape(-1, 128).T

    vec = _np.concatenate([tiles(v) for v in (
        g["lru_b_in"], g["lru_conv_w"], g["lru_conv_b"],
        g["lru_b_gates"].reshape(8, 2, 128).transpose(1, 0, 2), g["lru_a_param"], g["lru_b_out"],
        g["ffn_conv_w"], g["ffn_conv_b"], g["ln_g"], g["ln_b"], g["c_2"], g["c_ctx_2"], g["mod_b_2"],
        g["norm_mix_g_2"], g["norm_ffn_g_2"], g["conv_w_2"], g["conv_b_2"], g["conv_norm_g_2"],
        g["q_norm_g_2"], g["k_norm_g_2"], g["cq_norm_g_2"], g["ckv_norm_g_2"], g["final_norm_g_2"])], 1)
    arrays = {
        "xT": g["x"][0].T, "ctxT": g["ctx_2"][0].T, "vec": vec, "tab": tables(),
        "router_w": _np.concatenate([g["router_grp_w_2"], g["router_exp_w_2"]], 2),
        "router_b": _np.concatenate([g["router_grp_b_2"], g["router_exp_b_2"]], 1),
        "lru_w_in": g["lru_w_in"][0], "lru_w_gates": g["lru_w_gates"][0], "lru_w_out": g["lru_w_out"][0],
        "kv_w": g["kv_w"], "attn_w_q": g["attn_w_q"][0], "attn_w_out": g["attn_w_out"][0],
        "ffn_w_up": g["ffn_w_up"], "ffn_w_down": g["ffn_w_down"], "mod_w": g["mod_w_2"],
        "w_in_ab": g["w_in_ab_2"][0], "w_out_ab": g["w_out_ab_2"][0], "w_in_cd": g["w_in_cd_2"][0],
        "w_uq": g["w_uq_2"][0], "w_ukv": g["w_ukv_2"][0], "w_out_cd": g["w_out_cd_2"][0],
        "exp_w_gate": g["exp_w_gate_2"], "exp_w_up": g["exp_w_up_2"], "exp_w_down": g["exp_w_down_2"],
    }
    arrays = {k: _np.ascontiguousarray(v) for k, v in arrays.items()}
    nc = _bacc.Bacc("TRN2", target_bir_lowering=False, num_devices=1)
    aps = {k: nc.dram_tensor("in_" + k, v.shape, _mybir.dt.from_np(v.dtype), kind="ExternalInput").ap()
           for k, v in arrays.items()}
    aps["out"] = nc.dram_tensor("out", (1024, 256), _mybir.dt.float32, kind="ExternalOutput").ap()
    build(nc, aps)
    r = _run(nc, [{"in_" + k: v for k, v in arrays.items()}], core_ids=[0])
    return _np.ascontiguousarray(r.results[0]["out"].T)[None]
```
